# Optimizing a Trainium2 kernel written in Bass

```python
import math
import jax, jax.numpy as jnp
from jax import lax
import numpy as np

D_MODEL = 1024
BATCH = 1
SEQ = 512
DEPTH = 1
DEC_BATCH = 1
DEC_SEQ = 64
PAST_LEN = 256

CHUNK = 64
Q_BLOCK = 128
MLA_HEADS = 4
QK_NOPE = 128
QK_ROPE = 64
V_HEAD = 128
Q_LORA = 768
KV_LORA = 256
ROPE_BASE = 10000.0
GMLP_HEADS = 4
GMLP_HEAD_DIM = 128
GMLP_CHUNK = 128
MLA_WIDTH = MLA_HEADS * V_HEAD
GMLP_WIDTH = GMLP_HEADS * GMLP_HEAD_DIM
D_MIX = MLA_WIDTH + GMLP_WIDTH
D_IN = Q_LORA + KV_LORA + QK_ROPE + 2 * GMLP_WIDTH
PEER_HEADS = 8
N_KEYS = 128
N_EXPERTS = N_KEYS * N_KEYS
PEER_TOPK = 16
D_KEY = 256
PEER_BLOCK = 128
DEEPNORM_ALPHA = (2 * DEPTH) ** 0.25
DEEPNORM_BETA = (8 * DEPTH) ** -0.25
EPS = 1e-6
NEG = -1e30

kernel_name = 'hymba_mla_gmlp_peer_deepnorm_stream_step'

def _layer_norm(x, g, b):
    xf = x.astype(jnp.float32)
    mu = jnp.mean(xf, axis=-1, keepdims=True)
    var = jnp.mean(jnp.square(xf - mu), axis=-1, keepdims=True)
    return ((xf - mu) * lax.rsqrt(var + EPS) * g.astype(jnp.float32) + b.astype(jnp.float32)).astype(x.dtype)

def _rms_norm(x, g):
    xf = x.astype(jnp.float32)
    ms = jnp.mean(jnp.square(xf), axis=-1, keepdims=True)
    return (xf * lax.rsqrt(ms + EPS) * g.astype(jnp.float32)).astype(x.dtype)

def _rope(x, pos):
    half = QK_ROPE // 2
    inv_freq = jnp.power(jnp.float32(ROPE_BASE), -jnp.arange(half, dtype=jnp.float32) * (2.0 / QK_ROPE))
    ang = pos.astype(jnp.float32)[:, None] * inv_freq[None, :]
    shape = (pos.shape[0],) + (1,) * (x.ndim - 3) + (half,)
    cos = jnp.cos(ang).reshape(shape)
    sin = jnp.sin(ang).reshape(shape)
    xf = x.astype(jnp.float32)
    x1, x2 = xf[..., :half], xf[..., half:]
    return jnp.concatenate([x1 * cos - x2 * sin, x2 * cos + x1 * sin], axis=-1).astype(x.dtype)

def _chunk_causal_attention(q, k, v, q_pos, k_pos):
    b, t, h, dq = q.shape
    scale = 1.0 / math.sqrt(dq)
    k_chunk = k_pos // CHUNK

    def attend(args):
        qb, qpb = args
        s = jnp.einsum('bqhd,bkhd->bhqk', qb, k).astype(jnp.float32) * scale
        mask = (qpb // CHUNK)[:, None] >= k_chunk[None, :]
        s = jnp.where(mask[None, None], s, NEG)
        p = jax.nn.softmax(s, axis=-1).astype(v.dtype)
        return jnp.einsum('bhqk,bkhd->bqhd', p, v)

    if t > Q_BLOCK and t % Q_BLOCK == 0:
        nb = t // Q_BLOCK
        qs = jnp.moveaxis(q.reshape(b, nb, Q_BLOCK, h, dq), 1, 0)
        ps = q_pos.reshape(nb, Q_BLOCK)
        o = lax.map(attend, (qs, ps))
        return jnp.moveaxis(o, 0, 1).reshape(b, t, h, v.shape[-1])
    return attend((q, q_pos))

def _gmlp_mixer(u, v, g_v, b_v, w_s, b_s):
    b, t, _ = u.shape
    u = jax.nn.gelu(u)
    v = _layer_norm(jax.nn.gelu(v), g_v, b_v)
    npad = (-t) % GMLP_CHUNK
    vp = jnp.pad(v, ((0, 0), (0, npad), (0, 0)))
    nc = (t + npad) // GMLP_CHUNK
    vp = vp.reshape(b, nc, GMLP_CHUNK, GMLP_HEADS, GMLP_HEAD_DIM)
    blk = jnp.arange(GMLP_CHUNK) // CHUNK
    mask = blk[:, None] >= blk[None, :]
    ws = jnp.where(mask[None], w_s, jnp.zeros_like(w_s))
    mixed = jnp.einsum('hij,bnjhd->bnihd', ws, vp) + jnp.transpose(b_s)[None, None, :, :, None]
    mixed = mixed.reshape(b, nc * GMLP_CHUNK, GMLP_WIDTH)[:, :t]
    return u * mixed, v

def _peer(h, w_pq, sub_keys, peer_u, peer_v):
    b, t, d = h.shape
    n = b * t
    npad = (-n) % PEER_BLOCK
    hf = jnp.pad(h.reshape(n, d), ((0, npad), (0, 0))).reshape(-1, PEER_BLOCK, d)

    def one_block(xb):
        q = (xb @ w_pq).reshape(PEER_BLOCK, PEER_HEADS, 2, D_KEY // 2)
        s = jnp.einsum('thpd,hpnd->thpn', q, sub_keys).astype(jnp.float32)
        s_top, i_top = lax.top_k(s, PEER_TOPK)
        cand = s_top[:, :, 0, :, None] + s_top[:, :, 1, None, :]
        cidx = i_top[:, :, 0, :, None] * N_KEYS + i_top[:, :, 1, None, :]
        cand = cand.reshape(PEER_BLOCK, PEER_HEADS, PEER_TOPK * PEER_TOPK)
        cidx = cidx.reshape(PEER_BLOCK, PEER_HEADS, PEER_TOPK * PEER_TOPK)
        f_s, f_pos = lax.top_k(cand, PEER_TOPK)
        e_idx = jnp.take_along_axis(cidx, f_pos, axis=-1)
        g = jax.nn.softmax(f_s, axis=-1).astype(xb.dtype)
        act = jax.nn.gelu(jnp.einsum('thkd,td->thk', peer_u[e_idx], xb))
        return jnp.einsum('thk,thkd->td', g * act, peer_v[e_idx])

    out = lax.map(one_block, hf).reshape(-1, d)[:n]
    return out.reshape(b, t, d)

def _layer(x, c, cache_ckv, cache_kr, w_ada, b_ada, w_in, g_q, g_kv, w_uq, w_uk, w_uv, g_v, b_v,
           w_s, b_s, g_out_a, g_out_b, w_o, ln1_g, ln1_b, w_pq, sub_keys, peer_u, peer_v, ln2_g, ln2_b):
    b, t, _ = x.shape
    past = 0 if cache_ckv is None else cache_ckv.shape[1]
    pos = past + jnp.arange(t, dtype=jnp.int32)
    mod = jax.nn.silu(c) @ w_ada + b_ada
    sh1, sc1, gt1, sh2, sc2, gt2 = jnp.split(mod[:, None, :], 6, axis=-1)
    h = x * (1 + sc1) + sh1
    z = h @ w_in
    o1 = Q_LORA
    o2 = o1 + KV_LORA
    o3 = o2 + QK_ROPE
    o4 = o3 + GMLP_WIDTH
    cq_raw, ckv_raw, kr_raw = z[..., :o1], z[..., o1:o2], z[..., o2:o3]
    gu, gv = z[..., o3:o4], z[..., o4:]
    cq = _rms_norm(cq_raw, g_q)
    q = (cq @ w_uq).reshape(b, t, MLA_HEADS, QK_NOPE + QK_ROPE)
    q = jnp.concatenate([q[..., :QK_NOPE], _rope(q[..., QK_NOPE:], pos)], axis=-1)
    ckv = _rms_norm(ckv_raw, g_kv)
    kr = _rope(kr_raw, pos)
    if cache_ckv is None:
        ckv_all, kr_all = ckv, kr
    else:
        ckv_all = jnp.concatenate([cache_ckv, ckv], axis=1)
        kr_all = jnp.concatenate([cache_kr, kr], axis=1)
    n_keys = ckv_all.shape[1]
    k_pos = jnp.arange(n_keys, dtype=jnp.int32)
    k_nope = (ckv_all @ w_uk).reshape(b, n_keys, MLA_HEADS, QK_NOPE)
    val = (ckv_all @ w_uv).reshape(b, n_keys, MLA_HEADS, V_HEAD)
    k = jnp.concatenate([k_nope, jnp.broadcast_to(kr_all[:, :, None, :], (b, n_keys, MLA_HEADS, QK_ROPE))], axis=-1)
    a_out = _chunk_causal_attention(q, k, val, pos, k_pos).reshape(b, t, MLA_WIDTH)
    b_out, v_rows = _gmlp_mixer(gu, gv, g_v, b_v, w_s, b_s)
    mix = jnp.concatenate([_rms_norm(a_out, g_out_a), _rms_norm(b_out, g_out_b)], axis=-1) @ w_o
    x1 = _layer_norm(DEEPNORM_ALPHA * x + (1 + gt1) * mix, ln1_g, ln1_b)
    h2 = x1 * (1 + sc2) + sh2
    f = _peer(h2, w_pq, sub_keys, peer_u, peer_v)
    x2 = _layer_norm(DEEPNORM_ALPHA * x1 + (1 + gt2) * f, ln2_g, ln2_b)
    return x2, ckv, kr, v_rows

def setup_inputs(seed: int = 0) -> dict:
    key = jax.random.key(seed)
    ks = iter(jax.random.split(key, 40))

    def nrm(shape, s=1.0):
        return jax.random.normal(next(ks), shape, jnp.float32) * s

    L = DEPTH
    D = D_MODEL
    return {
        'x_prompt': nrm((BATCH, SEQ, D)),
        'x_sample': nrm((DEC_BATCH, DEC_SEQ, D)),
        'cache_ckv': nrm((L, DEC_BATCH, PAST_LEN, KV_LORA)),
        'cache_krope': nrm((L, DEC_BATCH, PAST_LEN, QK_ROPE)),
        'c_prompt': nrm((BATCH, D)),
        'c_sample': nrm((DEC_BATCH, D)),
        'ln_in_g': 1.0 + nrm((D,), 0.05),
        'ln_in_b': nrm((D,), 0.02),
        'w_ada': nrm((L, D, 6 * D), 0.2 * D ** -0.5),
        'b_ada': nrm((L, 6 * D), 0.01),
        'w_in': nrm((L, D, D_IN), D ** -0.5),
        'g_q': 1.0 + nrm((L, Q_LORA), 0.05),
        'g_kv': 1.0 + nrm((L, KV_LORA), 0.05),
        'w_uq': nrm((L, Q_LORA, MLA_HEADS * (QK_NOPE + QK_ROPE)), Q_LORA ** -0.5),
        'w_uk': nrm((L, KV_LORA, MLA_HEADS * QK_NOPE), KV_LORA ** -0.5),
        'w_uv': nrm((L, KV_LORA, MLA_HEADS * V_HEAD), DEEPNORM_BETA * KV_LORA ** -0.5),
        'g_v': 1.0 + nrm((L, GMLP_WIDTH), 0.05),
        'b_v': nrm((L, GMLP_WIDTH), 0.02),
        'w_s': nrm((L, GMLP_HEADS, GMLP_CHUNK, GMLP_CHUNK), 0.5 * GMLP_CHUNK ** -0.5),
        'b_s': 1.0 + nrm((L, GMLP_HEADS, GMLP_CHUNK), 0.01),
        'g_out_a': 1.0 + nrm((L, MLA_WIDTH), 0.05),
        'g_out_b': 1.0 + nrm((L, GMLP_WIDTH), 0.05),
        'w_o': nrm((L, D_MIX, D), DEEPNORM_BETA * D_MIX ** -0.5),
        'ln1_g': 1.0 + nrm((L, D), 0.05),
        'ln1_b': nrm((L, D), 0.02),
        'w_pq': nrm((L, D, PEER_HEADS * D_KEY), D ** -0.5),
        'sub_keys': nrm((L, PEER_HEADS, 2, N_KEYS, D_KEY // 2), (D_KEY // 2) ** -0.5),
        'peer_u': nrm((L, N_EXPERTS, D), D ** -0.5),
        'peer_v': nrm((L, N_EXPERTS, D), DEEPNORM_BETA),
        'ln2_g': 1.0 + nrm((L, D), 0.05),
        'ln2_b': nrm((L, D), 0.02),
    }

def reference(x_prompt, x_sample, cache_ckv, cache_krope, c_prompt, c_sample, ln_in_g, ln_in_b,
              w_ada, b_ada, w_in, g_q, g_kv, w_uq, w_uk, w_uv, g_v, b_v, w_s, b_s, g_out_a, g_out_b,
              w_o, ln1_g, ln1_b, w_pq, sub_keys, peer_u, peer_v, ln2_g, ln2_b):
    hp = _layer_norm(x_prompt, ln_in_g, ln_in_b)
    hs = _layer_norm(x_sample, ln_in_g, ln_in_b)
    ckv_p, kr_p, ckv_s, kr_s, gv_s = [], [], [], [], []
    for l in range(DEPTH):
        lw = (w_ada[l], b_ada[l], w_in[l], g_q[l], g_kv[l], w_uq[l], w_uk[l], w_uv[l], g_v[l], b_v[l],
              w_s[l], b_s[l], g_out_a[l], g_out_b[l], w_o[l], ln1_g[l], ln1_b[l], w_pq[l], sub_keys[l],
              peer_u[l], peer_v[l], ln2_g[l], ln2_b[l])
        hp, ckv_new_p, kr_new_p, _ = _layer(hp, c_prompt, None, None, *lw)
        hs, ckv_new_s, kr_new_s, v_new_s = _layer(hs, c_sample, cache_ckv[l], cache_krope[l], *lw)
        ckv_p.append(ckv_new_p)
        kr_p.append(kr_new_p)
        ckv_s.append(ckv_new_s)
        kr_s.append(kr_new_s)
        gv_s.append(v_new_s)
    return (hp, hs, jnp.stack(ckv_p), jnp.stack(kr_p), jnp.stack(ckv_s), jnp.stack(kr_s), jnp.stack(gv_s))


_drawn_inputs = setup_inputs


def setup_inputs(seed=0):
    import zlib

    import numpy as np

    out = dict(_drawn_inputs(seed))
    spreads = {}
    factors = {'b_v': 2.973, 'b_s': 3.676, 'ln2_b': 2.773}
    for name, (base, spread) in spreads.items():
        noise = np.random.default_rng([zlib.crc32(name.encode()), seed]).standard_normal(out[name].shape)
        drawn = base * np.exp(spread * noise) if base else spread * noise
        out[name] = __import__('jax').numpy.asarray(drawn.astype(out[name].dtype))
    for name, factor in factors.items():
        out[name] = (out[name] * factor).astype(out[name].dtype)
    return out
```

```python
from contextlib import ExitStack, contextmanager

import concourse.bass as bass
from concourse import mybir

F32 = mybir.dt.float32
F32R = mybir.dt.float32r
U32 = mybir.dt.uint32
ALU = mybir.AluOpType
ACT = mybir.ActivationFunctionType
AX = mybir.AxisListType

P = 128
D = 1024
KD = D // P
SEQ, DEC, PAST = 512, 64, 256
T = SEQ + DEC
H = T // 2
HALVES = ((0, H), (H, T))
TILES = [(t * P, P) for t in range(SEQ // P)] + [(SEQ, DEC)]
NT = len(TILES)
SAMPLE = NT - 1
CHUNK = 64
HEADS, NOPE, ROPE, VH = 4, 128, 64, 128
QL, KVL = 768, 256
QK, CK = QL // P, KVL // P
GH = 4
KEYS = SEQ + PAST + DEC
NEW = SEQ + PAST
VT = 7
PH, NK, TOPK = 8, 128, 16
HP = 2 * PH
SLOTS = PH * TOPK
EPS = 1e-6
ALPHA = 2.0 ** 0.25
SCALE = (NOPE + ROPE) ** -0.5
Z_CKV, Z_KR, Z_GU, Z_GV, Z_N = QK, QK + CK, QK + CK + 1, QK + CK + 1 + GH, QK + CK + 1 + 2 * GH
VEC_LEN = dict(ln_in_g=8, ln_in_b=8, b_ada=48, g_q=QK, g_kv=CK, g_v=GH, b_v=GH, g_out_a=HEADS,
               g_out_b=GH, ln1_g=8, ln1_b=8, c=16)
VEC_AT = {}
for _name, _n in VEC_LEN.items():
    VEC_AT[_name] = sum(VEC_LEN[k] for k in VEC_AT)
NVEC = sum(VEC_LEN.values())
C_ID, C_PERM, C_COS, C_SIN, C_IOTA = 0, P, 2 * P, 2 * P + T, 2 * P + 2 * T
NCONST = 2 * P + 2 * T + TOPK
RING = 4
ORDER = dict(ada=48, w_in=Z_N, w_uq=6, w_o=KD, w_pq=HP)
RING_AT, SPLIT_AT = {}, {}
_g = 0
for _name, _n in ORDER.items():
    RING_AT[_name] = _g
    SPLIT_AT[_name] = _g - ORDER["ada"]
    _g += _n
WIDTH = dict(ada=KD, w_in=KD, w_uq=QK, w_o=KD, w_pq=KD)
GBUF = 8


def wait(eng, sem, value):
    if not (isinstance(value, int) and value <= 0):
        eng.wait_ge(sem, value)


def in_steps(eng, n, unroll, body):
    full = n // unroll
    for b in range(min(n, unroll)):
        body(b, b)
    if full > 2:
        with eng.Fori(1, full) as i:
            for u in range(unroll):
                body(i * unroll + u, u)
    elif full == 2:
        for u in range(unroll):
            body(unroll + u, u)
    for b in range(max(full, 1) * unroll, n):
        body(b, b - full * unroll)


class Chain:

    def __init__(self, eng, sem):
        self.eng, self.sem, self.n, self.over = eng, sem, 0, 0

    def __call__(self, ins):
        ins.then_inc(self.sem, 1)
        self.n += 1
        self.eng.wait_ge(self.sem, self.n + self.over)

    @contextmanager
    def loop(self, start, end, per):
        with self.eng.Fori(start, end) as i:
            before, self.over = self.n, (i - start) * per
            yield i
            assert self.n - before == per, self.n - before
            self.over = 0
        self.n = before + (end - start) * per


def build(nc, a):
    with ExitStack() as ctx:
        def sem(name):
            return ctx.enter_context(nc.semaphore(name))

        base = 16512

        def at(name, shape, offset, dt=F32):
            return nc.alloc_sbuf_tensor_at(name, shape, dt, offset=base + offset)

        o = 0
        regions = {}
        for name, size in dict(consts=NCONST * 4, vecs=NVEC * 4, ones=512, mod=96 * 4, small=2048, x0=KD * T * 4,
                               hi=KD * T * 4, lo=KD * T * 4, wraw=RING * 4096, wsplit=4 * 4096,
                               z=Z_N * T * 4, tmp=KD * T * 4, rows=4 * T * 4,
                               q=6 * T * 4, k=HEADS * KEYS * 4, kr=KEYS * 4, ckv=CK * KEYS * 4,
                               p=8192).items():
            regions[name] = o
            o += (size + 31) // 32 * 32
        assert base + o <= 229344, base + o
        R = regions
        consts = at("consts_sb", [P, NCONST], R["consts"])
        vecs = at("vecs_sb", [P, NVEC], R["vecs"])
        ones = at("ones", [P, P], R["ones"])
        mod = at("mod", [P, 48, 2], R["mod"])
        silu_c = at("silu_c", [P, KD, 2], R["small"])
        stats = at("stats", [P, 2, 6], R["small"] + 64)
        meanvar = at("meanvar", [P, NT, 2], R["small"] + 128)
        rstd = at("rstd", [P, NT], R["small"] + 192)
        std = at("std", [P, NT], R["small"] + 224)
        negmax = at("negmax", [P, 32], R["small"] + 256)
        rowmax = at("rowmax", [P, 32], R["small"] + 384)
        rowsum = at("rowsum", [P, 32], R["small"] + 512)
        rinv = at("rinv", [P, 32], R["small"] + 640)
        x0T = at("x0T", [P, KD, T], R["x0"])
        act_hi = at("act_hi", [P, KD, T], R["hi"], F32R)
        act_lo = at("act_lo", [P, KD, T], R["lo"], F32R)
        w_raw = at("w_raw", [P, RING, D], R["wraw"])
        w_hi = at("w_hi", [P, 2, D], R["wsplit"], F32R)
        w_lo = at("w_lo", [P, 2, D], R["wsplit"] + 8192, F32R)
        z = at("z", [P, Z_N, T], R["z"])
        x_tok = at("x_tok", [P, NT, D], R["z"])
        val = at("val", [P, VT, HEADS * VH], R["z"])
        r_T = at("r_T", [P, KD, T], R["z"])
        h2T = at("h2T", [P, KD, T], R["z"] + KD * T * 4)
        tmp = at("tmp", [P, KD, T], R["tmp"])
        rows = at("rows", [P, 4, T], R["rows"])
        qT = at("qT", [P, 6, T], R["q"])
        kT = at("kT", [P, HEADS, KEYS], R["k"])
        krT = at("krT", [P, KEYS], R["kr"])
        ckvT = at("ckvT", [P, CK, KEYS], R["ckv"])
        sq = at("sq", [P, KD, T], R["q"])
        qpT = at("qpT", [P, HP, T], R["q"])
        skT = at("skT_sb", [P, HP, NK], R["p"])
        prob = at("prob", [P, 2, SEQ], R["p"])
        probT = at("probT", [P, 2, 4, P], R["p"] + 4096)
        v_tok = at("v_tok", [P, NT, GH * P], R["hi"])
        wsT = at("wsT_sb", [P, GH, P], R["hi"] + 10240)
        bs = at("bs_sb", [P, GH, P], R["hi"] + 12288)
        w_uk = at("w_uk_sb", [P, CK, HEADS * NOPE], R["lo"])
        w_uv = at("w_uv_sb", [P, CK, HEADS * VH], R["lo"] + 4096)
        score = at("score", [P, HP, NK], R["hi"])
        score2 = at("score2", [P, HP, NK], R["hi"] + 8192)
        cand = at("cand", [P, PH, 256], R["hi"] + 16384)
        cand2 = at("cand2", [P, PH, 256], R["hi"] + 24576)
        k_at = R["hi"] + 32768
        top = at("top", [P, HP, TOPK], k_at)
        top_i = at("top_i", [P, HP, TOPK], k_at + 1024, U32)
        top_f = at("top_f", [P, HP, TOPK], k_at + 2048)
        fin = at("fin", [P, PH, TOPK], k_at + 3072)
        assert k_at + 3584 <= R["wraw"]
        pos = at("pos", [P, PH, TOPK], R["small"] + 768, U32)
        pos_a = at("pos_a", [P, PH, TOPK], R["small"] + 1280, U32)
        ssum = at("ssum", [P, PH], R["small"] + 1792)
        expert = at("expert", [P, NT, SLOTS], R["tmp"], U32)
        gate = at("gate", [P, NT, SLOTS], R["tmp"] + 2560)
        e_f = at("e_f", [P, 3, SLOTS], R["tmp"] + 5120)
        act_v = at("act_v", [P, SLOTS], R["tmp"] + 6656)
        act_g = at("act_g", [P, SLOTS], R["tmp"] + 7168)
        idx8 = at("idx8", [P, 2, GBUF], R["tmp"] + 7680, U32)
        act8 = at("act8", [P, GBUF], R["tmp"] + 8064)
        h2_tok = at("h2_tok", [P, D], R["tmp"] + 8192)
        f_tok = at("f_tok", [P, D], R["tmp"] + 12288)
        y_tok = at("y_tok", [P, 2, D], R["hi"])
        gb2 = at("gb2", [P, 2, D], R["hi"] + 8192)
        gath = at("gath", [P, GBUF, D], R["wraw"])
        junk = at("junk", [P, D], R["rows"])
        o_tok = at("o_tok", [P, NT, KVL + ROPE], R["rows"])
        ident = consts[:, C_ID:C_ID + P]
        perm = consts[:, C_PERM:C_PERM + P]
        cosT = consts[:, C_COS:C_COS + T]
        sinT = consts[:, C_SIN:C_SIN + T]
        iota = consts[:, C_IOTA:C_IOTA + TOPK]

        def vec(name, k):
            return vecs[:, VEC_AT[name] + k:VEC_AT[name] + k + 1]

        ps = ctx.enter_context(nc.psum_tensor("ps", [P, 8, 512], F32))

        s_const, s_vec, s_cache, s_ukv, s_gm, s_sk, s_gb = map(sem, "s_const s_vec s_cache s_ukv s_gm s_sk s_gb".split())
        s_x = [sem(f"x_landed{i}") for i in range(NT)]
        s_w = [sem(f"w_landed{i}") for i in range(RING)]
        s_dve, s_act = sem("own_dve"), sem("own_act")
        names = """ones silu adaused ada var std xn xT x0e mod h32 hhi hlo whi wlo wused evac
            sqz rowsA cqrow gelu vmean vc2 vvar vvarr vn cqn cqhi cqlo ckvn krmm krr qmm qr kmm kev vmm vev
            vtt vte gmm bt sc mx ex pn pt pte pv pve rowsB rowr sqab mhi mlo m
            r1 mean1 meanr rc1 sq1 var1 varr h2 h2hi h2lo smm sev topk
            h2t h2te gu gd idx gvs act wgt fsub fexp var2 std2 wsm ax group facc ft fte r2 yt y out otr ote vot""".split()
        s = {n: sem("s_" + n) for n in names}
        s_y = [sem(f"y_written{i}") for i in range(2)]
        s_g = [sem(f"rows_landed{i}") for i in range(GBUF)]

        block = ctx.enter_context(nc.Block())

        N_LIN = ORDER["w_in"] + ORDER["w_uq"] + ORDER["w_o"] + ORDER["w_pq"]
        END = {n: SPLIT_AT[n] + ORDER[n] for n in ORDER}

        @block.sync
        def _(sp):
            def stream(name, dram):
                width = WIDTH[name] * P
                g0, s0 = RING_AT[name], SPLIT_AT[name]

                def load(b, u):
                    slot = (g0 + u) % RING
                    if name == "ada" or (isinstance(b, int) and g0 + b - RING < ORDER["ada"]):
                        wait(sp, s["adaused"], b + g0 - RING + 1)
                    else:
                        wait(sp, s["wlo"], b + s0 - RING + 1)
                    sp.dma_start(w_raw[:, slot, 0:width], dram[b]).then_inc(s_w[slot], 16)
                in_steps(sp, ORDER[name], RING, load)

            for name in ORDER:
                stream(name, a[name])
            sp.wait_ge(s["topk"], NT)
            sp.dma_start(gb2[:, 0], a["ln2_g"].partition_broadcast(P)).then_inc(s_gb, 16)
            sp.dma_start(gb2[:, 1], a["ln2_b"].partition_broadcast(P)).then_inc(s_gb, 16)
            for t, (t0, n) in enumerate(TILES):
                sp.wait_ge(s["y"], t + 1)
                dst = a["y_prompt"][t0:t0 + n] if t < SAMPLE else a["y_sample"]
                sp.dma_start(dst, y_tok[0:n, t % 2]).then_inc(s_y[t % 2], 16)
            for i in range(2):
                sp.wait_ge(s_y[i], 16 * len(TILES[i::2]))
            sp.wait_ge(s["out"], 16 * (1 + 2 * NT))

        @block.gpsimd
        def _(pool):
            pool.dma_start(vecs[:], a["vecs"]).then_inc(s_vec, 16)
            pool.dma_start(consts[:], a["consts"]).then_inc(s_const, 16)
            for t, (t0, n) in enumerate(TILES):
                src = a["x_prompt"][t0:t0 + n] if t < SAMPLE else a["x_sample"]
                pool.dma_start(x_tok[0:n, t], src).then_inc(s_x[t], 16)
            pool.dma_start(ckvT[:, :, SEQ:NEW], a["cacheT"]).then_inc(s_cache, 16)
            pool.dma_start(krT[:, SEQ:NEW], a["krcacheT"]).then_inc(s_cache, 16)
            pool.wait_ge(s["wused"], END["w_uq"])
            pool.dma_start(w_uk[:], a["w_uk"]).then_inc(s_ukv, 16)
            pool.dma_start(w_uv[:], a["w_uv"]).then_inc(s_ukv, 16)
            pool.dma_start(wsT[:], a["wsT"]).then_inc(s_gm, 16)
            pool.dma_start(bs[:], a["b_s"].partition_broadcast(P)).then_inc(s_gm, 16)
            pool.wait_ge(s["vte"], NT)
            pool.dma_start(a["new_v"], v_tok[0:DEC, SAMPLE, :]).then_inc(s["out"], 16)
            pool.wait_ge(s["pve"], HEADS * NT)
            pool.dma_start(skT[:], a["skT"]).then_inc(s_sk, 16)
            for t, (t0, n) in enumerate(TILES):
                pool.wait_ge(s["ote"], t + 1)
                dst_c, dst_k = (a["ckv_p"][t0:t0 + n], a["kr_p"][t0:t0 + n]) if t < SAMPLE else (a["ckv_s"], a["kr_s"])
                pool.dma_start(dst_c, o_tok[0:n, t, 0:KVL]).then_inc(s["out"], 16)
                pool.dma_start(dst_k, o_tok[0:n, t, KVL:]).then_inc(s["out"], 16)

            G = SLOTS // GBUF
            for t, (t0, n) in enumerate(TILES):
                for half, table in enumerate((a["peer_u"], a["peer_v"])):
                    g0 = (2 * t + half) * G
                    with pool.Fori(0, G) as i:
                        for u in range(GBUF):
                            if u == 0:
                                pool.wait_ge(s["idx"], i + g0 + 1)
                                pool.sem_inc(s["group"], 1)
                            pool.indirect_dma_start(
                                out=gath[0:n, u, :], out_offset=None, in_=table,
                                in_offset=bass.IndirectOffsetOnAxis(ap=idx8[0:n, 0, u:u + 1], axis=0),
                                ).then_inc(s_g[u], 16)

        @block.tensor
        def _(pe):
            def mm(out, lhsT, rhs, start, stop):
                return nc.tensor.matmul(out, lhsT, rhs, start=start, stop=stop)

            pe.wait_ge(s_const, 16)
            pe.wait_ge(s["xn"], NT)
            for k in range(KD):
                if k >= 3:
                    pe.wait_ge(s["x0e"], k - 2)
                b0 = 1 + 2 * (k % 3)
                for t, (t0, n) in enumerate(TILES):
                    out = ps[:, b0, t0:t0 + n] if t < SAMPLE else ps[:, b0 + 1, 0:DEC]
                    ins = nc.tensor.transpose(out, x_tok[0:n, t, k * P:(k + 1) * P], ident[0:n, 0:n])
                ins.then_inc(s["xT"], 1)

            pe.wait_ge(s["silu"], 1)

            def ada(b, u):
                pe.wait_ge(s_w[u], 16 * (b // RING) + 16 if isinstance(b, int) else (b - u) * (16 // RING) + 16)
                for k in range(KD):
                    ins = mm(ps[:, 0, 0:96].rearrange("p (f c) -> p f c", c=2)[:, b, :],
                             w_raw[:, u, k * P:(k + 1) * P], silu_c[:, k, :], k == 0, k == KD - 1)
                ins.then_inc(s["adaused"], 1)
            in_steps(pe, ORDER["ada"], RING, ada)

            def linear(name):
                kk, s0 = WIDTH[name], SPLIT_AT[name]

                def one(b, u):
                    g = s0 + u
                    wait(pe, s["wlo"], b + s0 + 1)
                    wait(pe, s["evac"], b + s0 - 1)
                    for half, (c0, c1) in enumerate(HALVES):
                        n = 0
                        for k in range(kk):
                            for w, x in ((w_hi, act_hi), (w_hi, act_lo), (w_lo, act_hi)):
                                ins = mm(ps[:, 2 * (g % 2) + half, 0:H], w[:, g % 2, k * P:(k + 1) * P],
                                         x[:, k, c0:c1], n == 0, n == 3 * kk - 1)
                                n += 1
                    ins.then_inc(s["wused"], 1)
                in_steps(pe, ORDER[name], RING, one)

            def column_sums(bank, src, blocks):
                for half, (c0, c1) in enumerate(HALVES):
                    for i, k in enumerate(blocks):
                        ins = mm(ps[:, bank + half, 0:H], ones[:], src[:, k, c0:c1], i == 0, i == len(blocks) - 1)
                return ins

            pe.wait_ge(s["mod"], 1)
            pe.wait_ge(s["hlo"], KD)
            linear("w_in")

            pe.wait_ge(s["sqz"], 1)
            column_sums(4, tmp, range(QK))
            column_sums(6, tmp, range(QK, QK + CK)).then_inc(s["rowsA"], 1)
            pe.wait_ge(s["gelu"], 1)
            pe.wait_ge(s["evac"], END["w_in"])
            column_sums(0, z, range(Z_GV, Z_GV + GH)).then_inc(s["vmean"], 1)
            pe.wait_ge(s["vc2"], 1)
            column_sums(2, tmp, range(GH)).then_inc(s["vvar"], 1)
            pe.wait_ge(s["cqrow"], 2)
            for half, (c0, c1) in enumerate(HALVES):
                ins = mm(ps[:, 4 + half, 0:H], perm, z[:, Z_KR, c0:c1], True, True)
            ins.then_inc(s["krmm"], 1)
            pe.wait_ge(s["vn"], 1)
            pe.wait_ge(s["cqlo"], 1)
            linear("w_uq")
            pe.wait_ge(s["evac"], END["w_uq"])
            pe.wait_ge(s["krr"], 1)
            for j in range(2):
                for half, (c0, c1) in enumerate(HALVES):
                    ins = mm(ps[:, 4 + 2 * j + half, 0:H], perm, qT[:, HEADS + j, c0:c1], True, True)
            ins.then_inc(s["qmm"], 1)
            pe.wait_ge(s["ckvn"], 1)
            pe.wait_ge(s_cache, 32)
            pe.wait_ge(s_ukv, 32)
            KH = KEYS // 2
            for h in range(HEADS):
                if h >= 2:
                    pe.wait_ge(s["kev"], h - 1)
                for half in range(2):
                    for c in range(CK):
                        ins = mm(ps[:, 2 * (h % 2) + half, 0:KH], w_uk[:, c, h * P:(h + 1) * P],
                                 ckvT[:, c, half * KH:(half + 1) * KH], c == 0, c == CK - 1)
                ins.then_inc(s["kmm"], 1)
            pe.wait_ge(s["qr"], 2)
            for i in range(VT):
                n = P if i < VT - 1 else DEC
                if i >= 4:
                    pe.wait_ge(s["vev"], i - 3)
                for c in range(CK):
                    ins = mm(ps[0:n, 4 + i % 4, :], ckvT[:, c, i * P:i * P + n], w_uv[:, c, :], c == 0, c == CK - 1)
                ins.then_inc(s["vmm"], 1)
            pe.wait_ge(s["kev"], HEADS)
            for t, (t0, n) in enumerate(TILES):
                if t >= 4:
                    pe.wait_ge(s["vte"], t - 3)
                for g in range(GH):
                    ins = nc.tensor.transpose(ps[0:n, t % 4, g * P:(g + 1) * P], z[:, Z_GV + g, t0:t0 + n], ident)
                ins.then_inc(s["vtt"], 1)
            pe.wait_ge(s["vev"], VT)
            pe.wait_ge(s_gm, 32)
            pe.wait_ge(s["wsm"], 1)
            for t, (t0, n) in enumerate(TILES):
                pe.wait_ge(s["vte"], t + 1)
                if t >= 4:
                    pe.wait_ge(s["bt"], t - 3)
                for g in range(GH):
                    ins = mm(ps[:, 4 + t % 4, g * P:g * P + n], v_tok[0:n, t, g * P:(g + 1) * P],
                             wsT[0:n, g, 0:n], True, True)
                ins.then_inc(s["gmm"], 1)

            units = [(h, t) for h in range(HEADS) for t in range(NT)]

            def keys(t):
                return (0, (t + 1) * P) if t < SAMPLE else (SEQ, PAST + DEC)

            def key_blocks(t):
                k0, n = keys(t)
                return [(k0 + j * P, min(P, n - j * P)) for j in range((n + P - 1) // P)]

            def scores(i):
                h, t = units[i]
                t0, n = TILES[t]
                k0, nk = keys(t)
                if i >= 2:
                    pe.wait_ge(s["ex"], i - 1)
                r = ROPE * (h % 2)
                mm(ps[0:n, i % 2, 0:nk], qT[:, h, t0:t0 + n], kT[:, h, k0:k0 + nk], True, False)
                mm(ps[0:n, i % 2, 0:nk], qT[r:r + ROPE, HEADS + h // 2, t0:t0 + n],
                   krT[r:r + ROPE, k0:k0 + nk], False, True).then_inc(s["sc"], 1)

            pe.wait_ge(s["vte"], NT)
            pe.wait_ge(s["bt"], NT)
            scores(0)
            for i, (h, t) in enumerate(units):
                if i + 1 < len(units):
                    scores(i + 1)
                t0, n = TILES[t]
                kb = key_blocks(t)
                pe.wait_ge(s["pn"], i + 1)
                if i >= 2:
                    pe.wait_ge(s["pte"], i - 1)
                for j, (k0, nk) in enumerate(kb):
                    ins = nc.tensor.transpose(ps[0:nk, 2 + i % 2, j * P:j * P + n],
                                              prob[0:n, i % 2, j * P:j * P + nk], ident[0:n, 0:n])
                ins.then_inc(s["pt"], 1)
                pe.wait_ge(s["pte"], i + 1)
                if i >= 2:
                    pe.wait_ge(s["pve"], i - 1)
                for j, (k0, nk) in enumerate(kb):
                    ins = mm(ps[:, 4 + i % 2, 0:n], val[0:nk, k0 // P, h * VH:(h + 1) * VH],
                             probT[0:nk, i % 2, j, 0:n], j == 0, j == len(kb) - 1)
                ins.then_inc(s["pv"], 1)
            for t, (t0, n) in enumerate(TILES):
                k0 = t0 if t < SAMPLE else NEW
                if t >= 2:
                    pe.wait_ge(s["ote"], t - 1)
                for c in range(CK):
                    nc.tensor.transpose(ps[0:n, 6 + t % 2, c * P:(c + 1) * P], ckvT[:, c, k0:k0 + n], ident)
                nc.tensor.transpose(ps[0:n, 6 + t % 2, KVL:KVL + ROPE], krT[0:ROPE, k0:k0 + n],
                                    ident[0:ROPE, 0:ROPE]).then_inc(s["otr"], 1)

            pe.wait_ge(s["sqab"], 1)
            column_sums(0, sq, range(HEADS))
            column_sums(2, sq, range(HEADS, KD)).then_inc(s["rowsB"], 1)
            pe.wait_ge(s["rowr"], 2)
            pe.wait_ge(s["mlo"], 1)
            linear("w_o")
            pe.wait_ge(s["evac"], END["w_o"])
            column_sums(4, r_T, range(KD)).then_inc(s["mean1"], 1)
            pe.wait_ge(s["sq1"], 1)
            column_sums(6, sq, range(KD)).then_inc(s["var1"], 1)
            pe.wait_ge(s["h2lo"], 1)
            linear("w_pq")
            pe.wait_ge(s["evac"], END["w_pq"])
            pe.wait_ge(s_sk, 16)
            for t, (t0, n) in enumerate(TILES):
                if t >= 1:
                    pe.wait_ge(s["sev"], t)
                for j in range(HP):
                    ins = mm(ps[0:n, 4 + j // 4, (j % 4) * NK:(j % 4 + 1) * NK], qpT[:, j, t0:t0 + n],
                             skT[:, j, :], True, True)
                ins.then_inc(s["smm"], 1)
            for t, (t0, n) in enumerate(TILES):
                for k in range(KD):
                    ins = nc.tensor.transpose(ps[0:n, k // 4, (k % 4) * P:(k % 4 + 1) * P], h2T[:, k, t0:t0 + n], ident)
                ins.then_inc(s["h2t"], 1)
                pe.wait_ge(s["facc"], t + 1)
                for k in range(KD):
                    ins = nc.tensor.transpose(ps[:, 2 + k // 4, (k % 4) * P:(k % 4) * P + n],
                                              f_tok[0:n, k * P:(k + 1) * P], ident[0:n, 0:n])
                ins.then_inc(s["ft"], 1)
                pe.wait_ge(s["r2"], t + 1)
                for k in range(KD):
                    ins = nc.tensor.transpose(ps[0:n, 4 + k // 4, (k % 4) * P:(k % 4 + 1) * P], r_T[:, k, t0:t0 + n], ident)
                ins.then_inc(s["yt"], 1)

        @block.scalar
        def _(act):
            step = Chain(act, s_act)

            def f(out, in_, func=ACT.Copy, **kw):
                return nc.scalar.activation(out, in_, func, **kw)

            act.wait_ge(s_vec, 16)
            f(silu_c[:].rearrange("p k c -> p (k c)"), vecs[:, VEC_AT["c"]:VEC_AT["c"] + 16], ACT.Silu).then_inc(s["silu"], 1)
            act.wait_ge(s["var"], 1)
            f(std[:], rstd[:], ACT.Sqrt).then_inc(s["std"], 1)
            for k in range(KD):
                act.wait_ge(s["h32"], k + 1)
                f(act_hi[:, k], tmp[:, k]).then_inc(s["hhi"], 1)

            def linear(name, evacuate):
                kk, s0, g0 = WIDTH[name], SPLIT_AT[name], RING_AT[name]

                def loads(b, u):
                    first = (g0 + u) // RING + 1
                    return 16 * first if isinstance(b, int) and b < RING else (b - u) * (16 // RING) + 16 * first

                def one(b, u):
                    slot = (g0 + u) % RING
                    act.wait_ge(s_w[slot], loads(b, u))
                    wait(act, s["wused"], b + s0 - 1)
                    f(w_hi[:, (s0 + u) % 2, 0:kk * P], w_raw[:, slot, 0:kk * P]).then_inc(s["whi"], 1)
                    if evacuate is not None and not (isinstance(b, int) and b == 0):
                        out(b - 1, u - 1)

                def out(b, u):
                    act.wait_ge(s["wused"], b + s0 + 1)
                    pair = 2 * ((s0 + u) % 2)
                    f(evacuate[:, b, :].rearrange("p (s h) -> p s h", s=2), ps[:, pair:pair + 2, 0:H]).then_inc(s["evac"], 1)
                in_steps(act, ORDER[name], RING, one)
                if evacuate is not None:
                    out(ORDER[name] - 1, ORDER[name] - 1)

            linear("w_in", z)
            act.wait_ge(s["evac"], END["w_in"])
            f(tmp[:, 0:QK + CK], z[:, 0:QK + CK], ACT.Square).then_inc(s["sqz"], 1)
            f(z[:, Z_GU:], z[:, Z_GU:], ACT.Gelu_apprx_tanh).then_inc(s["gelu"], 1)
            act.wait_ge(s["cqrow"], 1)
            f(rows[:, 0:2], rows[:, 0:2], ACT.Sqrt).then_inc(s["std"], 1)
            act.wait_ge(s["vvarr"], 1)
            f(rows[:, 3], rows[:, 3], ACT.Sqrt).then_inc(s["std"], 1)
            act.wait_ge(s["cqn"], 1)
            f(act_hi[:, 0:QK], tmp[:, 0:QK]).then_inc(s["cqhi"], 1)
            linear("w_uq", qT)
            for h in range(HEADS):
                act.wait_ge(s["kmm"], h + 1)
                f(kT[:, h, :].rearrange("p (s h) -> p s h", s=2),
                  ps[:, 2 * (h % 2):2 * (h % 2) + 2, 0:KEYS // 2]).then_inc(s["kev"], 1)
            for i in range(VT):
                n = P if i < VT - 1 else DEC
                act.wait_ge(s["vmm"], i + 1)
                f(val[0:n, i, :], ps[0:n, 4 + i % 4, :]).then_inc(s["vev"], 1)
            for t, (t0, n) in enumerate(TILES):
                act.wait_ge(s["vtt"], t + 1)
                f(v_tok[0:n, t, :], ps[0:n, t % 4, :]).then_inc(s["vte"], 1)
            units = [(h, t) for h in range(HEADS) for t in range(NT)]
            for i, (h, t) in enumerate(units):
                t0, n = TILES[t]
                act.wait_ge(s["mx"], i + 1)
                if i >= 2:
                    act.wait_ge(s["pt"], i - 1)
                if t < SAMPLE:
                    for r in range(2):
                        nk = t * P + (r + 1) * CHUNK
                        rr = slice(r * CHUNK, (r + 1) * CHUNK)
                        ins = f(prob[rr, i % 2, 0:nk], ps[rr, i % 2, 0:nk], ACT.Exp, bias=negmax[rr, i:i + 1],
                                scale=SCALE, accum_out=rowsum[rr, i:i + 1])
                else:
                    ins = f(prob[0:n, i % 2, 0:PAST + DEC], ps[0:n, i % 2, 0:PAST + DEC], ACT.Exp,
                            bias=negmax[0:n, i:i + 1], scale=SCALE, accum_out=rowsum[0:n, i:i + 1])
                ins.then_inc(s["ex"], 1)
                act.wait_ge(s["pt"], i + 1)
                if i >= 2:
                    act.wait_ge(s["pv"], i - 1)
                if t < SAMPLE:
                    ins = f(probT[:, i % 2, 0:t + 1, :], ps[:, 2 + i % 2, 0:(t + 1) * P].rearrange("p (j n) -> p j n", n=P))
                else:
                    f(probT[:, i % 2, 0:2, 0:n], ps[:, 2 + i % 2, 0:2 * P].rearrange("p (j n) -> p j n", n=P)[:, :, 0:n])
                    ins = f(probT[0:DEC, i % 2, 2, 0:n], ps[0:DEC, 2 + i % 2, 2 * P:2 * P + n])
                ins.then_inc(s["pte"], 1)
            for t, (t0, n) in enumerate(TILES):
                act.wait_ge(s["otr"], t + 1)
                f(o_tok[0:n, t, :], ps[0:n, 6 + t % 2, 0:KVL + ROPE]).then_inc(s["ote"], 1)
            act.wait_ge(s["pve"], HEADS * NT)
            act.wait_ge(s["bt"], NT)
            act.wait_ge(s["otr"], NT)
            act.wait_ge(s["out"], 16 * (1 + 2 * NT))
            f(sq[:], tmp[:], ACT.Square).then_inc(s["sqab"], 1)
            act.wait_ge(s["rowr"], 1)
            f(rows[:, 0:2], rows[:, 0:2], ACT.Sqrt).then_inc(s["std"], 1)
            act.wait_ge(s["m"], 1)
            f(act_hi[:], tmp[:]).then_inc(s["mhi"], 1)
            linear("w_o", None)
            act.wait_ge(s["rc1"], 1)
            f(sq[:], r_T[:], ACT.Square).then_inc(s["sq1"], 1)
            act.wait_ge(s["varr"], 1)
            f(rows[:, 1], rows[:, 1], ACT.Sqrt).then_inc(s["std"], 1)
            act.wait_ge(s["h2"], 1)
            f(act_hi[:], h2T[:]).then_inc(s["h2hi"], 1)
            linear("w_pq", qpT)
            for t, (t0, n) in enumerate(TILES):
                act.wait_ge(s["smm"], t + 1)
                if t >= 1:
                    act.wait_ge(s["topk"], t)
                else:
                    act.wait_ge(s["wused"], END["w_pq"])
                f(score[0:n].rearrange("p j n -> p (j n)"), ps[0:n, 4:8, :].rearrange("p b n -> p (b n)")).then_inc(s["sev"], 1)
                act.wait_ge(s["fsub"], t + 1)
                f(fin[0:n].rearrange("p h k -> p (h k)"), score2[0:n, 0], ACT.Exp).then_inc(s["fexp"], 1)
            for t, (t0, n) in enumerate(TILES):
                act.wait_ge(s["h2t"], t + 1)
                if t >= 1:
                    act.wait_ge(s["act"], t)
                f(h2_tok[0:n], ps[0:n, 0:2, :].rearrange("p b n -> p (b n)")).then_inc(s["h2te"], 1)
                act.wait_ge(s["act"], t + 1)
                f(act_g[0:n], act_v[0:n], ACT.Gelu_apprx_tanh).then_inc(s["wgt"], 1)
                act.wait_ge(s["var2"], t + 1)
                f(std[0:n, t:t + 1], rstd[0:n, t:t + 1], ACT.Sqrt).then_inc(s["std2"], 1)

        @block.vector
        def _(dve):
            v = nc.vector
            step = Chain(dve, s_dve)
            v.memset(ones[:], 1.0).then_inc(s["ones"], 1)
            step(v.memset(meanvar[:], 1.0))
            for t, (t0, n) in enumerate(TILES):
                dve.wait_ge(s_x[t], 16)
                for j in range(2):
                    step(v.bn_stats(stats[0:n, j], x_tok[0:n, t, j * 512:(j + 1) * 512]))
                step(v.bn_aggr(meanvar[0:n, t], stats[0:n]))
            v.tensor_scalar(rstd[:], meanvar[:, :, 1], EPS, None, ALU.add).then_inc(s["var"], 1)
            dve.wait_ge(s["std"], 1)
            step(v.reciprocal(rstd[:], std[:]))
            for t, (t0, n) in enumerate(TILES):
                v.tensor_scalar(x_tok[0:n, t], x_tok[0:n, t], meanvar[0:n, t, 0:1], rstd[0:n, t:t + 1],
                                ALU.subtract, ALU.mult).then_inc(s["xn"], 1)
            dve.wait_ge(s_vec, 16)
            for k in range(KD):
                dve.wait_ge(s["xT"], k + 1)
                b0 = 1 + 2 * (k % 3)
                v.tensor_scalar(x0T[:, k, 0:SEQ], ps[:, b0, :], vec("ln_in_g", k), vec("ln_in_b", k), ALU.mult, ALU.add)
                v.tensor_scalar(x0T[:, k, SEQ:T], ps[:, b0 + 1, 0:DEC], vec("ln_in_g", k), vec("ln_in_b", k),
                                ALU.mult, ALU.add).then_inc(s["x0e"], 1)
            dve.wait_ge(s["adaused"], ORDER["ada"])
            b_ada = vecs[:, VEC_AT["b_ada"]:VEC_AT["b_ada"] + 48].unsqueeze(2).to_broadcast([P, 48, 2])
            step(v.tensor_tensor(mod[:], ps[:, 0, 0:96].rearrange("p (f c) -> p f c", c=2), b_ada, ALU.add))
            step(v.tensor_scalar(mod[:, 8:24], mod[:, 8:24], 1.0, None, ALU.add))
            v.tensor_scalar(mod[:, 32:48], mod[:, 32:48], 1.0, None, ALU.add).then_inc(s["mod"], 1)
            dve.wait_ge(s["mod"], 1)
            SH1, SC1, GT1, SH2, SC2, GT2 = (KD * i for i in range(6))
            STREAMS = ((0, SEQ, 0), (SEQ, T, 1))

            def modulate(out, src, k, scale, shift):
                for c0, c1, c in STREAMS:
                    ins = v.tensor_scalar(out[:, k, c0:c1], src[:, k, c0:c1], mod[:, scale + k, c:c + 1],
                                          mod[:, shift + k, c:c + 1], ALU.mult, ALU.add)
                return ins

            dve.wait_ge(s["x0e"], KD)
            for k in range(KD):
                modulate(tmp, x0T, k, SC1, SH1).then_inc(s["h32"], 1)
            for k in range(KD):
                dve.wait_ge(s["hhi"], k + 1)
                v.tensor_tensor(act_lo[:, k], tmp[:, k], act_hi[:, k].bitcast(F32), ALU.subtract).then_inc(s["hlo"], 1)

            def linear(name, extra=None):
                kk, s0, g0 = WIDTH[name], SPLIT_AT[name], RING_AT[name]

                def one(b, u):
                    slot, g = (g0 + u) % RING, (s0 + u) % 2
                    dve.wait_ge(s["whi"], b + s0 + 1)
                    v.tensor_tensor(w_lo[:, g, 0:kk * P], w_raw[:, slot, 0:kk * P],
                                    w_hi[:, g, 0:kk * P].bitcast(F32), ALU.subtract).then_inc(s["wlo"], 1)
                    if extra is not None and not (isinstance(b, int) and b == 0):
                        extra(b - 1, u - 1)
                in_steps(dve, ORDER[name], RING, one)
                if extra is not None:
                    extra(ORDER[name] - 1, ORDER[name] - 1)

            def pair(bank):
                return ps[:, bank:bank + 2, 0:H]

            def row(i):
                return rows[:, i].rearrange("p (s h) -> p s h", s=2)

            linear("w_in")
            dve.wait_ge(s["rowsA"], 1)
            v.tensor_scalar(row(0), pair(4), 1.0 / QL, EPS, ALU.mult, ALU.add)
            v.tensor_scalar(row(1), pair(6), 1.0 / KVL, EPS, ALU.mult, ALU.add).then_inc(s["cqrow"], 1)
            dve.wait_ge(s["vmean"], 1)
            step(v.tensor_scalar(row(2), pair(0), 1.0 / (GH * P), None, ALU.mult))
            for g in range(GH):
                step(v.tensor_tensor(z[:, Z_GV + g], z[:, Z_GV + g], rows[:, 2], ALU.subtract))
                ins = v.tensor_tensor(tmp[:, g], z[:, Z_GV + g], z[:, Z_GV + g], ALU.mult)
                if g < GH - 1:
                    step(ins)
            ins.then_inc(s["vc2"], 1)
            dve.wait_ge(s["vvar"], 1)
            v.tensor_scalar(row(3), pair(2), 1.0 / (GH * P), EPS, ALU.mult, ALU.add).then_inc(s["vvarr"], 1)
            dve.wait_ge(s["std"], 2)
            v.reciprocal(rows[:, 0:2], rows[:, 0:2]).then_inc(s["cqrow"], 1)
            dve.wait_ge(s["cqrow"], 2)
            for k in range(QK):
                ins = v.scalar_tensor_tensor(tmp[:, k], z[:, k], vec("g_q", k), rows[:, 0], ALU.mult, ALU.mult)
            ins.then_inc(s["cqn"], 1)
            for c in range(CK):
                for c0, c1, o in ((0, SEQ, 0), (SEQ, T, PAST)):
                    ins = v.scalar_tensor_tensor(ckvT[:, c, c0 + o:c1 + o], z[:, Z_CKV + c, c0:c1], vec("g_kv", c),
                                                 rows[:, 1, c0:c1], ALU.mult, ALU.mult)
            ins.then_inc(s["ckvn"], 1)
            dve.wait_ge(s["cqhi"], 1)
            v.tensor_tensor(act_lo[:, 0:QK], tmp[:, 0:QK], act_hi[:, 0:QK].bitcast(F32), ALU.subtract).then_inc(s["cqlo"], 1)
            dve.wait_ge(s["std"], 3)
            step(v.reciprocal(rows[:, 3], rows[:, 3]))
            for g in range(GH):
                ins = v.scalar_tensor_tensor(z[:, Z_GV + g], z[:, Z_GV + g], vec("g_v", g), rows[:, 3], ALU.mult, ALU.mult)
                step(ins)
                ins = v.tensor_scalar(z[:, Z_GV + g], z[:, Z_GV + g], vec("b_v", g), None, ALU.add)
                if g < GH - 1:
                    step(ins)
            ins.then_inc(s["vn"], 1)
            dve.wait_ge(s["krmm"], 1)
            dve.wait_ge(s["cqlo"], 1)
            kr_rot = rows[:, 0]
            dve.wait_ge(s["vn"], 1)
            step(v.tensor_tensor(row(0), pair(4), sinT.rearrange("p (s h) -> p s h", s=2), ALU.mult))
            step(v.tensor_tensor(rows[:, 1], z[:, Z_KR], cosT, ALU.mult))
            step(v.tensor_tensor(krT[:, 0:SEQ], rows[:, 0, 0:SEQ], rows[:, 1, 0:SEQ], ALU.add))
            v.tensor_tensor(krT[:, NEW:], rows[:, 0, SEQ:T], rows[:, 1, SEQ:T], ALU.add).then_inc(s["krr"], 1)
            dve.wait_ge(s["krr"], 1)
            linear("w_uq")
            dve.wait_ge(s["qmm"], 1)
            for j in range(2):
                step(v.tensor_tensor(row(2 + j), pair(4 + 2 * j), sinT.rearrange("p (s h) -> p s h", s=2), ALU.mult))
                step(v.tensor_tensor(rows[:, j], qT[:, HEADS + j], cosT, ALU.mult))
                v.tensor_tensor(qT[:, HEADS + j], rows[:, j], rows[:, 2 + j], ALU.add).then_inc(s["qr"], 1)
            dve.wait_ge(s_gm, 32)
            v.memset(wsT[CHUNK:P, :, 0:CHUNK], 0.0).then_inc(s["wsm"], 1)
            for t, (t0, n) in enumerate(TILES):
                dve.wait_ge(s["gmm"], t + 1)
                step(v.tensor_tensor(tmp[:, HEADS:KD, t0:t0 + n],
                                     ps[:, 4 + t % 4, :].rearrange("p (g n) -> p g n", n=P)[:, :, 0:n], bs[:, :, 0:n], ALU.add))
                v.tensor_tensor(tmp[:, HEADS:KD, t0:t0 + n], tmp[:, HEADS:KD, t0:t0 + n],
                                z[:, Z_GU:Z_GU + GH, t0:t0 + n], ALU.mult).then_inc(s["bt"], 1)
            units = [(h, t) for h in range(HEADS) for t in range(NT)]

            def head_out(i):
                h, t = units[i]
                t0, n = TILES[t]
                dve.wait_ge(s["pv"], i + 1)
                v.tensor_copy(tmp[:, h, t0:t0 + n], ps[:, 4 + i % 2, 0:n]).then_inc(s["pve"], 1)

            for i, (h, t) in enumerate(units):
                t0, n = TILES[t]
                dve.wait_ge(s["sc"], i + 1)
                if t < SAMPLE:
                    for r in range(2):
                        rr = slice(r * CHUNK, (r + 1) * CHUNK)
                        ins = v.tensor_reduce(rowmax[rr, i:i + 1], ps[rr, i % 2, 0:t * P + (r + 1) * CHUNK], AX.X, ALU.max)
                        step(ins)
                else:
                    step(v.tensor_reduce(rowmax[0:n, i:i + 1], ps[0:n, i % 2, 0:PAST + DEC], AX.X, ALU.max))
                v.tensor_scalar(negmax[0:n, i:i + 1], rowmax[0:n, i:i + 1], -SCALE, None, ALU.mult).then_inc(s["mx"], 1)
                dve.wait_ge(s["ex"], i + 1)
                step(v.reciprocal(rinv[0:n, i:i + 1], rowsum[0:n, i:i + 1]))
                if t < SAMPLE:
                    step(v.memset(prob[0:CHUNK, i % 2, t * P + CHUNK:(t + 1) * P], 0.0))
                nk = (t + 1) * P if t < SAMPLE else PAST + DEC
                v.tensor_scalar(prob[0:n, i % 2, 0:nk], prob[0:n, i % 2, 0:nk], rinv[0:n, i:i + 1], None,
                                ALU.mult).then_inc(s["pn"], 1)
                if i >= 1:
                    head_out(i - 1)
            head_out(len(units) - 1)
            dve.wait_ge(s["rowsB"], 1)
            for j in range(2):
                ins = v.tensor_scalar(row(j), pair(2 * j), 1.0 / (HEADS * VH), EPS, ALU.mult, ALU.add)
                step(ins) if j == 0 else ins.then_inc(s["rowr"], 1)
            dve.wait_ge(s["std"], 4)
            v.reciprocal(rows[:, 0:2], rows[:, 0:2]).then_inc(s["rowr"], 1)
            dve.wait_ge(s["rowr"], 2)
            for k in range(KD):
                g, j = ("g_out_a", k) if k < HEADS else ("g_out_b", k - HEADS)
                ins = v.scalar_tensor_tensor(tmp[:, k], tmp[:, k], vec(g, j), rows[:, k // HEADS], ALU.mult, ALU.mult)
                if k < KD - 1:
                    step(ins)
            ins.then_inc(s["m"], 1)
            v.tensor_scalar(x0T[:], x0T[:], ALPHA, None, ALU.mult).then_inc(s["ax"], 1)
            dve.wait_ge(s["mhi"], 1)
            v.tensor_tensor(act_lo[:], tmp[:], act_hi[:].bitcast(F32), ALU.subtract).then_inc(s["mlo"], 1)
            dve.wait_ge(s["ax"], 1)

            def residual(b, u):
                s0 = SPLIT_AT["w_o"]
                dve.wait_ge(s["wused"], b + s0 + 1)
                bank = 2 * ((s0 + u) % 2)
                for c0, c1, c in ((0, H, 0), (H, SEQ, 0), (SEQ, T, 1)):
                    half = c0 // H
                    ins = v.scalar_tensor_tensor(r_T[:, b, c0:c1], ps[:, bank + half, c0 - half * H:c1 - half * H],
                                                 mod[:, GT1 + b, c:c + 1], x0T[:, b, c0:c1], ALU.mult, ALU.add)
                ins.then_inc(s["evac"], 1)
            linear("w_o", residual)
            dve.wait_ge(s["evac"], END["w_o"])
            dve.wait_ge(s["mean1"], 1)
            step(v.tensor_scalar(row(0), pair(4), 1.0 / D, None, ALU.mult))
            row0 = rows[:, 0].unsqueeze(1).to_broadcast([P, KD, T])
            v.tensor_tensor(r_T[:], r_T[:], row0, ALU.subtract).then_inc(s["rc1"], 1)
            dve.wait_ge(s["var1"], 1)
            v.tensor_scalar(row(1), pair(6), 1.0 / D, EPS, ALU.mult, ALU.add).then_inc(s["varr"], 1)
            dve.wait_ge(s["std"], 5)
            step(v.reciprocal(rows[:, 1], rows[:, 1]))
            for k in range(KD):
                step(v.scalar_tensor_tensor(x0T[:, k], r_T[:, k], vec("ln1_g", k), rows[:, 1], ALU.mult, ALU.mult))
                step(v.tensor_scalar(x0T[:, k], x0T[:, k], vec("ln1_b", k), None, ALU.add))
            for k in range(KD):
                ins = modulate(h2T, x0T, k, SC2, SH2)
            ins.then_inc(s["h2"], 1)
            dve.wait_ge(s["h2hi"], 1)
            v.tensor_tensor(act_lo[:], h2T[:], act_hi[:].bitcast(F32), ALU.subtract).then_inc(s["h2lo"], 1)
            linear("w_pq")

            def top16(vals, idx, src, scratch):
                step(v.max(vals[:, 0:8], src))
                v.max_index(idx[:, 0:8], vals[:, 0:8], src)
                step(v.match_replace(scratch, vals[:, 0:8], src, -3.0e38))
                step(v.max(vals[:, 8:16], scratch))
                v.max_index(idx[:, 8:16], vals[:, 8:16], scratch)

            for t, (t0, n) in enumerate(TILES):
                dve.wait_ge(s["sev"], t + 1)
                for j in range(HP):
                    top16(top[0:n, j], top_i[0:n, j], score[0:n, j], score2[0:n, j])
                step(v.tensor_copy(e_f[0:n, 0, 0:1], top[0:n, 0, 0:1]))
                step(v.tensor_copy(top_f[0:n], top_i[0:n]))
                for h in range(PH):
                    s1 = top[0:n, 2 * h].unsqueeze(2).to_broadcast([n, TOPK, TOPK])
                    s2 = top[0:n, 2 * h + 1].unsqueeze(1).to_broadcast([n, TOPK, TOPK])
                    step(v.tensor_tensor(cand[0:n, h].rearrange("p (a b) -> p a b", a=TOPK), s1, s2, ALU.add))
                    top16(fin[0:n, h], pos[0:n, h], cand[0:n, h], cand2[0:n, h])
                step(v.tensor_copy(e_f[0:n, 0, 0:1], fin[0:n, 0, 0:1]))
                for half, (op, arg) in enumerate(((ALU.logical_shift_right, 4), (ALU.bitwise_and, 15))):
                    step(v.tensor_scalar(pos_a[0:n], pos[0:n], arg, None, op))
                    step(v.tensor_copy(e_f[0:n, 2], pos_a[0:n].rearrange("p h k -> p (h k)")))
                    where = e_f[0:n, 2].unsqueeze(2).to_broadcast([n, SLOTS, TOPK])
                    hit = cand[0:n].rearrange("p h (k a) -> p (h k) a", a=TOPK)
                    step(v.tensor_tensor(hit, iota[0:n].unsqueeze(1).to_broadcast([n, SLOTS, TOPK]), where, ALU.is_equal))
                    ids = top_f[0:n].rearrange("p (h q) a -> p h q a", q=2)[:, :, half, :].unsqueeze(2).to_broadcast([n, PH, TOPK, TOPK])
                    hit4 = cand[0:n].rearrange("p h (k a) -> p h k a", a=TOPK)
                    step(v.tensor_tensor(hit4, hit4, ids, ALU.mult))
                    step(v.tensor_reduce(e_f[0:n, half], hit, AX.X, ALU.add))
                step(v.scalar_tensor_tensor(e_f[0:n, 2], e_f[0:n, 0], float(NK), e_f[0:n, 1], ALU.mult, ALU.add))
                v.tensor_copy(expert[0:n, t], e_f[0:n, 2])
                most = fin[0:n, :, 0:1].to_broadcast([n, PH, TOPK])
                v.tensor_tensor(score2[0:n, 0].rearrange("p (h k) -> p h k", h=PH), fin[0:n], most,
                                ALU.subtract).then_inc(s["fsub"], 1)
                dve.wait_ge(s["fexp"], t + 1)
                step(v.tensor_reduce(ssum[0:n], fin[0:n], AX.X, ALU.add))
                step(v.reciprocal(ssum[0:n], ssum[0:n]))
                v.tensor_tensor(gate[0:n, t].rearrange("p (h k) -> p h k", h=PH), fin[0:n],
                                ssum[0:n].unsqueeze(2).to_broadcast([n, PH, TOPK]), ALU.mult).then_inc(s["topk"], 1)
            dve.wait_ge(s["topk"], NT)

            G = SLOTS // GBUF
            for t, (t0, n) in enumerate(TILES):
                def indices(g):
                    v.tensor_copy(idx8[0:n, 0], expert[0:n, t].rearrange("p (g u) -> p g u", u=GBUF)[:, g]).then_inc(s["idx"], 1)

                dve.wait_ge(s["h2te"], t + 1)
                for half in range(2):
                    g0 = (2 * t + half) * G
                    if half == 1:
                        dve.wait_ge(s["wgt"], t + 1)
                        step(v.tensor_tensor(act_g[0:n], act_g[0:n], gate[0:n, t], ALU.mult))
                        step(v.memset(f_tok[0:n], 0.0))
                    with step.loop(0, G, GBUF) as i:
                        indices(i)
                        for u in range(GBUF):
                            dve.wait_ge(s_g[u], i * 16 + 16 * g0 + 16)
                            if half == 0:
                                step(v.tensor_tensor_reduce(gath[0:n, u], gath[0:n, u], h2_tok[0:n], 1.0, 0.0,
                                                            ALU.mult, ALU.add, act8[0:n, u:u + 1]))
                                if u == GBUF - 1:
                                    v.tensor_copy(act_v[0:n].rearrange("p (g u) -> p g u", u=GBUF)[:, i], act8[0:n])
                            else:
                                step(v.scalar_tensor_tensor(
                                    f_tok[0:n], gath[0:n, u],
                                    act_g[0:n].rearrange("p (g u) -> p g u", u=GBUF)[:, i, u:u + 1],
                                    f_tok[0:n], ALU.mult, ALU.add))
                    if half == 0:
                        v.tensor_copy(ssum[0:n, 0:1], act_v[0:n, 0:1]).then_inc(s["act"], 1)
                v.tensor_copy(ssum[0:n, 0:1], f_tok[0:n, 0:1]).then_inc(s["facc"], 1)
                dve.wait_ge(s["ft"], t + 1)
                c = 0 if t < SAMPLE else 1
                for k in range(KD):
                    step(v.tensor_scalar(junk[:, 0:n], ps[:, 2 + k // 4, (k % 4) * P:(k % 4) * P + n],
                                         mod[:, GT2 + k, c:c + 1], None, ALU.mult))
                    ins = v.scalar_tensor_tensor(r_T[:, k, t0:t0 + n], x0T[:, k, t0:t0 + n], ALPHA, junk[:, 0:n],
                                                 ALU.mult, ALU.add)
                    step(ins) if k < KD - 1 else ins.then_inc(s["r2"], 1)
                dve.wait_ge(s["yt"], t + 1)
                if t == 0:
                    dve.wait_ge(s_gb, 32)
                if t >= 2:
                    dve.wait_ge(s_y[t % 2], 16 * (t // 2))
                for j in range(2):
                    step(v.bn_stats(stats[0:n, j], ps[0:n, 4 + j, :]))
                step(v.bn_aggr(meanvar[0:n, t], stats[0:n]))
                v.tensor_scalar(rstd[0:n, t:t + 1], meanvar[0:n, t, 1:2], EPS, None, ALU.add).then_inc(s["var2"], 1)
                dve.wait_ge(s["std2"], t + 1)
                step(v.reciprocal(rstd[0:n, t:t + 1], std[0:n, t:t + 1]))
                step(v.tensor_scalar(y_tok[0:n, t % 2], ps[0:n, 4:6, :].rearrange("p b n -> p (b n)"), meanvar[0:n, t, 0:1],
                                     rstd[0:n, t:t + 1], ALU.subtract, ALU.mult))
                step(v.tensor_tensor(y_tok[0:n, t % 2], y_tok[0:n, t % 2], gb2[0:n, 0], ALU.mult))
                v.tensor_tensor(y_tok[0:n, t % 2], y_tok[0:n, t % 2], gb2[0:n, 1], ALU.add).then_inc(s["y"], 1)


_OUTS = dict(y_prompt=(1, SEQ, D), y_sample=(1, DEC, D), ckv_p=(1, 1, SEQ, KVL), kr_p=(1, 1, SEQ, ROPE),
             ckv_s=(1, 1, DEC, KVL), kr_s=(1, 1, DEC, ROPE), new_v=(1, 1, DEC, GH * P))


def layout(x):
    import numpy as np

    def blocked(w):
        n = w.shape[1] // P
        return w.reshape(w.shape[0] // P, P, n, P).transpose(2, 1, 0, 3).reshape(n, P, w.shape[0])

    def columns(v):
        return v.reshape(-1, P).T

    x = {k: np.asarray(v) for k, v in x.items()}
    w_in = x["w_in"][0]
    kr = w_in[:, QL + KVL:QL + KVL + ROPE]
    w_in = np.concatenate([w_in[:, :QL + KVL], kr, kr, w_in[:, QL + KVL + ROPE:]], axis=1)
    uq = x["w_uq"][0].reshape(QL, HEADS, NOPE + ROPE)
    w_uq = np.concatenate([uq[:, :, :NOPE].reshape(QL, -1), uq[:, :, NOPE:].reshape(QL, -1)], axis=1)
    c = np.stack([x["c_prompt"][0], x["c_sample"][0]])
    vecs = {k: columns(x[k].reshape(-1)) for k in VEC_LEN if k != "c"}
    vecs["c"] = c.reshape(2, KD, P).transpose(2, 1, 0).reshape(P, 2 * KD)
    krc = x["cache_krope"][0, 0].T
    half = ROPE // 2
    freq = np.power(np.float32(10000.0), -np.arange(half, dtype=np.float32) * np.float32(2.0 / ROPE)).astype(np.float32)
    positions = np.concatenate([np.arange(SEQ), PAST + np.arange(DEC)]).astype(np.float32)
    angle = positions[:, None] * freq[None, :]
    cos = np.tile(np.cos(angle).T, (4, 1))
    sin = np.tile(np.concatenate([-np.sin(angle).T, np.sin(angle).T]), (2, 1))
    perm = np.zeros((P, P))
    perm[np.arange(P) ^ half, np.arange(P)] = 1.0
    consts = np.concatenate([np.eye(P), perm, cos, sin, np.tile(np.arange(TOPK), (P, 1))], axis=1).astype(np.float32)
    out = dict(
        x_prompt=x["x_prompt"][0], x_sample=x["x_sample"][0], consts=consts,
        vecs=np.concatenate([vecs[k] for k in VEC_LEN], axis=1),
        cacheT=x["cache_ckv"][0, 0].T.reshape(CK, P, PAST).transpose(1, 0, 2),
        krcacheT=np.concatenate([krc, krc], axis=0),
        ada=blocked(x["w_ada"][0]), w_in=blocked(w_in), w_uq=blocked(w_uq), w_o=blocked(x["w_o"][0]), w_pq=blocked(x["w_pq"][0]),
        w_uk=x["w_uk"][0].reshape(CK, P, -1).transpose(1, 0, 2), w_uv=x["w_uv"][0].reshape(CK, P, -1).transpose(1, 0, 2),
        wsT=x["w_s"][0].transpose(2, 0, 1), b_s=x["b_s"][0].reshape(-1),
        skT=x["sub_keys"][0].transpose(3, 0, 1, 2).reshape(P, HP, NK),
        peer_u=x["peer_u"][0], peer_v=x["peer_v"][0], ln2_g=x["ln2_g"][0], ln2_b=x["ln2_b"][0])
    return {k: np.ascontiguousarray(v) for k, v in out.items()}


def kernel(**inputs):
    import concourse.bacc as bacc
    from concourse.bass_utils import run_bass_kernel_spmd

    nc = bacc.Bacc("TRN2", target_bir_lowering=False, num_devices=1)
    arrays = layout(inputs)
    a = {k: nc.dram_tensor(k, v.shape, F32, kind="ExternalInput").ap() for k, v in arrays.items()}
    for k, shape in _OUTS.items():
        a[k] = nc.dram_tensor(k, shape[-2:], F32, kind="ExternalOutput").ap()
    build(nc, a)
    r = run_bass_kernel_spmd(nc, [arrays], core_ids=[0])
    return tuple(r.results[0][k].reshape(shape) for k, shape in _OUTS.items())
```

```python
from contextlib import ExitStack

import concourse.bass as bass
from concourse import mybir

F32 = mybir.dt.float32
F32R = mybir.dt.float32r
U32 = mybir.dt.uint32
ALU = mybir.AluOpType
ACT = mybir.ActivationFunctionType
AX = mybir.AxisListType

P = 128
D = 1024
KD = D // P
SEQ, DEC, PAST = 512, 64, 256
T = SEQ + DEC
H = T // 2
HALVES = ((0, H), (H, T))
TILES = [(t * P, P) for t in range(SEQ // P)] + [(SEQ, DEC)]
NT = len(TILES)
SAMPLE = NT - 1
CHUNK = 64
HEADS, NOPE, ROPE, VH = 4, 128, 64, 128
QL, KVL = 768, 256
QK, CK = QL // P, KVL // P
GH = 4
KEYS = SEQ + PAST + DEC
NEW = SEQ + PAST
VT = 7
PH, NK, TOPK = 8, 128, 16
HP = 2 * PH
SLOTS = PH * TOPK
EPS = 1e-6
ALPHA = 2.0 ** 0.25
SCALE = (NOPE + ROPE) ** -0.5
Z_CKV, Z_KR, Z_GU, Z_GV, Z_N = QK, QK + CK, QK + CK + 1, QK + CK + 1 + GH, QK + CK + 1 + 2 * GH
VEC_LEN = dict(ln_in_g=8, ln_in_b=8, b_ada=48, g_q=QK, g_kv=CK, g_v=GH, b_v=GH, g_out_a=HEADS,
               g_out_b=GH, ln1_g=8, ln1_b=8, c=16)
VEC_AT = {}
for _name, _n in VEC_LEN.items():
    VEC_AT[_name] = sum(VEC_LEN[k] for k in VEC_AT)
NVEC = sum(VEC_LEN.values())
C_ID, C_PERM, C_COS, C_SIN, C_IOTA = 0, P, 2 * P, 2 * P + T, 2 * P + 2 * T
C_START = C_IOTA + P
NCONST = C_START + 2 * TOPK
ROW = [TOPK // (a + 1) for a in range(TOPK)]
START = [sum(ROW[:a]) for a in range(TOPK)]
NCAND = sum(ROW)
ND = T - P
PTILES = [(t * P, min(P, ND - t * P)) for t in range((ND + P - 1) // P)] + [(ND, P)]
NPT = len(PTILES)
GS = 64
NG = ND // GS
GROUP = 4
NB = NK
NGR = NB // GROUP
PER = 2 * SLOTS // NGR
GB = 4
RING = 4
ORDER = dict(ada=48, w_in=Z_N, w_uq=6, w_o=KD, w_pq=HP)
RING_AT, SPLIT_AT = {}, {}
_g = 0
for _name, _n in ORDER.items():
    RING_AT[_name] = _g
    SPLIT_AT[_name] = _g - ORDER["ada"]
    _g += _n
WIDTH = dict(ada=KD, w_in=KD, w_uq=QK, w_o=KD, w_pq=KD)


def wait(eng, sem, value):
    if not (isinstance(value, int) and value <= 0):
        eng.wait_ge(sem, value)


def in_steps(eng, n, unroll, body):
    full = n // unroll
    for b in range(min(n, unroll)):
        body(b, b)
    if full > 2:
        with eng.Fori(1, full) as i:
            for u in range(unroll):
                body(i * unroll + u, u)
    elif full == 2:
        for u in range(unroll):
            body(unroll + u, u)
    for b in range(max(full, 1) * unroll, n):
        body(b, b - full * unroll)


class Step:

    def __init__(self, at, i=None, by=0):
        self.at, self.i, self.by = at, i, by

    def __call__(self, times=1, plus=0):
        at = self.at * times + plus
        if self.i is None:
            return at
        assert at >= 0
        return self.i * (self.by * times) + at if at else self.i * (self.by * times)


class Chain:

    def __init__(self, eng, sem):
        self.eng, self.sem, self.n = eng, sem, 0

    def __call__(self, ins):
        ins.then_inc(self.sem, 1)
        self.n += 1
        self.eng.wait_ge(self.sem, self.n)


def build(nc, a):
    with ExitStack() as ctx:
        def sem(name):
            return ctx.enter_context(nc.semaphore(name))

        base = 16512

        def at(name, shape, offset, dt=F32):
            return nc.alloc_sbuf_tensor_at(name, shape, dt, offset=base + offset)

        o = 0
        regions = {}
        for name, size in dict(consts=NCONST * 4, vecs=NVEC * 4, ones=512, mod=96 * 4, small=2048, x0=KD * T * 4,
                               hi=KD * T * 4, lo=KD * T * 4, wraw=RING * 4096, wsplit=4 * 4096,
                               z=Z_N * T * 4, tmp=KD * T * 4, rows=4 * T * 4,
                               q=6 * T * 4, k=HEADS * KEYS * 4, kr=KEYS * 4, ckv=CK * KEYS * 4,
                               p=8192).items():
            regions[name] = o
            o += (size + 31) // 32 * 32
        assert base + o <= 229344, base + o
        R = regions
        consts = at("consts_sb", [P, NCONST], R["consts"])
        vecs = at("vecs_sb", [P, NVEC], R["vecs"])
        ones = at("ones", [P, P], R["ones"])
        mod = at("mod", [P, 48, 2], R["mod"])
        silu_c = at("silu_c", [P, KD, 2], R["small"])
        stats = at("stats", [P, 2, 6], R["small"] + 64)
        meanvar = at("meanvar", [P, NT, 2], R["small"] + 128)
        rstd = at("rstd", [P, NT], R["small"] + 192)
        std = at("std", [P, NT], R["small"] + 224)
        negmax = at("negmax", [P, 32], R["small"] + 256)
        rowmax = at("rowmax", [P, 32], R["small"] + 384)
        rowsum = at("rowsum", [P, 32], R["small"] + 512)
        rinv = at("rinv", [P, 32], R["small"] + 640)
        x0T = at("x0T", [P, KD, T], R["x0"])
        act_hi = at("act_hi", [P, KD, T], R["hi"], F32R)
        act_lo = at("act_lo", [P, KD, T], R["lo"], F32R)
        w_raw = at("w_raw", [P, RING, D], R["wraw"])
        w_hi = at("w_hi", [P, 2, D], R["wsplit"], F32R)
        w_lo = at("w_lo", [P, 2, D], R["wsplit"] + 8192, F32R)
        z = at("z", [P, Z_N, T], R["z"])
        x_tok = at("x_tok", [P, NT, D], R["z"])
        val = at("val", [P, VT, HEADS * VH], R["z"])
        r_T = at("r_T", [P, KD, T], R["z"])
        h2T = at("h2T", [P, KD, T], R["z"] + KD * T * 4)
        tmp = at("tmp", [P, KD, T], R["tmp"])
        rows = at("rows", [P, 4, T], R["rows"])
        qT = at("qT", [P, 6, T], R["q"])
        kT = at("kT", [P, HEADS, KEYS], R["k"])
        krT = at("krT", [P, KEYS], R["kr"])
        ckvT = at("ckvT", [P, CK, KEYS], R["ckv"])
        sq = at("sq", [P, KD, T], R["q"])
        prob = at("prob", [P, 2, SEQ], R["p"])
        probT = at("probT", [P, 2, 4, P], R["p"] + 4096)
        v_tok = at("v_tok", [P, NT, GH * P], R["hi"])
        wsT = at("wsT_sb", [P, GH, P], R["hi"] + 10240)
        bs = at("bs_sb", [P, GH, P], R["hi"] + 12288)
        w_uk = at("w_uk_sb", [P, CK, HEADS * NOPE], R["lo"])
        w_uv = at("w_uv_sb", [P, CK, HEADS * VH], R["lo"] + 4096)
        o_tok = at("o_tok", [P, NT, KVL + ROPE], R["rows"])

        B = R["z"]
        skT = at("skT_sb", [P, HP, NK], B)
        q_blk = at("q_blk", [P, 2, T], B + 8192)
        found = at("found", [P, 2, NPT, TOPK], B + 12800)
        found_i = at("found_i", [P, 2, NPT, TOPK], B + 13440, U32)
        scratch = at("scratch", [P, NK], B + 14080)
        piece = at("piece", [P, 2, NK, GS], B)
        hit = at("hit", [P, SLOTS, TOPK], B + 65536)
        o = B + 73728

        def small(name, shape, dt=F32):
            nonlocal o
            n = 4
            for x in shape[1:]:
                n *= x
            n = (n + 31) // 32 * 32
            o += n
            return at(name, shape, o - n, dt)
        cand = small("cand", [P, PH, NCAND])
        cand2 = small("cand2", [P, NCAND + 2])
        fin = small("fin", [P, PH, TOPK])
        pos = small("pos", [P, PH, TOPK], U32)
        pos_f = small("pos_f", [P, SLOTS])
        num_u = small("num_u", [P, 2, SLOTS], U32)
        num_f = small("num_f", [P, SLOTS])
        step_i = small("step_i", [P, PH, TOPK])
        diff = small("diff", [P, SLOTS])
        expo = small("expo", [P, SLOTS])
        ssum = small("ssum", [P, 16])
        chosen = small("chosen", [P, 3, SLOTS])
        assert o <= B + 81920
        top = at("top", [P, NPT, HP, TOPK], B + 90112)
        top_f = at("top_f", [P, NPT, HP, TOPK], B + 95232)
        sel = at("sel", [P, 3, ND], B + 100352)
        one_i = at("one_i", [P, 2, 8, NK], R["wsplit"])
        one_j = at("one_j", [P, 2, 8, NK], R["wsplit"] + 8192)
        expert = at("expert", [P, SLOTS], B + 113920, U32)
        gate_s = at("gate_s", [P, SLOTS], B + 114432)
        assert base + B + 114944 <= 229344
        v_hi = at("v_hi", [P, GROUP, D], B, F32R)
        v_lo = at("v_lo", [P, GROUP, D], B + 16384, F32R)
        GA = GROUP * ND * 4
        ga_hi = at("ga_hi", [P, 2, GROUP, ND], B + 32768, F32R)
        ga_lo = at("ga_lo", [P, 2, GROUP, ND], B + 32768 + 2 * GA, F32R)
        gath = at("gath", [P, GB, D], B + 32768 + 4 * GA)
        assert 32768 + 4 * GA + GB * 4096 <= 86016
        h2_tok = at("h2_tok", [P, D], B + 86016)
        f_tok = at("f_tok", [P, D], B + 90112)
        g_in = at("g_in", [P, 2, NG, 2, GS], B + 94208)
        a_g = at("a_g", [P, 2, ND], B + 101376)
        ga32 = at("ga32", [P, 2, ND], B + 104960)
        act_v = at("act_v", [P, SLOTS], B + 108544)
        act_g = at("act_g", [P, SLOTS], B + 109056)
        idx8 = at("idx8", [P, 2, PER], B + 109568, U32)
        act8 = at("act8", [P, 2, PER], B + 109632)

        def quarter(x, c):
            return x[:, :, c * D // 4:(c + 1) * D // 4]

        def raw_quarter(c):
            return w_raw[:, 2 + c % 2].rearrange("p (e n) -> p e n", e=GROUP)
        y_tok = at("y_tok", [P, 2, D], B)
        gb2 = at("gb2", [P, 2, D], B + 8192)
        ident = consts[:, C_ID:C_ID + P]
        perm = consts[:, C_PERM:C_PERM + P]
        cosT = consts[:, C_COS:C_COS + T]
        sinT = consts[:, C_SIN:C_SIN + T]
        iota = consts[:, C_IOTA:C_IOTA + NK]

        def vec(name, k):
            return vecs[:, VEC_AT[name] + k:VEC_AT[name] + k + 1]

        ps = ctx.enter_context(nc.psum_tensor("ps", [P, 8, 512], F32))

        s_const, s_vec, s_cache, s_ukv, s_gm, s_sk, s_gb = map(sem, "s_const s_vec s_cache s_ukv s_gm s_sk s_gb".split())
        s_x = [sem(f"x_landed{i}") for i in range(NT)]
        s_w = [sem(f"w_landed{i}") for i in range(RING)]
        s_dve, s_act = sem("own_dve"), sem("own_act")
        names = """ones silu adaused ada var std xn xT x0e mod h32 hhi hlo whi wlo wused evac
            sqz rowsA cqrow gelu vmean vc2 vvar vvarr vn cqn cqhi cqlo ckvn krmm krr qmm qr kmm kev vmm vev
            vtt vte gmm bt sc mx ex pn pt pte pv pve rowsB rowr sqab mhi mlo m
            r1 mean1 meanr rc1 sq1 var1 varr h2 h2hi h2lo smm sev topk
            h2t h2te gd idx act wgt fsub fexp top1 chose selt sele onei eqj onej gmat gst
            uhi ulo vhi vlo amm ag ga gahi galo fmm fe dots var2 std2 wsm ax group facc ft fte r2 yt y out otr ote vot""".split()
        s = {n: sem("s_" + n) for n in names}
        s_y = [sem(f"y_written{i}") for i in range(2)]
        s_g = [sem(f"rows_landed{i}") for i in range(GB)]
        s_u = [sem(f"u_landed{i}") for i in range(2)]
        s_v = [sem(f"v_landed{i}") for i in range(2)]
        s_gi = [sem(f"gates_landed{i}") for i in range(2)]
        s_gw = [sem(f"gates_written{i}") for i in range(2)]
        gates = nc.dram_tensor("dense_gates", (NG, P, NK, GS), F32, kind="Internal").ap()

        block = ctx.enter_context(nc.Block())

        N_LIN = ORDER["w_in"] + ORDER["w_uq"] + ORDER["w_o"] + ORDER["w_pq"]
        END = {n: SPLIT_AT[n] + ORDER[n] for n in ORDER}

        def each_step(eng, step):
            mid = NGR // 2

            def pairs(first, end, half):
                with eng.Fori(0, (end - first) // 2) as i:
                    step(Step(first, i, 2), 1, half)
                    step(Step(first + 1, i, 2), 0, half)
            step(Step(0), 0, 0, "first")
            step(Step(1), 1, 0)
            step(Step(2), 0, 0)
            pairs(3, mid - 1, 0)
            step(Step(mid - 1), 1, 0, "turn")
            step(Step(mid), 0, 1)
            pairs(mid + 1, NGR - 1, 1)
            step(Step(NGR - 1), 1, 1, "last")
            step(Step(NGR), 0, 1, "tail")

        def each_eight(eng, q, body):
            n = GS // 8
            if q == 0:
                for u in range(2):
                    body(Step(u), Step(u), u)
            first = 2 if q == 0 else 0
            with eng.Fori(0, (n - first) // 2) as i:
                for u in range(2):
                    body(Step(q * n + first + u, i, 2), Step(first + u, i, 2), u)

        @block.sync
        def _(sp):
            def stream(name, dram):
                width = WIDTH[name] * P
                g0, s0 = RING_AT[name], SPLIT_AT[name]

                def load(b, u):
                    slot = (g0 + u) % RING
                    if name == "ada" or (isinstance(b, int) and g0 + b - RING < ORDER["ada"]):
                        wait(sp, s["adaused"], b + g0 - RING + 1)
                    else:
                        wait(sp, s["wlo"], b + s0 - RING + 1)
                    sp.dma_start(w_raw[:, slot, 0:width], dram[b]).then_inc(s_w[slot], 16)
                in_steps(sp, ORDER[name], RING, load)

            for name in ORDER:
                stream(name, a[name])
            for q in range(NG):
                sp.wait_ge(s["gst"], GS // 4 * (q + 1))
                sp.dma_start(gates[q], piece[:, q % 2]).then_inc(s_gw[q % 2], 16)

            def load_u(g, j, slot):
                wait(sp, s["ulo"], g(GROUP, j - 1))
                sp.dma_start(w_raw[:, slot], a["peer_uT"][g(GROUP, j)]).then_inc(s_u[slot], 16)

            def load_v(g, c):
                wait(sp, s["vlo"], g(4, c - 1))
                sp.dma_start(w_raw[:, 2 + c % 2], a["peer_vq"].rearrange("g c p n -> (g c) p n")[g(4, c)]).then_inc(s_v[c % 2], 16)

            def load_gates(g, pair):
                wait(sp, s["ga"], g(GROUP, 2 * pair + 2 - GROUP))
                src = gates.rearrange("s j (b i) t -> b j s (i t)", i=2)[g(2, pair)]
                sp.dma_start(g_in[:, pair].rearrange("p s i t -> p s (i t)"), src).then_inc(s_gi[pair], 16)

            sp.wait_ge(s["wlo"], N_LIN)
            for b in range(2):
                load_u(Step(0), b, b)
            for i in range(2):
                sp.wait_ge(s_gw[i], 16 * len(range(i, NG, 2)))
            sp.wait_ge(s["sele"], NPT - 1)
            sp.wait_ge(s["chose"], NPT)
            for pair in range(2):
                load_gates(Step(0), pair)
            load_v(Step(0), 0)

            def sp_step(g, par, half, edge=None):
                if edge == "tail":
                    return
                for j in range(GROUP):
                    if not (edge == "last" and j >= 2):
                        load_u(g, j + 2, j % 2)
                    if j == 0:
                        load_v(g, 1)
                    if j == 1 and edge != "first":
                        load_gates(g, 1)
                    if j == 3 and edge != "last":
                        load_gates(Step(g.at + 1, g.i, g.by), 0)
                for c in (2, 3, 4):
                    if not (edge == "last" and c == 4):
                        load_v(g, c)
            each_step(sp, sp_step)
            sp.wait_ge(s["fmm"], KD * NGR)
            sp.dma_start(gb2[:, 0], a["ln2_g"].partition_broadcast(P)).then_inc(s_gb, 16)
            sp.dma_start(gb2[:, 1], a["ln2_b"].partition_broadcast(P)).then_inc(s_gb, 16)
            for t, (t0, n) in enumerate(TILES):
                sp.wait_ge(s["y"], t + 1)
                dst = a["y_prompt"][t0:t0 + n] if t < SAMPLE else a["y_sample"]
                sp.dma_start(dst, y_tok[0:n, t % 2]).then_inc(s_y[t % 2], 16)
            for i in range(2):
                sp.wait_ge(s_y[i], 16 * len(TILES[i::2]))
            sp.wait_ge(s["out"], 16 * (1 + 2 * NT))

        @block.gpsimd
        def _(pool):
            pool.dma_start(vecs[:], a["vecs"]).then_inc(s_vec, 16)
            pool.dma_start(consts[:], a["consts"]).then_inc(s_const, 16)
            for t, (t0, n) in enumerate(TILES):
                src = a["x_prompt"][t0:t0 + n] if t < SAMPLE else a["x_sample"]
                pool.dma_start(x_tok[0:n, t], src).then_inc(s_x[t], 16)
            pool.dma_start(ckvT[:, :, SEQ:NEW], a["cacheT"]).then_inc(s_cache, 16)
            pool.dma_start(krT[:, SEQ:NEW], a["krcacheT"]).then_inc(s_cache, 16)
            pool.wait_ge(s["wused"], END["w_uq"])
            pool.dma_start(w_uk[:], a["w_uk"]).then_inc(s_ukv, 16)
            pool.dma_start(w_uv[:], a["w_uv"]).then_inc(s_ukv, 16)
            pool.dma_start(wsT[:], a["wsT"]).then_inc(s_gm, 16)
            pool.dma_start(bs[:], a["b_s"].partition_broadcast(P)).then_inc(s_gm, 16)
            pool.wait_ge(s["vte"], NT)
            pool.dma_start(a["new_v"], v_tok[0:DEC, SAMPLE, :]).then_inc(s["out"], 16)
            for t, (t0, n) in enumerate(TILES):
                pool.wait_ge(s["ote"], t + 1)
                dst_c, dst_k = (a["ckv_p"][t0:t0 + n], a["kr_p"][t0:t0 + n]) if t < SAMPLE else (a["ckv_s"], a["kr_s"])
                pool.dma_start(dst_c, o_tok[0:n, t, 0:KVL]).then_inc(s["out"], 16)
                pool.dma_start(dst_k, o_tok[0:n, t, KVL:]).then_inc(s["out"], 16)

            pool.wait_ge(s["h2"], 1)
            pool.dma_start(skT[:], a["skT"]).then_inc(s_sk, 16)
            for b in range(HP):
                slot, g = (RING_AT["w_pq"] + b) % RING, (SPLIT_AT["w_pq"] + b) % 2
                pool.wait_ge(s["whi"], SPLIT_AT["w_pq"] + b + 1)
                nc.gpsimd.tensor_tensor(w_lo[:, g], w_raw[:, slot], w_hi[:, g].bitcast(F32), ALU.subtract).then_inc(s["wlo"], 1)

            def eight_gates(g, k, w):
                pool.wait_ge(s["eqj"], g(1, 1))
                if g.i is not None:
                    pool.sem_inc(s["group"], 1)
                gate = sel[:, 2].rearrange("p (g u) -> p g u", u=8)[:, g()]
                nc.gpsimd.tensor_tensor(one_j[:, w], one_j[:, w], gate.unsqueeze(2).to_broadcast([P, 8, NK]),
                                        ALU.mult).then_inc(s["onej"], 1)
            for q in range(NG):
                each_eight(pool, q, eight_gates)

            pool.wait_ge(s["chose"], NPT)
            for i in range(2):
                pool.wait_ge(s_gw[i], 16 * len(range(i, NG, 2)))

            def pool_step(g, par, half, edge=None):
                if edge == "tail":
                    return
                table = a["peer_v"] if half else a["peer_u"]
                looped = g.i is not None
                for u in range(PER):
                    if u == 0:
                        pool.wait_ge(s["idx"], g(1, 1))
                        if looped:
                            pool.sem_inc(s["group"], 1)
                    if not (edge == "first" and u < GB):
                        pool.wait_ge(s["gd"], g(PER, u - GB + 1))
                        if looped:
                            pool.sem_inc(s["group"], 1)
                    pool.indirect_dma_start(out=gath[:, u % GB, :], out_offset=None, in_=table,
                                            in_offset=bass.IndirectOffsetOnAxis(ap=idx8[:, par, u:u + 1], axis=0)
                                            ).then_inc(s_g[u % GB], 16)
            each_step(pool, pool_step)

        @block.tensor
        def _(pe):
            def mm(out, lhsT, rhs, start, stop):
                return nc.tensor.matmul(out, lhsT, rhs, start=start, stop=stop)

            pe.wait_ge(s_const, 16)
            pe.wait_ge(s["xn"], NT)
            for k in range(KD):
                if k >= 3:
                    pe.wait_ge(s["x0e"], k - 2)
                b0 = 1 + 2 * (k % 3)
                for t, (t0, n) in enumerate(TILES):
                    out = ps[:, b0, t0:t0 + n] if t < SAMPLE else ps[:, b0 + 1, 0:DEC]
                    ins = nc.tensor.transpose(out, x_tok[0:n, t, k * P:(k + 1) * P], ident[0:n, 0:n])
                ins.then_inc(s["xT"], 1)

            pe.wait_ge(s["silu"], 1)

            def ada(b, u):
                pe.wait_ge(s_w[u], 16 * (b // RING) + 16 if isinstance(b, int) else (b - u) * (16 // RING) + 16)
                for k in range(KD):
                    ins = mm(ps[:, 0, 0:96].rearrange("p (f c) -> p f c", c=2)[:, b, :],
                             w_raw[:, u, k * P:(k + 1) * P], silu_c[:, k, :], k == 0, k == KD - 1)
                ins.then_inc(s["adaused"], 1)
            in_steps(pe, ORDER["ada"], RING, ada)

            def linear(name, behind=None):
                kk, s0 = WIDTH[name], SPLIT_AT[name]

                def one(b, u):
                    g = s0 + u
                    wait(pe, s["wlo"], b + s0 + 1)
                    wait(pe, s["evac"], b + s0 - 1)
                    for half, (c0, c1) in enumerate(HALVES):
                        n = 0
                        for k in range(kk):
                            for w, x in ((w_hi, act_hi), (w_hi, act_lo), (w_lo, act_hi)):
                                ins = mm(ps[:, 2 * (g % 2) + half, 0:H], w[:, g % 2, k * P:(k + 1) * P],
                                         x[:, k, c0:c1], n == 0, n == 3 * kk - 1)
                                n += 1
                    ins.then_inc(s["wused"], 1)
                    if behind is not None and not (isinstance(b, int) and b == 0):
                        behind(b - 1, u - 1)
                in_steps(pe, ORDER[name], RING, one)
                if behind is not None:
                    behind(ORDER[name] - 1, ORDER[name] - 1)

            def column_sums(bank, src, blocks):
                for half, (c0, c1) in enumerate(HALVES):
                    for i, k in enumerate(blocks):
                        ins = mm(ps[:, bank + half, 0:H], ones[:], src[:, k, c0:c1], i == 0, i == len(blocks) - 1)
                return ins

            pe.wait_ge(s["mod"], 1)
            pe.wait_ge(s["hlo"], KD)
            linear("w_in")

            pe.wait_ge(s["sqz"], 1)
            column_sums(4, tmp, range(QK))
            column_sums(6, tmp, range(QK, QK + CK)).then_inc(s["rowsA"], 1)
            pe.wait_ge(s["gelu"], 1)
            pe.wait_ge(s["evac"], END["w_in"])
            column_sums(0, z, range(Z_GV, Z_GV + GH)).then_inc(s["vmean"], 1)
            pe.wait_ge(s["vc2"], 1)
            column_sums(2, tmp, range(GH)).then_inc(s["vvar"], 1)
            pe.wait_ge(s["cqrow"], 2)
            for half, (c0, c1) in enumerate(HALVES):
                ins = mm(ps[:, 4 + half, 0:H], perm, z[:, Z_KR, c0:c1], True, True)
            ins.then_inc(s["krmm"], 1)
            pe.wait_ge(s["vn"], 1)
            pe.wait_ge(s["cqlo"], 1)
            linear("w_uq")
            pe.wait_ge(s["evac"], END["w_uq"])
            pe.wait_ge(s["krr"], 1)
            for j in range(2):
                for half, (c0, c1) in enumerate(HALVES):
                    ins = mm(ps[:, 4 + 2 * j + half, 0:H], perm, qT[:, HEADS + j, c0:c1], True, True)
            ins.then_inc(s["qmm"], 1)
            pe.wait_ge(s["ckvn"], 1)
            pe.wait_ge(s_cache, 32)
            pe.wait_ge(s_ukv, 32)
            KH = KEYS // 2
            for h in range(HEADS):
                if h >= 2:
                    pe.wait_ge(s["kev"], h - 1)
                for half in range(2):
                    for c in range(CK):
                        ins = mm(ps[:, 2 * (h % 2) + half, 0:KH], w_uk[:, c, h * P:(h + 1) * P],
                                 ckvT[:, c, half * KH:(half + 1) * KH], c == 0, c == CK - 1)
                ins.then_inc(s["kmm"], 1)
            pe.wait_ge(s["qr"], 2)
            for i in range(VT):
                n = P if i < VT - 1 else DEC
                if i >= 4:
                    pe.wait_ge(s["vev"], i - 3)
                for c in range(CK):
                    ins = mm(ps[0:n, 4 + i % 4, :], ckvT[:, c, i * P:i * P + n], w_uv[:, c, :], c == 0, c == CK - 1)
                ins.then_inc(s["vmm"], 1)
            pe.wait_ge(s["kev"], HEADS)
            for t, (t0, n) in enumerate(TILES):
                if t >= 4:
                    pe.wait_ge(s["vte"], t - 3)
                for g in range(GH):
                    ins = nc.tensor.transpose(ps[0:n, t % 4, g * P:(g + 1) * P], z[:, Z_GV + g, t0:t0 + n], ident)
                ins.then_inc(s["vtt"], 1)
            pe.wait_ge(s["vev"], VT)
            pe.wait_ge(s_gm, 32)
            pe.wait_ge(s["wsm"], 1)
            for t, (t0, n) in enumerate(TILES):
                pe.wait_ge(s["vte"], t + 1)
                if t >= 4:
                    pe.wait_ge(s["bt"], t - 3)
                for g in range(GH):
                    ins = mm(ps[:, 4 + t % 4, g * P:g * P + n], v_tok[0:n, t, g * P:(g + 1) * P],
                             wsT[0:n, g, 0:n], True, True)
                ins.then_inc(s["gmm"], 1)

            units = [(h, t) for h in range(HEADS) for t in range(NT)]

            def keys(t):
                return (0, (t + 1) * P) if t < SAMPLE else (SEQ, PAST + DEC)

            def key_blocks(t):
                k0, n = keys(t)
                return [(k0 + j * P, min(P, n - j * P)) for j in range((n + P - 1) // P)]

            def scores(i):
                h, t = units[i]
                t0, n = TILES[t]
                k0, nk = keys(t)
                if i >= 2:
                    pe.wait_ge(s["ex"], i - 1)
                r = ROPE * (h % 2)
                mm(ps[0:n, i % 2, 0:nk], qT[:, h, t0:t0 + n], kT[:, h, k0:k0 + nk], True, False)
                mm(ps[0:n, i % 2, 0:nk], qT[r:r + ROPE, HEADS + h // 2, t0:t0 + n],
                   krT[r:r + ROPE, k0:k0 + nk], False, True).then_inc(s["sc"], 1)

            pe.wait_ge(s["vte"], NT)
            pe.wait_ge(s["bt"], NT)
            scores(0)
            for i, (h, t) in enumerate(units):
                if i + 1 < len(units):
                    scores(i + 1)
                t0, n = TILES[t]
                kb = key_blocks(t)
                pe.wait_ge(s["pn"], i + 1)
                if i >= 2:
                    pe.wait_ge(s["pte"], i - 1)
                for j, (k0, nk) in enumerate(kb):
                    ins = nc.tensor.transpose(ps[0:nk, 2 + i % 2, j * P:j * P + n],
                                              prob[0:n, i % 2, j * P:j * P + nk], ident[0:n, 0:n])
                ins.then_inc(s["pt"], 1)
                pe.wait_ge(s["pte"], i + 1)
                if i >= 2:
                    pe.wait_ge(s["pve"], i - 1)
                for j, (k0, nk) in enumerate(kb):
                    ins = mm(ps[:, 4 + i % 2, 0:n], val[0:nk, k0 // P, h * VH:(h + 1) * VH],
                             probT[0:nk, i % 2, j, 0:n], j == 0, j == len(kb) - 1)
                ins.then_inc(s["pv"], 1)
            for t, (t0, n) in enumerate(TILES):
                k0 = t0 if t < SAMPLE else NEW
                if t >= 2:
                    pe.wait_ge(s["ote"], t - 1)
                for c in range(CK):
                    nc.tensor.transpose(ps[0:n, 6 + t % 2, c * P:(c + 1) * P], ckvT[:, c, k0:k0 + n], ident)
                nc.tensor.transpose(ps[0:n, 6 + t % 2, KVL:KVL + ROPE], krT[0:ROPE, k0:k0 + n],
                                    ident[0:ROPE, 0:ROPE]).then_inc(s["otr"], 1)

            pe.wait_ge(s["sqab"], 1)
            column_sums(0, sq, range(HEADS))
            column_sums(2, sq, range(HEADS, KD)).then_inc(s["rowsB"], 1)
            pe.wait_ge(s["rowr"], 2)
            pe.wait_ge(s["mlo"], 1)
            linear("w_o")
            pe.wait_ge(s["evac"], END["w_o"])
            column_sums(4, r_T, range(KD)).then_inc(s["mean1"], 1)
            pe.wait_ge(s["sq1"], 1)
            column_sums(6, sq, range(KD)).then_inc(s["var1"], 1)
            pe.wait_ge(s["h2"], 1)
            pe.wait_ge(s["varr"], 1)
            for k in range(KD):
                ins = nc.tensor.transpose(ps[:, 4 + k // 4, (k % 4) * P:(k % 4 + 1) * P], h2T[:, k, ND:T], ident)
            ins.then_inc(s["h2t"], 1)
            pe.wait_ge(s["h2te"], 1)
            pe.wait_ge(s["h2lo"], 1)
            pe.wait_ge(s_sk, 16)

            def sub_scores(b, u):
                s0 = SPLIT_AT["w_pq"]
                pe.wait_ge(s["evac"], b + s0 + 1)
                wait(pe, s["top1"], b - 1)
                for t, (t0, n) in enumerate(PTILES):
                    ins = mm(ps[0:n, 4 + 2 * (u % 2) + t // 4, (t % 4) * NK:(t % 4 + 1) * NK],
                             q_blk[:, u % 2, t0:t0 + n], skT[:, b, :], True, True)
                ins.then_inc(s["smm"], 1)
            linear("w_pq", sub_scores)

            def transpose_choices(t):
                t0, n = PTILES[t]
                pe.wait_ge(s["chose"], t + 1)
                wait(pe, s["sele"], t)
                for c in range(3):
                    ins = nc.tensor.transpose(ps[:, 4, c * P:c * P + n], chosen[0:n, c, :], ident[0:n, 0:n])
                ins.then_inc(s["selt"], 1)

            pe.wait_ge(s["top1"], HP)
            transpose_choices(0)
            for q in range(NG):
                if q % 2 == 0 and q // 2 + 1 < NPT - 1:
                    transpose_choices(q // 2 + 1)

                def eight(g, k, w):
                    pe.wait_ge(s["onei"], g(1, 1))
                    pe.wait_ge(s["onej"], g(1, 1))
                    for v in range(2):
                        wait(pe, s["gst"], g(2, v - 1))
                        for u in range(4 * v, 4 * v + 4):
                            ins = mm(ps[:, 6 + v, (u % 4) * NK:(u % 4 + 1) * NK], one_j[:, w, u], one_i[:, w, u], True, True)
                        ins.then_inc(s["gmat"], 1)
                each_eight(pe, q, eight)

            def three(out, w, x, i, n):
                (w1, w2), (x1, x2) = w, x
                mm(out, w1, x1, i == 0, False)
                mm(out, w1, x2, False, False)
                return mm(out, w2, x1, False, i == n - 1)

            def pe_step(g, par, half, edge=None):
                if edge != "tail":
                    for j in range(GROUP):
                        pe.wait_ge(s["ulo"], g(GROUP, j + 1))
                        wait(pe, s["ag"], g(GROUP, j - 1))
                        for k in range(KD):
                            c = slice(k * P, (k + 1) * P)
                            ins = three(ps[:, j % 2, 0:ND], (w_hi[:, j % 2, c], w_lo[:, j % 2, c]),
                                        (act_hi[:, k, 0:ND], act_lo[:, k, 0:ND]), k, KD)
                        ins.then_inc(s["amm"], 1)
                if edge == "first":
                    return
                pe.wait_ge(s["galo"], g(GROUP))
                for d in range(KD):
                    if d % 2 == 0:
                        pe.wait_ge(s["vlo"], g(4, d // 2 + 1 - 4))
                    wait(pe, s["fe"], g(KD, d - 3 - KD))
                    c = slice(d * P, (d + 1) * P)
                    for e in range(GROUP):
                        ins = three(ps[:, 2 + d % 4, 0:ND], (v_hi[:, e, c], v_lo[:, e, c]),
                                    (ga_hi[:, 1 - par, e], ga_lo[:, 1 - par, e]), e, GROUP)
                    ins.then_inc(s["fmm"], 1)
            each_step(pe, pe_step)

            pe.wait_ge(s["ag"], NB)
            pe.wait_ge(s["gd"], 2 * SLOTS)
            for k in range(KD):
                ins = nc.tensor.transpose(ps[:, k // 4, (k % 4) * P:(k % 4 + 1) * P], f_tok[:, k * P:(k + 1) * P], ident)
            ins.then_inc(s["ft"], 1)
            pe.wait_ge(s["fe"], KD * NGR)
            for t, (t0, n) in enumerate(TILES):
                if t0 + n > ND:
                    pe.wait_ge(s["r2"], 1)
                if t >= 2:
                    pe.wait_ge(s["y"], t - 1)
                for k in range(KD):
                    ins = nc.tensor.transpose(ps[0:n, 2 + 2 * (t % 2) + k // 4, (k % 4) * P:(k % 4 + 1) * P],
                                              x0T[:, k, t0:t0 + n], ident)
                ins.then_inc(s["yt"], 1)

        @block.scalar
        def _(act):
            step = Chain(act, s_act)

            def f(out, in_, func=ACT.Copy, **kw):
                return nc.scalar.activation(out, in_, func, **kw)

            act.wait_ge(s_vec, 16)
            f(silu_c[:].rearrange("p k c -> p (k c)"), vecs[:, VEC_AT["c"]:VEC_AT["c"] + 16], ACT.Silu).then_inc(s["silu"], 1)
            act.wait_ge(s["var"], 1)
            f(std[:], rstd[:], ACT.Sqrt).then_inc(s["std"], 1)
            for k in range(KD):
                act.wait_ge(s["h32"], k + 1)
                f(act_hi[:, k], tmp[:, k]).then_inc(s["hhi"], 1)

            def linear(name, evacuate):
                kk, s0, g0 = WIDTH[name], SPLIT_AT[name], RING_AT[name]

                def loads(b, u):
                    first = (g0 + u) // RING + 1
                    return 16 * first if isinstance(b, int) and b < RING else (b - u) * (16 // RING) + 16 * first

                def one(b, u):
                    slot = (g0 + u) % RING
                    act.wait_ge(s_w[slot], loads(b, u))
                    wait(act, s["wused"], b + s0 - 1)
                    f(w_hi[:, (s0 + u) % 2, 0:kk * P], w_raw[:, slot, 0:kk * P]).then_inc(s["whi"], 1)
                    if evacuate is not None and not (isinstance(b, int) and b == 0):
                        out(b - 1, u - 1)

                def out(b, u):
                    act.wait_ge(s["wused"], b + s0 + 1)
                    pair = 2 * ((s0 + u) % 2)
                    to = q_blk[:, u % 2, :] if evacuate is q_blk else evacuate[:, b, :]
                    if evacuate is q_blk:
                        wait(act, s["smm"], b - 1)
                    f(to.rearrange("p (s h) -> p s h", s=2), ps[:, pair:pair + 2, 0:H]).then_inc(s["evac"], 1)
                in_steps(act, ORDER[name], RING, one)
                if evacuate is not None:
                    out(ORDER[name] - 1, ORDER[name] - 1)

            linear("w_in", z)
            act.wait_ge(s["evac"], END["w_in"])
            f(tmp[:, 0:QK + CK], z[:, 0:QK + CK], ACT.Square).then_inc(s["sqz"], 1)
            f(z[:, Z_GU:], z[:, Z_GU:], ACT.Gelu_apprx_tanh).then_inc(s["gelu"], 1)
            act.wait_ge(s["cqrow"], 1)
            f(rows[:, 0:2], rows[:, 0:2], ACT.Sqrt).then_inc(s["std"], 1)
            act.wait_ge(s["vvarr"], 1)
            f(rows[:, 3], rows[:, 3], ACT.Sqrt).then_inc(s["std"], 1)
            act.wait_ge(s["cqn"], 1)
            f(act_hi[:, 0:QK], tmp[:, 0:QK]).then_inc(s["cqhi"], 1)
            linear("w_uq", qT)
            for h in range(HEADS):
                act.wait_ge(s["kmm"], h + 1)
                f(kT[:, h, :].rearrange("p (s h) -> p s h", s=2),
                  ps[:, 2 * (h % 2):2 * (h % 2) + 2, 0:KEYS // 2]).then_inc(s["kev"], 1)
            for i in range(VT):
                n = P if i < VT - 1 else DEC
                act.wait_ge(s["vmm"], i + 1)
                f(val[0:n, i, :], ps[0:n, 4 + i % 4, :]).then_inc(s["vev"], 1)
            for t, (t0, n) in enumerate(TILES):
                act.wait_ge(s["vtt"], t + 1)
                f(v_tok[0:n, t, :], ps[0:n, t % 4, :]).then_inc(s["vte"], 1)
            units = [(h, t) for h in range(HEADS) for t in range(NT)]
            for i, (h, t) in enumerate(units):
                t0, n = TILES[t]
                act.wait_ge(s["mx"], i + 1)
                if i >= 2:
                    act.wait_ge(s["pt"], i - 1)
                if t < SAMPLE:
                    for r in range(2):
                        nk = t * P + (r + 1) * CHUNK
                        rr = slice(r * CHUNK, (r + 1) * CHUNK)
                        ins = f(prob[rr, i % 2, 0:nk], ps[rr, i % 2, 0:nk], ACT.Exp, bias=negmax[rr, i:i + 1],
                                scale=SCALE, accum_out=rowsum[rr, i:i + 1])
                else:
                    ins = f(prob[0:n, i % 2, 0:PAST + DEC], ps[0:n, i % 2, 0:PAST + DEC], ACT.Exp,
                            bias=negmax[0:n, i:i + 1], scale=SCALE, accum_out=rowsum[0:n, i:i + 1])
                ins.then_inc(s["ex"], 1)
                act.wait_ge(s["pt"], i + 1)
                if i >= 2:
                    act.wait_ge(s["pv"], i - 1)
                if t < SAMPLE:
                    ins = f(probT[:, i % 2, 0:t + 1, :], ps[:, 2 + i % 2, 0:(t + 1) * P].rearrange("p (j n) -> p j n", n=P))
                else:
                    f(probT[:, i % 2, 0:2, 0:n], ps[:, 2 + i % 2, 0:2 * P].rearrange("p (j n) -> p j n", n=P)[:, :, 0:n])
                    ins = f(probT[0:DEC, i % 2, 2, 0:n], ps[0:DEC, 2 + i % 2, 2 * P:2 * P + n])
                ins.then_inc(s["pte"], 1)
            for t, (t0, n) in enumerate(TILES):
                act.wait_ge(s["otr"], t + 1)
                f(o_tok[0:n, t, :], ps[0:n, 6 + t % 2, 0:KVL + ROPE]).then_inc(s["ote"], 1)
            act.wait_ge(s["pve"], HEADS * NT)
            act.wait_ge(s["bt"], NT)
            act.wait_ge(s["otr"], NT)
            act.wait_ge(s["out"], 16 * (1 + 2 * NT))
            f(sq[:], tmp[:], ACT.Square).then_inc(s["sqab"], 1)
            act.wait_ge(s["rowr"], 1)
            f(rows[:, 0:2], rows[:, 0:2], ACT.Sqrt).then_inc(s["std"], 1)
            act.wait_ge(s["m"], 1)
            f(act_hi[:], tmp[:]).then_inc(s["mhi"], 1)
            linear("w_o", None)
            act.wait_ge(s["rc1"], 1)
            f(sq[:], r_T[:], ACT.Square).then_inc(s["sq1"], 1)
            act.wait_ge(s["varr"], 1)
            f(rows[:, 1], rows[:, 1], ACT.Sqrt).then_inc(s["std"], 1)
            act.wait_ge(s["h2"], 1)
            f(act_hi[:], h2T[:]).then_inc(s["h2hi"], 1)
            act.wait_ge(s["h2t"], 1)
            f(h2_tok[:], ps[:, 4:6, :].rearrange("p b n -> p (b n)")).then_inc(s["h2te"], 1)
            linear("w_pq", q_blk)
            def transposed(t):
                t0, n = PTILES[t]
                act.wait_ge(s["selt"], t + 1)
                f(sel[:, :, t0:t0 + n], ps[:, 4, 0:3 * P].rearrange("p (c n) -> p c n", c=3)[:, :, 0:n]).then_inc(s["sele"], 1)

            def exponentials(t):
                n = PTILES[t][1]
                act.wait_ge(s["fsub"], t + 1)
                f(expo[0:n], diff[0:n], ACT.Exp).then_inc(s["fexp"], 1)

            exponentials(0)
            transposed(0)
            exponentials(1)
            for q in range(NG):
                if q >= 2:
                    act.wait_ge(s_gw[q % 2], 16 * (q // 2))

                def eight(g, k, w):
                    for v in range(2):
                        act.wait_ge(s["gmat"], g(2, v + 1))
                        to = piece[:, q % 2].rearrange("p i (g v t) -> p g v t i", v=2, t=4)[:, k(), v]
                        f(to, ps[:, 6 + v, :].rearrange("p (t i) -> p t i", t=4)).then_inc(s["gst"], 1)
                each_eight(act, q, eight)
                if q % 2 == 0 and q // 2 + 1 < NPT - 1:
                    transposed(q // 2 + 1)
                if q % 2 == 1 and q // 2 + 2 < NPT:
                    exponentials(q // 2 + 2)

            def u_high(g, j):
                slot = j % 2
                act.wait_ge(s_u[slot], g(8 * GROUP, (j - slot) * 8 + 16))
                wait(act, s["amm"], g(GROUP, j - 1))
                f(w_hi[:, slot], w_raw[:, slot]).then_inc(s["uhi"], 1)

            def v_high(g, c):
                act.wait_ge(s_v[c % 2], g(32, c // 2 * 16 + 16))
                wait(act, s["fmm"], g(KD, 2 * c + 2 - KD))
                f(quarter(v_hi, c), raw_quarter(c)).then_inc(s["vhi"], 1)

            def act_step(g, par, half, edge=None):
                for j in range(GROUP):
                    behind = not (edge == "first" and j == 0) and not (edge == "tail" and j > 0)
                    i, pj = (j - 1) % GROUP, par if j else 1 - par
                    if behind:
                        act.wait_ge(s["amm"], g(GROUP, j))
                        wait(act, s["ga"], g(GROUP, j - 2))
                        f(a_g[:, i % 2], ps[:, i % 2, 0:ND], ACT.Gelu_apprx_tanh).then_inc(s["ag"], 1)
                    if edge != "tail" and not (edge == "last" and j == GROUP - 1):
                        u_high(g, j + 1)
                    if edge != "first" and j == 0:
                        v_high(Step(g.at - 1, g.i, g.by), 3)
                    if behind:
                        act.wait_ge(s["ga"], g(GROUP, j))
                        f(ga_hi[:, pj, i], ga32[:, i % 2]).then_inc(s["gahi"], 1)
                if edge != "tail":
                    for c in range(3):
                        v_high(g, c)
                if edge == "turn":
                    act.wait_ge(s["act"], 1)
                    f(act_g[:], act_v[:], ACT.Gelu_apprx_tanh).then_inc(s["wgt"], 1)
            act.wait_ge(s["wused"], N_LIN)
            u_high(Step(0), 0)
            for i in range(2):
                act.wait_ge(s_gw[i], 16 * len(range(i, NG, 2)))
            each_step(act, act_step)
            for t, (t0, n) in enumerate(TILES):
                act.wait_ge(s["var2"], t + 1)
                f(std[0:n, t:t + 1], rstd[0:n, t:t + 1], ACT.Sqrt).then_inc(s["std2"], 1)

        @block.vector
        def _(dve):
            v = nc.vector
            step = Chain(dve, s_dve)
            v.memset(ones[:], 1.0).then_inc(s["ones"], 1)
            step(v.memset(meanvar[:], 1.0))
            for t, (t0, n) in enumerate(TILES):
                dve.wait_ge(s_x[t], 16)
                for j in range(2):
                    step(v.bn_stats(stats[0:n, j], x_tok[0:n, t, j * 512:(j + 1) * 512]))
                step(v.bn_aggr(meanvar[0:n, t], stats[0:n]))
            v.tensor_scalar(rstd[:], meanvar[:, :, 1], EPS, None, ALU.add).then_inc(s["var"], 1)
            dve.wait_ge(s["std"], 1)
            step(v.reciprocal(rstd[:], std[:]))
            for t, (t0, n) in enumerate(TILES):
                v.tensor_scalar(x_tok[0:n, t], x_tok[0:n, t], meanvar[0:n, t, 0:1], rstd[0:n, t:t + 1],
                                ALU.subtract, ALU.mult).then_inc(s["xn"], 1)
            dve.wait_ge(s_vec, 16)
            for k in range(KD):
                dve.wait_ge(s["xT"], k + 1)
                b0 = 1 + 2 * (k % 3)
                v.tensor_scalar(x0T[:, k, 0:SEQ], ps[:, b0, :], vec("ln_in_g", k), vec("ln_in_b", k), ALU.mult, ALU.add)
                v.tensor_scalar(x0T[:, k, SEQ:T], ps[:, b0 + 1, 0:DEC], vec("ln_in_g", k), vec("ln_in_b", k),
                                ALU.mult, ALU.add).then_inc(s["x0e"], 1)
            dve.wait_ge(s["adaused"], ORDER["ada"])
            b_ada = vecs[:, VEC_AT["b_ada"]:VEC_AT["b_ada"] + 48].unsqueeze(2).to_broadcast([P, 48, 2])
            step(v.tensor_tensor(mod[:], ps[:, 0, 0:96].rearrange("p (f c) -> p f c", c=2), b_ada, ALU.add))
            step(v.tensor_scalar(mod[:, 8:24], mod[:, 8:24], 1.0, None, ALU.add))
            v.tensor_scalar(mod[:, 32:48], mod[:, 32:48], 1.0, None, ALU.add).then_inc(s["mod"], 1)
            dve.wait_ge(s["mod"], 1)
            SH1, SC1, GT1, SH2, SC2, GT2 = (KD * i for i in range(6))
            STREAMS = ((0, SEQ, 0), (SEQ, T, 1))

            def modulate(out, src, k, scale, shift):
                for c0, c1, c in STREAMS:
                    ins = v.tensor_scalar(out[:, k, c0:c1], src[:, k, c0:c1], mod[:, scale + k, c:c + 1],
                                          mod[:, shift + k, c:c + 1], ALU.mult, ALU.add)
                return ins

            dve.wait_ge(s["x0e"], KD)
            for k in range(KD):
                modulate(tmp, x0T, k, SC1, SH1).then_inc(s["h32"], 1)
            for k in range(KD):
                dve.wait_ge(s["hhi"], k + 1)
                v.tensor_tensor(act_lo[:, k], tmp[:, k], act_hi[:, k].bitcast(F32), ALU.subtract).then_inc(s["hlo"], 1)

            def linear(name, extra=None):
                kk, s0, g0 = WIDTH[name], SPLIT_AT[name], RING_AT[name]

                def one(b, u):
                    slot, g = (g0 + u) % RING, (s0 + u) % 2
                    dve.wait_ge(s["whi"], b + s0 + 1)
                    v.tensor_tensor(w_lo[:, g, 0:kk * P], w_raw[:, slot, 0:kk * P],
                                    w_hi[:, g, 0:kk * P].bitcast(F32), ALU.subtract).then_inc(s["wlo"], 1)
                    if extra is not None and not (isinstance(b, int) and b == 0):
                        extra(b - 1, u - 1)
                in_steps(dve, ORDER[name], RING, one)
                if extra is not None:
                    extra(ORDER[name] - 1, ORDER[name] - 1)

            def pair(bank):
                return ps[:, bank:bank + 2, 0:H]

            def row(i):
                return rows[:, i].rearrange("p (s h) -> p s h", s=2)

            linear("w_in")
            dve.wait_ge(s["rowsA"], 1)
            v.tensor_scalar(row(0), pair(4), 1.0 / QL, EPS, ALU.mult, ALU.add)
            v.tensor_scalar(row(1), pair(6), 1.0 / KVL, EPS, ALU.mult, ALU.add).then_inc(s["cqrow"], 1)
            dve.wait_ge(s["vmean"], 1)
            step(v.tensor_scalar(row(2), pair(0), 1.0 / (GH * P), None, ALU.mult))
            for g in range(GH):
                step(v.tensor_tensor(z[:, Z_GV + g], z[:, Z_GV + g], rows[:, 2], ALU.subtract))
                ins = v.tensor_tensor(tmp[:, g], z[:, Z_GV + g], z[:, Z_GV + g], ALU.mult)
                if g < GH - 1:
                    step(ins)
            ins.then_inc(s["vc2"], 1)
            dve.wait_ge(s["vvar"], 1)
            v.tensor_scalar(row(3), pair(2), 1.0 / (GH * P), EPS, ALU.mult, ALU.add).then_inc(s["vvarr"], 1)
            dve.wait_ge(s["std"], 2)
            v.reciprocal(rows[:, 0:2], rows[:, 0:2]).then_inc(s["cqrow"], 1)
            dve.wait_ge(s["cqrow"], 2)
            for k in range(QK):
                ins = v.scalar_tensor_tensor(tmp[:, k], z[:, k], vec("g_q", k), rows[:, 0], ALU.mult, ALU.mult)
            ins.then_inc(s["cqn"], 1)
            for c in range(CK):
                for c0, c1, o in ((0, SEQ, 0), (SEQ, T, PAST)):
                    ins = v.scalar_tensor_tensor(ckvT[:, c, c0 + o:c1 + o], z[:, Z_CKV + c, c0:c1], vec("g_kv", c),
                                                 rows[:, 1, c0:c1], ALU.mult, ALU.mult)
            ins.then_inc(s["ckvn"], 1)
            dve.wait_ge(s["cqhi"], 1)
            v.tensor_tensor(act_lo[:, 0:QK], tmp[:, 0:QK], act_hi[:, 0:QK].bitcast(F32), ALU.subtract).then_inc(s["cqlo"], 1)
            dve.wait_ge(s["std"], 3)
            step(v.reciprocal(rows[:, 3], rows[:, 3]))
            for g in range(GH):
                ins = v.scalar_tensor_tensor(z[:, Z_GV + g], z[:, Z_GV + g], vec("g_v", g), rows[:, 3], ALU.mult, ALU.mult)
                step(ins)
                ins = v.tensor_scalar(z[:, Z_GV + g], z[:, Z_GV + g], vec("b_v", g), None, ALU.add)
                if g < GH - 1:
                    step(ins)
            ins.then_inc(s["vn"], 1)
            dve.wait_ge(s["krmm"], 1)
            dve.wait_ge(s["cqlo"], 1)
            kr_rot = rows[:, 0]
            dve.wait_ge(s["vn"], 1)
            step(v.tensor_tensor(row(0), pair(4), sinT.rearrange("p (s h) -> p s h", s=2), ALU.mult))
            step(v.tensor_tensor(rows[:, 1], z[:, Z_KR], cosT, ALU.mult))
            step(v.tensor_tensor(krT[:, 0:SEQ], rows[:, 0, 0:SEQ], rows[:, 1, 0:SEQ], ALU.add))
            v.tensor_tensor(krT[:, NEW:], rows[:, 0, SEQ:T], rows[:, 1, SEQ:T], ALU.add).then_inc(s["krr"], 1)
            dve.wait_ge(s["krr"], 1)
            linear("w_uq")
            dve.wait_ge(s["qmm"], 1)
            for j in range(2):
                step(v.tensor_tensor(row(2 + j), pair(4 + 2 * j), sinT.rearrange("p (s h) -> p s h", s=2), ALU.mult))
                step(v.tensor_tensor(rows[:, j], qT[:, HEADS + j], cosT, ALU.mult))
                v.tensor_tensor(qT[:, HEADS + j], rows[:, j], rows[:, 2 + j], ALU.add).then_inc(s["qr"], 1)
            dve.wait_ge(s_gm, 32)
            v.memset(wsT[CHUNK:P, :, 0:CHUNK], 0.0).then_inc(s["wsm"], 1)
            for t, (t0, n) in enumerate(TILES):
                dve.wait_ge(s["gmm"], t + 1)
                step(v.tensor_tensor(tmp[:, HEADS:KD, t0:t0 + n],
                                     ps[:, 4 + t % 4, :].rearrange("p (g n) -> p g n", n=P)[:, :, 0:n], bs[:, :, 0:n], ALU.add))
                v.tensor_tensor(tmp[:, HEADS:KD, t0:t0 + n], tmp[:, HEADS:KD, t0:t0 + n],
                                z[:, Z_GU:Z_GU + GH, t0:t0 + n], ALU.mult).then_inc(s["bt"], 1)
            units = [(h, t) for h in range(HEADS) for t in range(NT)]

            def head_out(i):
                h, t = units[i]
                t0, n = TILES[t]
                dve.wait_ge(s["pv"], i + 1)
                v.tensor_copy(tmp[:, h, t0:t0 + n], ps[:, 4 + i % 2, 0:n]).then_inc(s["pve"], 1)

            for i, (h, t) in enumerate(units):
                t0, n = TILES[t]
                dve.wait_ge(s["sc"], i + 1)
                if t < SAMPLE:
                    for r in range(2):
                        rr = slice(r * CHUNK, (r + 1) * CHUNK)
                        ins = v.tensor_reduce(rowmax[rr, i:i + 1], ps[rr, i % 2, 0:t * P + (r + 1) * CHUNK], AX.X, ALU.max)
                        step(ins)
                else:
                    step(v.tensor_reduce(rowmax[0:n, i:i + 1], ps[0:n, i % 2, 0:PAST + DEC], AX.X, ALU.max))
                v.tensor_scalar(negmax[0:n, i:i + 1], rowmax[0:n, i:i + 1], -SCALE, None, ALU.mult).then_inc(s["mx"], 1)
                dve.wait_ge(s["ex"], i + 1)
                step(v.reciprocal(rinv[0:n, i:i + 1], rowsum[0:n, i:i + 1]))
                if t < SAMPLE:
                    step(v.memset(prob[0:CHUNK, i % 2, t * P + CHUNK:(t + 1) * P], 0.0))
                nk = (t + 1) * P if t < SAMPLE else PAST + DEC
                v.tensor_scalar(prob[0:n, i % 2, 0:nk], prob[0:n, i % 2, 0:nk], rinv[0:n, i:i + 1], None,
                                ALU.mult).then_inc(s["pn"], 1)
                if i >= 1:
                    head_out(i - 1)
            head_out(len(units) - 1)
            dve.wait_ge(s["rowsB"], 1)
            for j in range(2):
                ins = v.tensor_scalar(row(j), pair(2 * j), 1.0 / (HEADS * VH), EPS, ALU.mult, ALU.add)
                step(ins) if j == 0 else ins.then_inc(s["rowr"], 1)
            dve.wait_ge(s["std"], 4)
            v.reciprocal(rows[:, 0:2], rows[:, 0:2]).then_inc(s["rowr"], 1)
            dve.wait_ge(s["rowr"], 2)
            for k in range(KD):
                g, j = ("g_out_a", k) if k < HEADS else ("g_out_b", k - HEADS)
                ins = v.scalar_tensor_tensor(tmp[:, k], tmp[:, k], vec(g, j), rows[:, k // HEADS], ALU.mult, ALU.mult)
                if k < KD - 1:
                    step(ins)
            ins.then_inc(s["m"], 1)
            v.tensor_scalar(x0T[:], x0T[:], ALPHA, None, ALU.mult).then_inc(s["ax"], 1)
            dve.wait_ge(s["mhi"], 1)
            v.tensor_tensor(act_lo[:], tmp[:], act_hi[:].bitcast(F32), ALU.subtract).then_inc(s["mlo"], 1)
            dve.wait_ge(s["ax"], 1)

            def residual(b, u):
                s0 = SPLIT_AT["w_o"]
                dve.wait_ge(s["wused"], b + s0 + 1)
                bank = 2 * ((s0 + u) % 2)
                for c0, c1, c in ((0, H, 0), (H, SEQ, 0), (SEQ, T, 1)):
                    half = c0 // H
                    ins = v.scalar_tensor_tensor(r_T[:, b, c0:c1], ps[:, bank + half, c0 - half * H:c1 - half * H],
                                                 mod[:, GT1 + b, c:c + 1], x0T[:, b, c0:c1], ALU.mult, ALU.add)
                ins.then_inc(s["evac"], 1)
            linear("w_o", residual)
            dve.wait_ge(s["evac"], END["w_o"])
            dve.wait_ge(s["mean1"], 1)
            step(v.tensor_scalar(row(0), pair(4), 1.0 / D, None, ALU.mult))
            row0 = rows[:, 0].unsqueeze(1).to_broadcast([P, KD, T])
            v.tensor_tensor(r_T[:], r_T[:], row0, ALU.subtract).then_inc(s["rc1"], 1)
            dve.wait_ge(s["var1"], 1)
            v.tensor_scalar(row(1), pair(6), 1.0 / D, EPS, ALU.mult, ALU.add).then_inc(s["varr"], 1)
            dve.wait_ge(s["std"], 5)
            step(v.reciprocal(rows[:, 1], rows[:, 1]))
            for k in range(KD):
                step(v.scalar_tensor_tensor(x0T[:, k], r_T[:, k], vec("ln1_g", k), rows[:, 1], ALU.mult, ALU.mult))
                step(v.tensor_scalar(x0T[:, k], x0T[:, k], vec("ln1_b", k), None, ALU.add))
            for k in range(KD):
                ins = modulate(h2T, x0T, k, SC2, SH2)
            ins.then_inc(s["h2"], 1)
            dve.wait_ge(s["h2hi"], 1)
            v.tensor_tensor(act_lo[:], h2T[:], act_hi[:].bitcast(F32), ALU.subtract).then_inc(s["h2lo"], 1)
            step(v.tensor_scalar(x0T[:], x0T[:], ALPHA, None, ALU.mult))

            def top16(vals, idx, src, scr):
                step(v.max(vals[:, 0:8], src))
                v.max_index(idx[:, 0:8], vals[:, 0:8], src)
                step(v.match_replace(scr, vals[:, 0:8], src, -3.0e38))
                step(v.max(vals[:, 8:16], scr))
                v.max_index(idx[:, 8:16], vals[:, 8:16], scr)

            def sub_tops(b):
                dve.wait_ge(s["smm"], b + 1)
                par = b % 2
                for t, (t0, n) in enumerate(PTILES):
                    top16(found[0:n, par, t], found_i[0:n, par, t],
                          ps[0:n, 4 + 2 * par + t // 4, (t % 4) * NK:(t % 4 + 1) * NK], scratch[0:n])
                step(v.tensor_copy(top[:, :, b, :], found[:, par]))
                v.tensor_copy(top_f[:, :, b, :], found_i[:, par]).then_inc(s["top1"], 1)

            step(v.memset(found[:], 0.0))
            step(v.memset(found_i[:].bitcast(F32), 0.0))
            for b in range(HP):
                sub_tops(b)
            dve.wait_ge(s["top1"], HP)

            starts = consts[:, C_START:C_START + TOPK]
            start_steps = consts[:, C_START + TOPK:C_START + 2 * TOPK]

            def choose(t):
                t0, n = PTILES[t]
                lists = top[0:n, t].rearrange("p (h q) a -> p h q a", q=2)
                ids = top_f[0:n, t].rearrange("p (h q) a -> p h q a", q=2)
                s1, s2 = lists[:, :, 0], lists[:, :, 1]
                for a0 in range(5):
                    out = cand[0:n, :, START[a0]:START[a0] + ROW[a0]]
                    v.tensor_tensor(out, s2[:, :, 0:ROW[a0]], s1[:, :, a0:a0 + 1].to_broadcast([n, PH, ROW[a0]]), ALU.add)
                for i in range(2):
                    v.tensor_tensor(cand[0:n, :, START[5] + i:START[8]:2], s1[:, :, 5:8],
                                    s2[:, :, i:i + 1].to_broadcast([n, PH, 3]), ALU.add)
                step(v.tensor_tensor(cand[0:n, :, START[8]:NCAND], s1[:, :, 8:16], s2[:, :, 0:1].to_broadcast([n, PH, 8]), ALU.add))
                for h in range(PH):
                    top16(fin[0:n, h], pos[0:n, h], cand[0:n, h], cand2[0:n, 0:NCAND])
                v.tensor_tensor(diff[0:n].rearrange("p (h k) -> p h k", h=PH), fin[0:n],
                                fin[0:n, :, 0:1].to_broadcast([n, PH, TOPK]), ALU.subtract).then_inc(s["fsub"], 1)
                steps = step_i[0:n]
                step(v.tensor_copy(steps[:, :, 0:1], ids[:, :, 0, 0:1]))
                step(v.tensor_tensor(steps[:, :, 1:], ids[:, :, 0, 1:], ids[:, :, 0, 0:TOPK - 1], ALU.subtract))
                step(v.scalar_tensor_tensor(steps, steps, 64.0, start_steps[0:n].unsqueeze(1).to_broadcast([n, PH, TOPK]),
                                            ALU.mult, ALU.add))
                step(v.tensor_copy(pos_f[0:n], pos[0:n].rearrange("p h k -> p (h k)")))
                h4 = hit[0:n].rearrange("p (h k) a -> p h k a", h=PH)
                step(v.tensor_tensor(hit[0:n], pos_f[0:n].unsqueeze(2).to_broadcast([n, SLOTS, TOPK]),
                                     starts[0:n].unsqueeze(1).to_broadcast([n, SLOTS, TOPK]), ALU.is_ge))
                step(v.tensor_tensor(h4, h4, steps.unsqueeze(2).to_broadcast([n, PH, TOPK, TOPK]), ALU.mult))
                step(v.tensor_reduce(num_f[0:n], hit[0:n], AX.X, ALU.add))
                step(v.tensor_copy(num_u[0:n, 0], num_f[0:n]))
                step(v.tensor_scalar(num_u[0:n, 1], num_u[0:n, 0], 63, None, ALU.bitwise_and))
                step(v.tensor_scalar(num_u[0:n, 0], num_u[0:n, 0], 6, None, ALU.logical_shift_right))
                if t >= 1:
                    dve.wait_ge(s["selt"], t)
                step(v.tensor_copy(chosen[0:n, 0], num_u[0:n, 0]))
                step(v.tensor_copy(num_f[0:n], num_u[0:n, 1]))
                step(v.tensor_tensor(num_f[0:n], pos_f[0:n], num_f[0:n], ALU.subtract))
                step(v.tensor_tensor(hit[0:n], num_f[0:n].unsqueeze(2).to_broadcast([n, SLOTS, TOPK]),
                                     iota[0:n, 0:TOPK].unsqueeze(1).to_broadcast([n, SLOTS, TOPK]), ALU.is_equal))
                step(v.tensor_tensor(h4, h4, ids[:, :, 1].unsqueeze(2).to_broadcast([n, PH, TOPK, TOPK]), ALU.mult))
                step(v.tensor_reduce(chosen[0:n, 1], hit[0:n], AX.X, ALU.add))
                dve.wait_ge(s["fexp"], t + 1)
                e3 = expo[0:n].rearrange("p (h k) -> p h k", h=PH)
                step(v.tensor_reduce(ssum[0:n, 0:PH], e3, AX.X, ALU.add))
                step(v.reciprocal(ssum[0:n, 0:PH], ssum[0:n, 0:PH]))
                if t == NPT - 1:
                    step(v.scalar_tensor_tensor(pos_f[0:n], chosen[0:n, 0], float(NK), chosen[0:n, 1], ALU.mult, ALU.add))
                    v.tensor_copy(expert[:], pos_f[:])
                g3 = (gate_s[:] if t == NPT - 1 else chosen[0:n, 2]).rearrange("p (h k) -> p h k", h=PH)
                v.tensor_tensor(g3, e3, ssum[0:n, 0:PH].unsqueeze(2).to_broadcast([n, PH, TOPK]), ALU.mult).then_inc(s["chose"], 1)
                dve.wait_ge(s["chose"], t + 1)

            choose(0)
            choose(1)
            for q in range(NG):
                dve.wait_ge(s["sele"], q // 2 + 1)

                def rows_of(g, k, w):
                    wait(dve, s["gmat"], g(2, -2))
                    for c, rows8, done in ((1, one_j, "eqj"), (0, one_i, "onei")):
                        number = sel[:, c].rearrange("p (g u) -> p g u", u=8)[:, g()]
                        v.tensor_tensor(rows8[:, w], iota.unsqueeze(1).to_broadcast([P, 8, NK]),
                                        number.unsqueeze(2).to_broadcast([P, 8, NK]), ALU.is_equal).then_inc(s[done], 1)
                each_eight(dve, q, rows_of)
                if q % 2 == 1 and q // 2 + 2 < NPT:
                    choose(q // 2 + 2)
            dve.wait_ge(s["gmat"], ND // 4)

            def u_low(g, j):
                slot = j % 2
                dve.wait_ge(s["uhi"], g(GROUP, j + 1))
                v.tensor_tensor(w_lo[:, slot], w_raw[:, slot], w_hi[:, slot].bitcast(F32), ALU.subtract).then_inc(s["ulo"], 1)

            def v_low(g, c):
                dve.wait_ge(s["vhi"], g(4, c + 1))
                v.tensor_tensor(quarter(v_lo, c), raw_quarter(c), quarter(v_hi, c).bitcast(F32),
                                ALU.subtract).then_inc(s["vlo"], 1)

            def indices(group, par):
                v.tensor_copy(idx8[:, par], expert[:].rearrange("p (g u) -> p g u", u=PER)[:, group]).then_inc(s["idx"], 1)

            def slot_op(g, par, half, u):
                dve.wait_ge(s_g[u % GB], g(PER // GB * 16, u // GB * 16 + 16))
                if half == 0:
                    v.tensor_tensor_reduce(gath[:, u % GB], gath[:, u % GB], h2_tok[:], 1.0, 0.0, ALU.mult, ALU.add,
                                           act8[:, par, u:u + 1]).then_inc(s["gd"], 1)
                else:
                    dve.wait_ge(s["gd"], g(PER, u))
                    w = act_g[:].rearrange("p (g u) -> p g u", u=PER)[:, g(1, -(NGR // 2)), u:u + 1]
                    v.scalar_tensor_tensor(f_tok[:], gath[:, u % GB], w, f_tok[:], ALU.mult, ALU.add).then_inc(s["gd"], 1)

            def dve_step(g, par, half, edge=None):
                for j in range(GROUP):
                    behind = not (edge == "first" and j == 0) and not (edge == "tail" and j > 0)
                    i, pj = (j - 1) % GROUP, par if j else 1 - par
                    if edge != "tail" and not (edge == "last" and j == GROUP - 1):
                        u_low(g, j + 1)
                    if behind:
                        dve.wait_ge(s["ag"], g(GROUP, j))
                        dve.wait_ge(s_gi[i // 2], g(16, 16 if j else 0))
                        wait(dve, s["gahi"], g(GROUP, j - 2))
                        wait(dve, s["galo"], g(GROUP, j - 2))
                        v.tensor_tensor(ga32[:, i % 2].rearrange("p (s t) -> p s t", s=NG),
                                        a_g[:, i % 2].rearrange("p (s t) -> p s t", s=NG),
                                        g_in[:, i // 2, :, i % 2, :], ALU.mult).then_inc(s["ga"], 1)
                    if edge != "first" and j == 0:
                        v_low(Step(g.at - 1, g.i, g.by), 3)
                    if behind:
                        dve.wait_ge(s["gahi"], g(GROUP, j))
                        v.tensor_tensor(ga_lo[:, pj, i], ga32[:, i % 2], ga_hi[:, pj, i].bitcast(F32), ALU.subtract).then_inc(s["galo"], 1)
                    if j == 1 and edge not in ("last", "tail"):
                        indices(0 if edge == "turn" else g(1, 1) if half == 0 else g(1, 1 - NGR // 2), 1 - par)
                    if edge != "tail" and j % 2:
                        slot_op(g, par, half, j // 2)
                for d in range(KD):
                    if edge != "first":
                        dve.wait_ge(s["fmm"], g(KD, d + 1 - KD))
                        wait(dve, s["fe"], g(KD, d + 1 - 2 * KD))
                        v.scalar_tensor_tensor(x0T[:, d, 0:ND], ps[:, 2 + d % 4, 0:ND], mod[:, GT2 + d, 0:1],
                                               x0T[:, d, 0:ND], ALU.mult, ALU.add).then_inc(s["fe"], 1)
                    if edge != "tail" and d % 2 == 0 and d >= 2:
                        v_low(g, d // 2 - 1)
                    if edge != "tail" and d in (0, 1, 3, 4, 5, 7):
                        slot_op(g, par, half, 2 + (0, 1, 3, 4, 5, 7).index(d))
                if edge == "tail":
                    return
                if half == 0:
                    dve.wait_ge(s["gd"], g(PER, PER))
                    v.tensor_copy(act_v[:].rearrange("p (g u) -> p g u", u=PER)[:, g()], act8[:, par]).then_inc(s["dots"], 1)
                if edge == "turn":
                    dve.wait_ge(s["dots"], NGR // 2)
                    v.memset(f_tok[:], 0.0).then_inc(s["act"], 1)
                    dve.wait_ge(s["wgt"], 1)
                    v.tensor_tensor(act_g[:], act_g[:], gate_s[:], ALU.mult).then_inc(s["act"], 1)
                    dve.wait_ge(s["act"], 2)

            u_low(Step(0), 0)
            indices(0, 0)
            each_step(dve, dve_step)
            dve.wait_ge(s["ft"], 1)
            for k in range(KD):
                for c0, c1, c in ((ND, SEQ, 0), (SEQ, T, 1)):
                    ins = v.scalar_tensor_tensor(x0T[:, k, c0:c1], ps[:, k // 4, (k % 4) * P + c0 - ND:(k % 4) * P + c1 - ND],
                                                 mod[:, GT2 + k, c:c + 1], x0T[:, k, c0:c1], ALU.mult, ALU.add)
            ins.then_inc(s["r2"], 1)
            dve.wait_ge(s_gb, 32)
            for t, (t0, n) in enumerate(TILES):
                dve.wait_ge(s["yt"], t + 1)
                if t >= 2:
                    dve.wait_ge(s_y[t % 2], 16 * (t // 2))
                src = ps[0:n, 2 + 2 * (t % 2):4 + 2 * (t % 2), :]
                for j in range(2):
                    step(v.bn_stats(stats[0:n, j], src[:, j]))
                step(v.bn_aggr(meanvar[0:n, t], stats[0:n]))
                v.tensor_scalar(rstd[0:n, t:t + 1], meanvar[0:n, t, 1:2], EPS, None, ALU.add).then_inc(s["var2"], 1)
                dve.wait_ge(s["std2"], t + 1)
                step(v.reciprocal(rstd[0:n, t:t + 1], std[0:n, t:t + 1]))
                step(v.tensor_scalar(y_tok[0:n, t % 2], src.rearrange("p b n -> p (b n)"), meanvar[0:n, t, 0:1],
                                     rstd[0:n, t:t + 1], ALU.subtract, ALU.mult))
                step(v.tensor_tensor(y_tok[0:n, t % 2], y_tok[0:n, t % 2], gb2[0:n, 0], ALU.mult))
                v.tensor_tensor(y_tok[0:n, t % 2], y_tok[0:n, t % 2], gb2[0:n, 1], ALU.add).then_inc(s["y"], 1)


_OUTS = dict(y_prompt=(1, SEQ, D), y_sample=(1, DEC, D), ckv_p=(1, 1, SEQ, KVL), kr_p=(1, 1, SEQ, ROPE),
             ckv_s=(1, 1, DEC, KVL), kr_s=(1, 1, DEC, ROPE), new_v=(1, 1, DEC, GH * P))


def layout(x):
    import numpy as np

    def blocked(w):
        n = w.shape[1] // P
        return w.reshape(w.shape[0] // P, P, n, P).transpose(2, 1, 0, 3).reshape(n, P, w.shape[0])

    def columns(v):
        return v.reshape(-1, P).T

    x = {k: np.asarray(v) for k, v in x.items()}
    w_in = x["w_in"][0]
    kr = w_in[:, QL + KVL:QL + KVL + ROPE]
    w_in = np.concatenate([w_in[:, :QL + KVL], kr, kr, w_in[:, QL + KVL + ROPE:]], axis=1)
    uq = x["w_uq"][0].reshape(QL, HEADS, NOPE + ROPE)
    w_uq = np.concatenate([uq[:, :, :NOPE].reshape(QL, -1), uq[:, :, NOPE:].reshape(QL, -1)], axis=1)
    c = np.stack([x["c_prompt"][0], x["c_sample"][0]])
    vecs = {k: columns(x[k].reshape(-1)) for k in VEC_LEN if k != "c"}
    vecs["c"] = c.reshape(2, KD, P).transpose(2, 1, 0).reshape(P, 2 * KD)
    krc = x["cache_krope"][0, 0].T
    half = ROPE // 2
    freq = np.power(np.float32(10000.0), -np.arange(half, dtype=np.float32) * np.float32(2.0 / ROPE)).astype(np.float32)
    positions = np.concatenate([np.arange(SEQ), PAST + np.arange(DEC)]).astype(np.float32)
    angle = positions[:, None] * freq[None, :]
    cos = np.tile(np.cos(angle).T, (4, 1))
    sin = np.tile(np.concatenate([-np.sin(angle).T, np.sin(angle).T]), (2, 1))
    perm = np.zeros((P, P))
    perm[np.arange(P) ^ half, np.arange(P)] = 1.0
    consts = np.concatenate([np.eye(P), perm, cos, sin, np.tile(np.arange(NK), (P, 1)),
                             np.tile(START, (P, 1)), np.tile(np.diff([0] + START), (P, 1))], axis=1).astype(np.float32)
    out = dict(
        x_prompt=x["x_prompt"][0], x_sample=x["x_sample"][0], consts=consts,
        vecs=np.concatenate([vecs[k] for k in VEC_LEN], axis=1),
        cacheT=x["cache_ckv"][0, 0].T.reshape(CK, P, PAST).transpose(1, 0, 2),
        krcacheT=np.concatenate([krc, krc], axis=0),
        ada=blocked(x["w_ada"][0]), w_in=blocked(w_in), w_uq=blocked(w_uq), w_o=blocked(x["w_o"][0]), w_pq=blocked(x["w_pq"][0]),
        w_uk=x["w_uk"][0].reshape(CK, P, -1).transpose(1, 0, 2), w_uv=x["w_uv"][0].reshape(CK, P, -1).transpose(1, 0, 2),
        wsT=x["w_s"][0].transpose(2, 0, 1), b_s=x["b_s"][0].reshape(-1),
        skT=x["sub_keys"][0].transpose(3, 0, 1, 2).reshape(P, HP, NK),
        peer_uT=x["peer_u"][0].reshape(NB, P, KD, P).transpose(0, 3, 2, 1).reshape(NB, P, D),
        peer_vq=x["peer_v"][0].reshape(NGR, GROUP, P, 4, D // 4).transpose(0, 3, 2, 1, 4).reshape(NGR, 4, P, D),
        peer_u=x["peer_u"][0], peer_v=x["peer_v"][0], ln2_g=x["ln2_g"][0], ln2_b=x["ln2_b"][0])
    return {k: np.ascontiguousarray(v) for k, v in out.items()}


def kernel(**inputs):
    import concourse.bacc as bacc
    from concourse.bass_utils import run_bass_kernel_spmd

    nc = bacc.Bacc("TRN2", target_bir_lowering=False, num_devices=1)
    arrays = layout(inputs)
    a = {k: nc.dram_tensor(k, v.shape, F32, kind="ExternalInput").ap() for k, v in arrays.items()}
    for k, shape in _OUTS.items():
        a[k] = nc.dram_tensor(k, shape[-2:], F32, kind="ExternalOutput").ap()
    build(nc, a)
    r = run_bass_kernel_spmd(nc, [arrays], core_ids=[0])
    return tuple(r.results[0][k].reshape(shape) for k, shape in _OUTS.items())
```

```python
from contextlib import ExitStack

import concourse.bass as bass
from concourse import mybir

F32 = mybir.dt.float32
F32R = mybir.dt.float32r
U32 = mybir.dt.uint32
ALU = mybir.AluOpType
ACT = mybir.ActivationFunctionType
AX = mybir.AxisListType

P = 128
D = 1024
KD = D // P
SEQ, DEC, PAST = 512, 64, 256
T = SEQ + DEC
H = T // 2
HALVES = ((0, H), (H, T))
TILES = [(t * P, P) for t in range(SEQ // P)] + [(SEQ, DEC)]
NT = len(TILES)
SAMPLE = NT - 1
CHUNK = 64
HEADS, NOPE, ROPE, VH = 4, 128, 64, 128
QL, KVL = 768, 256
QK, CK = QL // P, KVL // P
GH = 4
KEYS = SEQ + PAST + DEC
NEW = SEQ + PAST
VT = 7
PH, NK, TOPK = 8, 128, 16
HP = 2 * PH
SLOTS = PH * TOPK
EPS = 1e-6
ALPHA = 2.0 ** 0.25
SCALE = (NOPE + ROPE) ** -0.5
Z_CKV, Z_KR, Z_GU, Z_GV, Z_N = QK, QK + CK, QK + CK + 1, QK + CK + 1 + GH, QK + CK + 1 + 2 * GH
VEC_LEN = dict(ln_in_g=8, ln_in_b=8, b_ada=48, g_q=QK, g_kv=CK, g_v=GH, b_v=GH, g_out_a=HEADS,
               g_out_b=GH, ln1_g=8, ln1_b=8, c=16)
VEC_AT = {}
for _name, _n in VEC_LEN.items():
    VEC_AT[_name] = sum(VEC_LEN[k] for k in VEC_AT)
NVEC = sum(VEC_LEN.values())
C_ID, C_PERM, C_COS, C_SIN, C_IOTA = 0, P, 2 * P, 2 * P + T, 2 * P + 2 * T
C_START = C_IOTA + P
NCONST = C_START + 2 * TOPK
ROW = [TOPK // (a + 1) for a in range(TOPK)]
START = [sum(ROW[:a]) for a in range(TOPK)]
NCAND = sum(ROW)
ND = T - P
PTILES = [(t * P, min(P, ND - t * P)) for t in range((ND + P - 1) // P)] + [(ND, P)]
NPT = len(PTILES)
GS = 64
NG = ND // GS
GROUP = 4
NB = NK
NGR = NB // GROUP
PER = 2 * SLOTS // NGR
EARLY = GROUP - 1
EARLY_AT = (7, 7, 0, 5, 0, 6, 0, 0, 7)
assert sum(EARLY_AT) == NGR
CHOOSE_AFTER = {1: 2, 3: 3, NG - 1: NPT - 1}
GB = 4
RING = 4
ORDER = dict(ada=2 * KD, w_in=Z_KR, w_in2=Z_N - Z_KR, w_uq=6, ada2=4 * KD, w_o=KD, w_pq=HP)
RING_AT, SPLIT_AT = {}, {}
_g = 0
for _name, _n in ORDER.items():
    RING_AT[_name] = _g
    SPLIT_AT[_name] = sum(ORDER[k] for k in SPLIT_AT if not k.startswith("ada"))
    _g += _n
FIRST = dict(ada=0, ada2=ORDER["ada"], w_in=0, w_in2=Z_KR)
WIDTH = dict(ada=KD, ada2=KD, w_in=KD, w_in2=KD, w_uq=QK, w_o=KD, w_pq=KD)


def wait(eng, sem, value):
    if not (isinstance(value, int) and value <= 0):
        eng.wait_ge(sem, value)


def in_steps(eng, n, unroll, body):
    full = n // unroll
    for b in range(min(n, unroll)):
        body(b, b)
    if full > 2:
        with eng.Fori(1, full) as i:
            for u in range(unroll):
                body(i * unroll + u, u)
    elif full == 2:
        for u in range(unroll):
            body(unroll + u, u)
    for b in range(max(full, 1) * unroll, n):
        body(b, b - full * unroll)


class Step:

    def __init__(self, at, i=None, by=0):
        self.at, self.i, self.by = at, i, by

    def __call__(self, times=1, plus=0):
        at = self.at * times + plus
        if self.i is None:
            return at
        assert at >= 0
        return self.i * (self.by * times) + at if at else self.i * (self.by * times)

    def plus(self, n):
        return Step(self.at + n, self.i, self.by)


class Chain:

    def __init__(self, eng, sem):
        self.eng, self.sem, self.n = eng, sem, 0

    def __call__(self, ins):
        ins.then_inc(self.sem, 1)
        self.n += 1
        self.eng.wait_ge(self.sem, self.n)


def build(nc, a):
    with ExitStack() as ctx:
        def sem(name):
            return ctx.enter_context(nc.semaphore(name))

        base = 16512

        def at(name, shape, offset, dt=F32):
            return nc.alloc_sbuf_tensor_at(name, shape, dt, offset=base + offset)

        o = 0
        regions = {}
        for name, size in dict(consts=NCONST * 4, vecs=NVEC * 4, ones=512, mod=96 * 4, small=2048, x0=KD * T * 4,
                               hi=KD * T * 4, lo=KD * T * 4, wraw=RING * 4096, wsplit=4 * 4096,
                               z=Z_N * T * 4, tmp=KD * T * 4, rows=4 * T * 4,
                               q=6 * T * 4, k=HEADS * KEYS * 4, kr=KEYS * 4, ckv=CK * KEYS * 4,
                               p=8192, cond=2048).items():
            regions[name] = o
            o += (size + 31) // 32 * 32
        assert base + o <= 229344, base + o
        R = regions
        consts = at("consts_sb", [P, NCONST], R["consts"])
        vecs = at("vecs_sb", [P, NVEC], R["vecs"])
        ones = at("ones", [P, P], R["ones"])
        mod = at("mod", [P, 48, 2], R["mod"])
        cond = at("cond", [P, 512], R["cond"])
        silu_c = at("silu_c", [P, KD, 2], R["small"])
        stats = at("stats", [P, 2, 6], R["small"] + 64)
        meanvar = at("meanvar", [P, NT, 2], R["small"] + 128)
        rstd = at("rstd", [P, NT], R["small"] + 192)
        std = at("std", [P, NT], R["small"] + 224)
        negmax = at("negmax", [P, 32], R["small"] + 256)
        rowmax = at("rowmax", [P, 32], R["small"] + 384)
        rowsum = at("rowsum", [P, 32], R["small"] + 512)
        rinv = at("rinv", [P, 32], R["small"] + 640)
        x0T = at("x0T", [P, KD, T], R["x0"])
        act_hi = at("act_hi", [P, KD, T], R["hi"], F32R)
        act_lo = at("act_lo", [P, KD, T], R["lo"], F32R)
        w_raw = at("w_raw", [P, RING, D], R["wraw"])
        w_hi = at("w_hi", [P, 2, D], R["wsplit"], F32R)
        w_lo = at("w_lo", [P, 2, D], R["wsplit"] + 8192, F32R)
        z = at("z", [P, Z_N, T], R["z"])
        x_tok = at("x_tok", [P, NT, D], R["z"])
        val = at("val", [P, VT, HEADS * VH], R["z"])
        r_T = at("r_T", [P, KD, T], R["z"])
        h2T = at("h2T", [P, KD, T], R["z"] + KD * T * 4)
        tmp = at("tmp", [P, KD, T], R["tmp"])
        rows = at("rows", [P, 4, T], R["rows"])
        qT = at("qT", [P, 6, T], R["q"])
        kT = at("kT", [P, HEADS, KEYS], R["k"])
        krT = at("krT", [P, KEYS], R["kr"])
        ckvT = at("ckvT", [P, CK, KEYS], R["ckv"])
        sq = at("sq", [P, KD, T], R["q"])
        prob = at("prob", [P, 2, SEQ], R["p"])
        probT = at("probT", [P, 2, 4, P], R["p"] + 4096)
        v_tok = at("v_tok", [P, NT, GH * P], R["hi"])
        wsT = at("wsT_sb", [P, GH, P], R["hi"] + 10240)
        bs = at("bs_sb", [P, GH, P], R["hi"] + 12288)
        w_uk = at("w_uk_sb", [P, CK, HEADS * NOPE], R["lo"])
        w_uv = at("w_uv_sb", [P, CK, HEADS * VH], R["lo"] + 4096)
        o_tok = at("o_tok", [P, NT, KVL + ROPE], R["rows"])

        B = R["z"]
        skT = at("skT_sb", [P, HP, NK], B)
        q_blk = at("q_blk", [P, 2, T], B + 8192)
        found = at("found", [P, 2, NPT, TOPK], B + 12800)
        found_i = at("found_i", [P, 2, NPT, TOPK], B + 13440, U32)
        scratch = at("scratch", [P, NPT, NK], B + 14080)
        piece = at("piece", [P, 2, NK, GS], B)
        hit = at("hit", [P, SLOTS, TOPK], B + 65536)
        cand2 = at("cand2", [P, PH, NCAND + 2], B + 65536)
        o = B + 73728

        def small(name, shape, dt=F32):
            nonlocal o
            n = 4
            for x in shape[1:]:
                n *= x
            n = (n + 31) // 32 * 32
            o += n
            return at(name, shape, o - n, dt)
        cand = small("cand", [P, PH, NCAND])
        fin = small("fin", [P, PH, TOPK])
        pos = small("pos", [P, PH, TOPK], U32)
        pos_f = small("pos_f", [P, SLOTS])
        num_u = small("num_u", [P, 2, SLOTS], U32)
        num_f = small("num_f", [P, SLOTS])
        step_i = small("step_i", [P, PH, TOPK])
        diff = small("diff", [P, SLOTS])
        expo = small("expo", [P, SLOTS])
        ssum = small("ssum", [P, 16])
        chosen = small("chosen", [P, 3, SLOTS])
        assert o <= B + 81920
        top = at("top", [P, NPT, HP, TOPK], B + 90112)
        top_f = at("top_f", [P, NPT, HP, TOPK], B + 95232)
        sel = at("sel", [P, 3, ND], B + 100352)
        one_i = at("one_i", [P, 4, 4, NK], R["wsplit"])
        one_j = at("one_j", [P, 4, 4, NK], R["wsplit"] + 8192)
        expert = at("expert", [P, SLOTS], B + 113920, U32)
        gate_s = at("gate_s", [P, SLOTS], B + 114432)
        assert base + B + 114944 <= 229344
        e_hi = at("e_hi", [P, 2, D // 2], B + 105728, F32R)
        e_lo = at("e_lo", [P, 2, D // 2], B + 109824, F32R)
        e_out = at("e_out", [P, 2, ND], B + 86016)
        v_hi = at("v_hi", [P, GROUP, D], B, F32R)
        v_lo = at("v_lo", [P, GROUP, D], B + 16384, F32R)
        GA = GROUP * ND * 4
        ga_hi = at("ga_hi", [P, 2, GROUP, ND], B + 32768, F32R)
        ga_lo = at("ga_lo", [P, 2, GROUP, ND], B + 32768 + 2 * GA, F32R)
        gath = at("gath", [P, GB, D], B + 32768 + 4 * GA)
        assert 32768 + 4 * GA + GB * 4096 <= 77824
        h2_tok = at("h2_tok", [P, D], B + 81920)
        f_tok = at("f_tok", [P, D], B + 90112)
        g_in = at("g_in", [P, 2, NG, 2, GS], B + 94208)
        a_early = at("a_early", [P, 2, ND], B + 77824)
        a_g = at("a_g", [P, 2, ND], B + 101376)
        ga32 = at("ga32", [P, 2, ND], B + 104960)
        act_v = at("act_v", [P, SLOTS], B + 108544)
        act_g = at("act_g", [P, SLOTS], B + 109056)
        idx8 = at("idx8", [P, 2, PER], B + 109568, U32)
        act8 = at("act8", [P, 2, PER], B + 109632)

        def quarter(x, c):
            return x[:, :, c * D // 4:(c + 1) * D // 4]

        def raw_quarter(c):
            return w_raw[:, 2 + c % 2].rearrange("p (e n) -> p e n", e=GROUP)
        y_tok = at("y_tok", [P, 4, D], B)
        gb2 = at("gb2", [P, 2, D], B + 16384)
        ident = consts[:, C_ID:C_ID + P]
        perm = consts[:, C_PERM:C_PERM + P]
        cosT = consts[:, C_COS:C_COS + T]
        sinT = consts[:, C_SIN:C_SIN + T]
        iota = consts[:, C_IOTA:C_IOTA + NK]

        def vec(name, k):
            return vecs[:, VEC_AT[name] + k:VEC_AT[name] + k + 1]

        ps = ctx.enter_context(nc.psum_tensor("ps", [P, 8, 512], F32))

        s_const, s_vec, s_cache, s_ukv, s_gm, s_sk, s_gb = map(sem, "s_const s_vec s_cache s_ukv s_gm s_sk s_gb".split())
        s_x = [sem(f"x_landed{i}") for i in range(NT)]
        s_w = [sem(f"w_landed{i}") for i in range(RING)]
        s_dve = sem("own_dve")
        names = """ones lo_odd silu adaused adaev adat var std xn xT x0e mod h32 hhi hlo whi wlo wused evac sqz rowsA
            cqrow vmean vc2 vvar vvarr vn cqn cqhi cqlo ckvn krmm krr qmm qr kmm kev vmm vev vtt vte gmm bt sc
            mx ex pn pt pte pv pve rowsB rowr sqa sqb mhi mlo m mean1 rc1 sq1 var1 varr h2 h2hi h2lo smm h2t
            h2te gd idx act wgt fsub fexp top1 chose selt sele onei eqj onej gmat gst ehi elo emm eg uhi ulo vhi
            vlo amm ag ga gahi galo fmm fe dots var2 std2 wsm ax group ft r2 yt y yn yg rstd2 out otr ote""".split()
        s = {n: sem("s_" + n) for n in names}
        s_y = [sem(f"y_written{i}") for i in range(4)]
        s_g = [sem(f"rows_landed{i}") for i in range(GB)]
        s_u = [sem(f"u_landed{i}") for i in range(2)]
        s_v = [sem(f"v_landed{i}") for i in range(2)]
        s_gi = [sem(f"gates_landed{i}") for i in range(2)]
        s_gw = [sem(f"gates_written{i}") for i in range(2)]
        s_e = [sem(f"early_landed{i}") for i in range(2)]
        s_eo = [sem(f"early_written{i}") for i in range(2)]
        s_er = [sem(f"early_read{i}") for i in range(2)]
        early = nc.dram_tensor("early_activations", (NGR, P, ND), F32, kind="Internal").ap()
        gates = nc.dram_tensor("dense_gates", (NG, P, NK, GS), F32, kind="Internal").ap()

        block = ctx.enter_context(nc.Block())

        END = {n: SPLIT_AT[n] + ORDER[n] for n in ORDER}
        N_LIN = END["w_pq"]
        ODD = dict(h=0, cq=KD // 2, m=KD // 2 + QK // 2, h2=KD + QK // 2)

        def each_step(eng, step):
            mid = NGR // 2

            def pairs(first, end, half):
                with eng.Fori(0, (end - first) // 2) as i:
                    step(Step(first, i, 2), 1, half)
                    step(Step(first + 1, i, 2), 0, half)
            step(Step(0), 0, 0, "first")
            step(Step(1), 1, 0)
            step(Step(2), 0, 0)
            pairs(3, mid - 1, 0)
            step(Step(mid - 1), 1, 0, "turn")
            step(Step(mid), 0, 1)
            pairs(mid + 1, NGR - 1, 1)
            step(Step(NGR - 1), 1, 1, "last")
            step(Step(NGR), 0, 1, "tail")

        def each_four(eng, q, body):
            n = GS // 4
            if q == 0:
                for u in range(4):
                    body(Step(u), Step(u), u)
            first = 4 if q == 0 else 0
            with eng.Fori(0, (n - first) // 4) as i:
                for u in range(4):
                    body(Step(q * n + first + u, i, 4), Step(first + u, i, 4), u)

        @block.sync
        def _(sp):
            def stream(name, dram):
                width = WIDTH[name] * P
                g0 = RING_AT[name]

                def load(b, u):
                    slot = (g0 + u) % RING
                    held = name if not isinstance(b, int) or b >= RING else \
                        next((k for k in ORDER if 0 <= g0 + b - RING - RING_AT[k] < ORDER[k]), "ada")
                    if held.startswith("ada"):
                        wait(sp, s["adaused"], b + (g0 - RING - RING_AT[held] + FIRST[held] + 1))
                    else:
                        wait(sp, s["wlo"], b + (g0 - RING - RING_AT[held] + SPLIT_AT[held] + 1))
                    sp.dma_start(w_raw[:, slot, 0:width], dram[b]).then_inc(s_w[slot], 16)
                in_steps(sp, ORDER[name], RING, load)

            for name in ORDER:
                stream(name, a[name.rstrip("2")][FIRST[name]:] if name in FIRST else a[name])
            def early_blocks(b0, b1):
                for b in range(b0, b1):
                    if b + 2 < NGR:
                        sp.wait_ge(s["elo"], 2 * b + 2)
                        load_early(b + 2)
                    sp.wait_ge(s["eg"], b + 1)
                    sp.dma_start(early[b], e_out[:, b % 2]).then_inc(s_eo[b % 2], 16)

            def load_early(b):
                sp.dma_start(w_raw[:, 2 + b % 2], a["peer_uT"][GROUP * b + EARLY]).then_inc(s_e[b % 2], 16)

            def load_u(g, par, j):
                wait(sp, s["ulo"], g(EARLY, j - 1))
                slot = (par + j) % 2
                sp.dma_start(w_raw[:, slot], a["peer_uT"][g(GROUP, j)]).then_inc(s_u[slot], 16)

            sp.wait_ge(s["wlo"], N_LIN)
            for b in range(2):
                load_early(b)
            for j in range(2):
                load_u(Step(0), 0, j)
            e0 = sum(EARLY_AT[:2])
            early_blocks(0, e0)
            for q in range(NG):
                sp.wait_ge(s["gst"], GS // 4 * (q + 1))
                sp.dma_start(gates[q], piece[:, q % 2]).then_inc(s_gw[q % 2], 16)
                n = EARLY_AT[2 + q]
                early_blocks(e0, e0 + n)
                e0 += n

            def load_v(g, c):
                wait(sp, s["vlo"], g(4, c - 1))
                src = a["peer_vq"].rearrange("g c p n -> (g c) p n")[g(4, c)]
                sp.dma_start(w_raw[:, 2 + c % 2], src).then_inc(s_v[c % 2], 16)

            def load_gates(g, pair):
                wait(sp, s["ga"], g(GROUP, 2 * pair + 2 - GROUP))
                src = gates.rearrange("s j (b i) t -> b j s (i t)", i=2)[g(2, pair)]
                sp.dma_start(g_in[:, pair].rearrange("p s i t -> p s (i t)"), src).then_inc(s_gi[pair], 16)

            for i in range(2):
                sp.wait_ge(s_gw[i], 16 * len(range(i, NG, 2)))
            sp.wait_ge(s["sele"], NPT - 1)
            sp.wait_ge(s["chose"], NPT)
            for pair in range(2):
                load_gates(Step(0), pair)
            sp.wait_ge(s["elo"], 2 * NGR)
            for i in range(2):
                sp.wait_ge(s_eo[i], 16 * len(range(i, NGR, 2)))
            load_v(Step(0), 0)

            def sp_step(g, par, half, edge=None):
                if edge == "tail":
                    return
                after = g.plus(1)
                for j in range(EARLY):
                    if j == 0:
                        load_u(g, par, 2)
                        load_v(g, 1)
                    elif edge != "last":
                        load_u(after, 1 - par, j - 1)
                    if j == 1:
                        if edge != "first":
                            load_gates(g, 1)
                        wait(sp, s["ga"], g(GROUP, -GROUP))
                        sp.dma_start(a_early[:, par], early[g()]).then_inc(s_er[par], 16)
                    if j == 2 and edge != "last":
                        load_gates(after, 0)
                for c in (2, 3, 4):
                    if not (edge == "last" and c == 4):
                        load_v(g, c)
            each_step(sp, sp_step)
            sp.wait_ge(s["fmm"], KD * NGR)
            sp.dma_start(gb2[:, 0], a["ln2_g"].partition_broadcast(P)).then_inc(s_gb, 16)
            sp.dma_start(gb2[:, 1], a["ln2_b"].partition_broadcast(P)).then_inc(s_gb, 16)
            for t, (t0, n) in enumerate(TILES):
                sp.wait_ge(s["y"], t + 1)
                dst = a["y_prompt"][t0:t0 + n] if t < SAMPLE else a["y_sample"]
                sp.dma_start(dst, y_tok[0:n, t % 4]).then_inc(s_y[t % 4], 16)
            for i in range(4):
                sp.wait_ge(s_y[i], 16 * len(TILES[i::4]))
            sp.wait_ge(s["out"], 16 * (1 + 2 * NT))

        @block.gpsimd
        def _(pool):
            def low_parts(name, b0=0, b1=None):
                kk = WIDTH[name]
                for b in range(b0, ORDER[name] if b1 is None else b1):
                    slot, g = (RING_AT[name] + b) % RING, (SPLIT_AT[name] + b) % 2
                    wait(pool, s["wlo"], SPLIT_AT[name] + b)
                    pool.wait_ge(s["whi"], SPLIT_AT[name] + b + 1)
                    nc.gpsimd.tensor_tensor(w_lo[:, g, 0:kk * P], w_raw[:, slot, 0:kk * P],
                                            w_hi[:, g, 0:kk * P].bitcast(F32), ALU.subtract).then_inc(s["wlo"], 1)

            def low_blocks(src, high, n):
                for k in range(1, n, 2):
                    pool.wait_ge(s[high], k + 1)
                    nc.gpsimd.tensor_tensor(act_lo[:, k], src[:, k], act_hi[:, k].bitcast(F32), ALU.subtract).then_inc(s["lo_odd"], 1)

            pool.dma_start(vecs[:], a["vecs"]).then_inc(s_vec, 16)
            pool.dma_start(consts[:], a["consts"]).then_inc(s_const, 16)
            for t, (t0, n) in enumerate(TILES):
                src = a["x_prompt"][t0:t0 + n] if t < SAMPLE else a["x_sample"]
                pool.dma_start(x_tok[0:n, t], src).then_inc(s_x[t], 16)
            pool.dma_start(ckvT[:, :, SEQ:NEW], a["cacheT"]).then_inc(s_cache, 16)
            pool.dma_start(krT[:, SEQ:NEW], a["krcacheT"]).then_inc(s_cache, 16)
            low_parts("w_in", 0, 1)
            low_blocks(tmp, "hhi", KD)
            low_parts("w_in2")
            low_parts("w_uq", 0, 1)
            low_blocks(tmp, "cqhi", QK)
            low_parts("w_uq", 1)
            pool.wait_ge(s["wused"], END["w_uq"])
            pool.dma_start(w_uk[:], a["w_uk"]).then_inc(s_ukv, 16)
            pool.dma_start(w_uv[:], a["w_uv"]).then_inc(s_ukv, 16)
            pool.dma_start(wsT[:], a["wsT"]).then_inc(s_gm, 16)
            pool.dma_start(bs[:], a["b_s"].partition_broadcast(P)).then_inc(s_gm, 16)
            pool.wait_ge(s["vte"], NT)
            pool.dma_start(a["new_v"], v_tok[0:DEC, SAMPLE, :]).then_inc(s["out"], 16)
            for t, (t0, n) in enumerate(TILES):
                pool.wait_ge(s["ote"], t + 1)
                dst_c, dst_k = (a["ckv_p"][t0:t0 + n], a["kr_p"][t0:t0 + n]) if t < SAMPLE else (a["ckv_s"], a["kr_s"])
                pool.dma_start(dst_c, o_tok[0:n, t, 0:KVL]).then_inc(s["out"], 16)
                pool.dma_start(dst_k, o_tok[0:n, t, KVL:]).then_inc(s["out"], 16)

            low_parts("w_o", 0, 1)
            low_blocks(tmp, "mhi", KD)
            low_parts("w_pq", 0, 1)
            low_blocks(h2T, "h2hi", KD)
            pool.wait_ge(s["h2"], KD)
            pool.dma_start(skT[:], a["skT"]).then_inc(s_sk, 16)
            low_parts("w_pq", 1)

            def times_gates(g, k, w):
                pool.wait_ge(s["eqj"], g(1, 1))
                if g.i is not None:
                    pool.sem_inc(s["group"], 1)
                gate = sel[:, 2].rearrange("p (g u) -> p g u", u=4)[:, g()]
                nc.gpsimd.tensor_tensor(one_j[:, w], one_j[:, w], gate.unsqueeze(2).to_broadcast([P, 4, NK]),
                                        ALU.mult).then_inc(s["onej"], 1)
            def early_lows(b0, b1):
                for b in range(b0, min(b1, NGR)):
                    for h in range(2):
                        pool.wait_ge(s["ehi"], 2 * b + h + 1)
                        nc.gpsimd.tensor_tensor(e_lo[:, h], w_raw[:, 2 + b % 2, h * (D // 2):(h + 1) * (D // 2)],
                                                e_hi[:, h].bitcast(F32), ALU.subtract).then_inc(s["elo"], 1)
            e0 = sum(EARLY_AT[:2])
            early_lows(0, e0 + 1)
            for q in range(NG):
                each_four(pool, q, times_gates)
                n = EARLY_AT[2 + q]
                early_lows(e0 + 1, e0 + n + 1)
                e0 += n

            pool.wait_ge(s["chose"], NPT)
            for i in range(2):
                pool.wait_ge(s_gw[i], 16 * len(range(i, NG, 2)))

            def pool_step(g, par, half, edge=None):
                if edge == "tail":
                    return
                table = a["peer_v"] if half else a["peer_u"]
                looped = g.i is not None
                for u in range(PER):
                    if u == 0:
                        pool.wait_ge(s["idx"], g(1, 1))
                        if looped:
                            pool.sem_inc(s["group"], 1)
                    if not (edge == "first" and u < GB):
                        pool.wait_ge(s["gd"], g(PER, u - GB + 1))
                        if looped:
                            pool.sem_inc(s["group"], 1)
                    pool.indirect_dma_start(out=gath[:, u % GB, :], out_offset=None, in_=table,
                                            in_offset=bass.IndirectOffsetOnAxis(ap=idx8[:, par, u:u + 1], axis=0)
                                            ).then_inc(s_g[u % GB], 16)
            each_step(pool, pool_step)
            pool.wait_ge(s_gb, 32)
            for t, (t0, n) in enumerate(TILES):
                pool.wait_ge(s["yg"], t + 1)
                nc.gpsimd.tensor_tensor(y_tok[0:n, t % 4], y_tok[0:n, t % 4], gb2[0:n, 1], ALU.add).then_inc(s["y"], 1)

        @block.tensor
        def _(pe):
            def mm(out, lhsT, rhs, start, stop):
                return nc.tensor.matmul(out, lhsT, rhs, start=start, stop=stop)

            def ada_rows(g):
                wait(pe, s["adaev"], g)
                for j in range(4):
                    f = 4 * g + j
                    r = f if f < ORDER["ada"] else RING_AT["ada2"] + f - ORDER["ada"]
                    pe.wait_ge(s_w[r % RING], 16 * (r // RING + 1))
                    for i in range(2):
                        ins = mm(ps[0:2, 7, :], silu_c[:, 2 * j + i, :], w_raw[:, r % RING, i * 512:(i + 1) * 512],
                                 j == i == 0, j == 3 and i == 1)
                    ins.then_inc(s["adaused"], 1)

            def ada_columns(g, out):
                pe.wait_ge(s["adaev"], g + 1)
                for j in range(4):
                    ins = nc.tensor.transpose(out[:, 2 * j:2 * j + 2], cond[0:2, j * P:(j + 1) * P], ident[0:2, 0:2])
                ins.then_inc(s["adat"], 1)

            pe.wait_ge(s["silu"], 1)
            pe.wait_ge(s_const, 16)
            for g in range(ORDER["ada"] // 4):
                ada_rows(g)
                ada_columns(g, ps[:, 0, 8 * g:8 * g + 8])
            pe.wait_ge(s["xn"], NT)
            for k in range(KD):
                if k >= 3:
                    pe.wait_ge(s["x0e"], k - 2)
                b0 = 1 + 2 * (k % 3)
                for t, (t0, n) in enumerate(TILES):
                    out = ps[:, b0, t0:t0 + n] if t < SAMPLE else ps[:, b0 + 1, 0:DEC]
                    ins = nc.tensor.transpose(out, x_tok[0:n, t, k * P:(k + 1) * P], ident[0:n, 0:n])
                ins.then_inc(s["xT"], 1)


            def linear(name, ready, behind=None, at={}):
                kk, s0 = WIDTH[name], SPLIT_AT[name]

                def one(b, u):
                    g = s0 + u
                    first = isinstance(b, int) and b == 0
                    if isinstance(b, int) and b in at:
                        at[b]()
                    pe.wait_ge(s["wlo"], b + s0 + 1)
                    wait(pe, s["evac"], b + s0 - 1)
                    for half, (c0, c1) in enumerate(HALVES):
                        n = 0
                        for k in range(kk):
                            if first and half == 0:
                                if k % 2:
                                    pe.wait_ge(s["lo_odd"], ODD[ready] + k // 2 + 1)
                                else:
                                    pe.wait_ge(s[ready + "lo"], k // 2 + 1)
                            for w, x in ((w_hi, act_hi), (w_hi, act_lo), (w_lo, act_hi)):
                                ins = mm(ps[:, 2 * (g % 2) + half, 0:H], w[:, g % 2, k * P:(k + 1) * P],
                                         x[:, k, c0:c1], n == 0, n == 3 * kk - 1)
                                n += 1
                    ins.then_inc(s["wused"], 1)
                    if behind is not None and not first:
                        behind(b - 1, u - 1)
                in_steps(pe, ORDER[name], RING, one)
                if behind is not None:
                    behind(ORDER[name] - 1, ORDER[name] - 1)

            def column_sums(bank, src, blocks, ready=None):
                for i, k in enumerate(blocks):
                    if ready is not None:
                        pe.wait_ge(ready, i + 1)
                    for half, (c0, c1) in enumerate(HALVES):
                        ins = mm(ps[:, bank + half, 0:H], ones[:], src[:, k, c0:c1], i == 0, i == len(blocks) - 1)
                return ins

            pe.wait_ge(s["mod"], 1)
            linear("w_in", "h")

            def low_rank_sums():
                pe.wait_ge(s["sqz"], Z_KR)
                column_sums(4, tmp, range(QK))
                column_sums(6, tmp, range(QK, QK + CK)).then_inc(s["rowsA"], 1)
            linear("w_in2", "h", at={1: low_rank_sums})
            pe.wait_ge(s["evac"], END["w_in2"])
            pe.wait_ge(s["cqrow"], 2)
            column_sums(6, z, range(Z_GV, Z_GV + GH)).then_inc(s["vmean"], 1)

            def v_squares():
                pe.wait_ge(s["vc2"], 1)
                column_sums(4, tmp, range(GH)).then_inc(s["vvar"], 1)

            def swapped_kr():
                for half, (c0, c1) in enumerate(HALVES):
                    ins = mm(ps[:, 6 + half, 0:H], perm, z[:, Z_KR, c0:c1], True, True)
                ins.then_inc(s["krmm"], 1)
            linear("w_uq", "cq", at={2: v_squares, 3: swapped_kr})
            pe.wait_ge(s["vn"], 1)
            pe.wait_ge(s["evac"], END["w_uq"])
            pe.wait_ge(s["krr"], 1)
            for j in range(2):
                for half, (c0, c1) in enumerate(HALVES):
                    ins = mm(ps[:, 4 + 2 * j + half, 0:H], perm, qT[:, HEADS + j, c0:c1], True, True)
            ins.then_inc(s["qmm"], 1)
            pe.wait_ge(s["ckvn"], 1)
            pe.wait_ge(s_cache, 32)
            pe.wait_ge(s_ukv, 32)
            KH = KEYS // 2
            for h in range(HEADS):
                if h >= 2:
                    pe.wait_ge(s["kev"], h - 1)
                for half in range(2):
                    for c in range(CK):
                        ins = mm(ps[:, 2 * (h % 2) + half, 0:KH], w_uk[:, c, h * P:(h + 1) * P],
                                 ckvT[:, c, half * KH:(half + 1) * KH], c == 0, c == CK - 1)
                ins.then_inc(s["kmm"], 1)
            pe.wait_ge(s["qr"], 2)
            for i in range(VT):
                n = P if i < VT - 1 else DEC
                if i >= 4:
                    pe.wait_ge(s["vev"], i - 3)
                for c in range(CK):
                    ins = mm(ps[0:n, 4 + i % 4, :], ckvT[:, c, i * P:i * P + n], w_uv[:, c, :], c == 0, c == CK - 1)
                ins.then_inc(s["vmm"], 1)
            pe.wait_ge(s["kev"], HEADS)
            for t, (t0, n) in enumerate(TILES):
                if t >= 4:
                    pe.wait_ge(s["vte"], t - 3)
                for g in range(GH):
                    ins = nc.tensor.transpose(ps[0:n, t % 4, g * P:(g + 1) * P], z[:, Z_GV + g, t0:t0 + n], ident)
                ins.then_inc(s["vtt"], 1)
            pe.wait_ge(s["vev"], VT)
            pe.wait_ge(s_gm, 32)
            pe.wait_ge(s["wsm"], 1)
            for t, (t0, n) in enumerate(TILES):
                pe.wait_ge(s["vte"], t + 1)
                if t >= 4:
                    pe.wait_ge(s["bt"], t - 3)
                for g in range(GH):
                    ins = mm(ps[:, 4 + t % 4, g * P:g * P + n], v_tok[0:n, t, g * P:(g + 1) * P],
                             wsT[0:n, g, 0:n], True, True)
                ins.then_inc(s["gmm"], 1)

            units = [(h, t) for h in range(HEADS) for t in range(NT)]

            def keys(t):
                return (0, (t + 1) * P) if t < SAMPLE else (SEQ, PAST + DEC)

            def key_blocks(t):
                k0, n = keys(t)
                return [(k0 + j * P, min(P, n - j * P)) for j in range((n + P - 1) // P)]

            def scores(i):
                h, t = units[i]
                t0, n = TILES[t]
                k0, nk = keys(t)
                if i >= 2:
                    pe.wait_ge(s["ex"], i - 1)
                r = ROPE * (h % 2)
                mm(ps[0:n, i % 2, 0:nk], qT[:, h, t0:t0 + n], kT[:, h, k0:k0 + nk], True, False)
                mm(ps[0:n, i % 2, 0:nk], qT[r:r + ROPE, HEADS + h // 2, t0:t0 + n],
                   krT[r:r + ROPE, k0:k0 + nk], False, True).then_inc(s["sc"], 1)

            pe.wait_ge(s["vte"], NT)
            pe.wait_ge(s["bt"], NT)
            for t, (t0, n) in enumerate(TILES):
                k0 = t0 if t < SAMPLE else NEW
                if t >= 2:
                    pe.wait_ge(s["ote"], t - 1)
                for c in range(CK):
                    nc.tensor.transpose(ps[0:n, 6 + t % 2, c * P:(c + 1) * P], ckvT[:, c, k0:k0 + n], ident)
                nc.tensor.transpose(ps[0:n, 6 + t % 2, KVL:KVL + ROPE], krT[0:ROPE, k0:k0 + n],
                                    ident[0:ROPE, 0:ROPE]).then_inc(s["otr"], 1)
            pe.wait_ge(s["ote"], NT)
            first = ORDER["ada"] // 4
            scores(0)
            for i, (h, t) in enumerate(units):
                if i + 1 < len(units):
                    scores(i + 1)
                if i % 2 == 0 and 0 < i <= ORDER["ada2"] // 2:
                    ada_columns(first + i // 2 - 1, ps[:, 6, 4 * i - 8:4 * i])
                if i % 2 == 0 and i < ORDER["ada2"] // 2:
                    ada_rows(first + i // 2)
                t0, n = TILES[t]
                kb = key_blocks(t)
                pe.wait_ge(s["pn"], i + 1)
                if i >= 2:
                    pe.wait_ge(s["pte"], i - 1)
                for j, (k0, nk) in enumerate(kb):
                    ins = nc.tensor.transpose(ps[0:nk, 2 + i % 2, j * P:j * P + n],
                                              prob[0:n, i % 2, j * P:j * P + nk], ident[0:n, 0:n])
                ins.then_inc(s["pt"], 1)
                pe.wait_ge(s["pte"], i + 1)
                if i >= 2:
                    pe.wait_ge(s["pve"], i - 1)
                for j, (k0, nk) in enumerate(kb):
                    ins = mm(ps[:, 4 + i % 2, 0:n], val[0:nk, k0 // P, h * VH:(h + 1) * VH],
                             probT[0:nk, i % 2, j, 0:n], j == 0, j == len(kb) - 1)
                ins.then_inc(s["pv"], 1)
            pe.wait_ge(s["sqb"], 1)
            column_sums(2, z, range(Z_GV, Z_GV + GH))
            column_sums(0, z, range(Z_GU, Z_GU + HEADS), s["sqa"]).then_inc(s["rowsB"], 1)
            pe.wait_ge(s["rowr"], 2)

            def sum_residual(b, u):
                pe.wait_ge(s["evac"], b + SPLIT_AT["w_o"] + 1)
                for half, (c0, c1) in enumerate(HALVES):
                    ins = mm(ps[:, 4 + half, 0:H], ones[:], r_T[:, b, c0:c1], b == 0, b == KD - 1)
                ins.then_inc(s["mean1"], 1)
            linear("w_o", "m", sum_residual)
            column_sums(6, sq, range(KD), s["sq1"]).then_inc(s["var1"], 1)

            def gathering_h2():
                for k in range(KD):
                    ins = nc.tensor.transpose(ps[:, 4 + k // 4, (k % 4) * P:(k % 4 + 1) * P], h2T[:, k, ND:T], ident)
                ins.then_inc(s["h2t"], 1)

            def sub_scores(b, u):
                s0 = SPLIT_AT["w_pq"]
                if isinstance(b, int) and b == 0:
                    pe.wait_ge(s["h2te"], 1)
                    pe.wait_ge(s_sk, 16)
                pe.wait_ge(s["evac"], b + s0 + 1)
                wait(pe, s["top1"], b - 1)
                for t, (t0, n) in enumerate(PTILES):
                    ins = mm(ps[0:n, 4 + 2 * (u % 2) + t // 4, (t % 4) * NK:(t % 4 + 1) * NK],
                             q_blk[:, u % 2, t0:t0 + n], skT[:, b, :], True, True)
                ins.then_inc(s["smm"], 1)
            linear("w_pq", "h2", sub_scores, at={1: gathering_h2})

            def transpose_choices(t):
                t0, n = PTILES[t]
                pe.wait_ge(s["chose"], t + 1)
                wait(pe, s["sele"], t)
                for c in range(3):
                    ins = nc.tensor.transpose(ps[:, 4, c * P:c * P + n], chosen[0:n, c, :], ident[0:n, 0:n])
                ins.then_inc(s["selt"], 1)

            def three(out, w, x, i, n):
                (w1, w2), (x1, x2) = w, x
                mm(out, w1, x1, i == 0, False)
                mm(out, w1, x2, False, False)
                return mm(out, w2, x1, False, i == n - 1)

            def early_products(b0, b1):
                for b in range(b0, b1):
                    wait(pe, s["eg"], b - 1)
                    for h in range(2):
                        pe.wait_ge(s["elo"], 2 * b + h + 1)
                        for i in range(KD // 2):
                            c = slice(i * P, (i + 1) * P)
                            k = h * (KD // 2) + i
                            ins = three(ps[:, b % 2, 0:ND], (e_hi[:, h, c], e_lo[:, h, c]),
                                        (act_hi[:, k, 0:ND], act_lo[:, k, 0:ND]), k, KD)
                        ins.then_inc(s["emm"], 1)

            early_products(0, EARLY_AT[0])
            pe.wait_ge(s["top1"], HP)
            transpose_choices(0)
            e0 = sum(EARLY_AT[:2])
            early_products(EARLY_AT[0], e0)
            for q in range(NG):
                if q % 2 == 0 and q // 2 + 1 < NPT - 1:
                    transpose_choices(q // 2 + 1)

                def four(g, k, w):
                    pe.wait_ge(s["onei"], g(1, 1))
                    pe.wait_ge(s["onej"], g(1, 1))
                    wait(pe, s["gst"], g(1, -1))
                    for u in range(4):
                        ins = mm(ps[:, 6 + w % 2, u * NK:(u + 1) * NK], one_j[:, w, u], one_i[:, w, u], True, True)
                    ins.then_inc(s["gmat"], 1)
                each_four(pe, q, four)
                n = EARLY_AT[2 + q]
                early_products(e0, e0 + n)
                e0 += n

            def pe_step(g, par, half, edge=None):
                if edge != "tail":
                    for j in range(EARLY):
                        w = (par + j) % 2
                        pe.wait_ge(s["ulo"], g(EARLY, j + 1))
                        wait(pe, s["ag"], g(EARLY, j - 1))
                        for k in range(KD):
                            c = slice(k * P, (k + 1) * P)
                            ins = three(ps[:, w, 0:ND], (w_hi[:, w, c], w_lo[:, w, c]),
                                        (act_hi[:, k, 0:ND], act_lo[:, k, 0:ND]), k, KD)
                        ins.then_inc(s["amm"], 1)
                if edge == "first":
                    return
                pe.wait_ge(s["galo"], g(GROUP))
                for d in range(KD):
                    if d % 2 == 0:
                        pe.wait_ge(s["vlo"], g(4, d // 2 + 1 - 4))
                    wait(pe, s["fe"], g(KD, d - 3 - KD))
                    c = slice(d * P, (d + 1) * P)
                    for e in range(GROUP):
                        ins = three(ps[:, 2 + d % 4, 0:ND], (v_hi[:, e, c], v_lo[:, e, c]),
                                    (ga_hi[:, 1 - par, e], ga_lo[:, 1 - par, e]), e, GROUP)
                    ins.then_inc(s["fmm"], 1)
            each_step(pe, pe_step)

            pe.wait_ge(s["ag"], EARLY * NGR)
            pe.wait_ge(s["gd"], 2 * SLOTS)
            for k in range(KD):
                ins = nc.tensor.transpose(ps[:, k // 4, (k % 4) * P:(k % 4 + 1) * P], f_tok[:, k * P:(k + 1) * P], ident)
            ins.then_inc(s["ft"], 1)
            pe.wait_ge(s["fe"], KD * NGR)
            for t, (t0, n) in enumerate(TILES):
                if t0 + n > ND:
                    pe.wait_ge(s["r2"], 1)
                if t >= 2:
                    pe.wait_ge(s["yn"], t - 1)
                for k in range(KD):
                    ins = nc.tensor.transpose(ps[0:n, 2 + 2 * (t % 2) + k // 4, (k % 4) * P:(k % 4 + 1) * P],
                                              x0T[:, k, t0:t0 + n], ident)
                ins.then_inc(s["yt"], 1)

        @block.scalar
        def _(act):
            def f(out, in_, func=ACT.Copy, **kw):
                return nc.scalar.activation(out, in_, func, **kw)

            act.wait_ge(s_vec, 16)
            f(silu_c[:].rearrange("p k c -> p (k c)"), vecs[:, VEC_AT["c"]:VEC_AT["c"] + 16], ACT.Silu).then_inc(s["silu"], 1)

            def ada_copy(g):
                act.wait_ge(s["adaused"], 4 * g + 4)
                wait(act, s["adat"], g)
                f(cond[0:2, :], ps[0:2, 7, :]).then_inc(s["adaev"], 1)
            for g in range(ORDER["ada"] // 4):
                if g == 2:
                    act.wait_ge(s["var"], 1)
                    f(std[:], rstd[:], ACT.Sqrt).then_inc(s["std"], 1)
                ada_copy(g)
            def first_high(name):
                s0, g0 = SPLIT_AT[name], RING_AT[name]
                act.wait_ge(s_w[g0 % RING], 16 * (g0 // RING + 1))
                wait(act, s["wused"], s0 - 1)
                f(w_hi[:, s0 % 2, 0:WIDTH[name] * P], w_raw[:, g0 % RING, 0:WIDTH[name] * P]).then_inc(s["whi"], 1)

            first_high("w_in")
            for k in range(KD):
                act.wait_ge(s["h32"], k + 1)
                f(act_hi[:, k], tmp[:, k]).then_inc(s["hhi"], 1)

            def linear(name, evacuate, at={}, then=None):
                kk, s0, g0 = WIDTH[name], SPLIT_AT[name], RING_AT[name]

                def loads(b, u):
                    first = (g0 + u) // RING + 1
                    return 16 * first if isinstance(b, int) and b < RING else (b - u) * (16 // RING) + 16 * first

                def one(b, u):
                    slot = (g0 + u) % RING
                    if not (isinstance(b, int) and b == 0):
                        act.wait_ge(s_w[slot], loads(b, u))
                        wait(act, s["wused"], b + s0 - 1)
                        f(w_hi[:, (s0 + u) % 2, 0:kk * P], w_raw[:, slot, 0:kk * P]).then_inc(s["whi"], 1)
                    if isinstance(b, int) and b in at:
                        at[b]()
                    if evacuate is not None and not (isinstance(b, int) and b == 0):
                        out(b - 1, u - 1)

                def out(b, u):
                    act.wait_ge(s["wused"], b + s0 + 1)
                    pair = 2 * ((s0 + u) % 2)
                    to = q_blk[:, u % 2, :] if evacuate is q_blk else evacuate[:, b, :]
                    if evacuate is q_blk:
                        wait(act, s["smm"], b - 1)
                    func = ACT.Gelu_apprx_tanh if name == "w_in2" and b > 0 else ACT.Copy
                    f(to.rearrange("p (s h) -> p s h", s=2), ps[:, pair:pair + 2, 0:H], func).then_inc(s["evac"], 1)
                in_steps(act, ORDER[name], RING, one)
                if then is not None:
                    first_high(then)
                if evacuate is not None:
                    out(ORDER[name] - 1, ORDER[name] - 1)

            linear("w_in", z, then="w_in2")

            def low_rank_deviations():
                act.wait_ge(s["cqrow"], 1)
                f(rows[:, 0:2], rows[:, 0:2], ACT.Sqrt).then_inc(s["std"], 1)
            linear("w_in2", z[:, Z_KR:], at={2: low_rank_deviations}, then="w_uq")
            act.wait_ge(s["cqn"], 1)
            act.wait_ge(s["wused"], END["w_in2"])
            for k in range(QK):
                f(act_hi[:, k], tmp[:, k]).then_inc(s["cqhi"], 1)

            def v_deviation():
                act.wait_ge(s["vvarr"], 1)
                f(rows[:, 3], rows[:, 3], ACT.Sqrt).then_inc(s["std"], 1)
            linear("w_uq", qT, at={3: v_deviation})
            for h in range(HEADS):
                act.wait_ge(s["kmm"], h + 1)
                f(kT[:, h, :].rearrange("p (s h) -> p s h", s=2),
                  ps[:, 2 * (h % 2):2 * (h % 2) + 2, 0:KEYS // 2]).then_inc(s["kev"], 1)
            for i in range(VT):
                n = P if i < VT - 1 else DEC
                act.wait_ge(s["vmm"], i + 1)
                f(val[0:n, i, :], ps[0:n, 4 + i % 4, :]).then_inc(s["vev"], 1)
            for t, (t0, n) in enumerate(TILES):
                act.wait_ge(s["vtt"], t + 1)
                f(v_tok[0:n, t, :], ps[0:n, t % 4, :]).then_inc(s["vte"], 1)
            for t, (t0, n) in enumerate(TILES):
                act.wait_ge(s["otr"], t + 1)
                f(o_tok[0:n, t, :], ps[0:n, 6 + t % 2, 0:KVL + ROPE]).then_inc(s["ote"], 1)
            act.wait_ge(s["bt"], NT)
            f(z[:, Z_GV:], tmp[:, HEADS:KD], ACT.Square).then_inc(s["sqb"], 1)

            def head_squares(h):
                act.wait_ge(s["pve"], (h + 1) * NT)
                f(z[:, Z_GU + h], tmp[:, h], ACT.Square).then_inc(s["sqa"], 1)

            units = [(h, t) for h in range(HEADS) for t in range(NT)]
            for i, (h, t) in enumerate(units):
                t0, n = TILES[t]
                act.wait_ge(s["mx"], i + 1)
                if i >= 2:
                    act.wait_ge(s["pt"], i - 1)
                if t < SAMPLE:
                    for r in range(2):
                        nk = t * P + (r + 1) * CHUNK
                        rr = slice(r * CHUNK, (r + 1) * CHUNK)
                        ins = f(prob[rr, i % 2, 0:nk], ps[rr, i % 2, 0:nk], ACT.Exp, bias=negmax[rr, i:i + 1],
                                scale=SCALE, accum_out=rowsum[rr, i:i + 1])
                else:
                    ins = f(prob[0:n, i % 2, 0:PAST + DEC], ps[0:n, i % 2, 0:PAST + DEC], ACT.Exp,
                            bias=negmax[0:n, i:i + 1], scale=SCALE, accum_out=rowsum[0:n, i:i + 1])
                ins.then_inc(s["ex"], 1)
                act.wait_ge(s["pt"], i + 1)
                if i >= 2:
                    act.wait_ge(s["pv"], i - 1)
                if t < SAMPLE:
                    ins = f(probT[:, i % 2, 0:t + 1, :], ps[:, 2 + i % 2, 0:(t + 1) * P].rearrange("p (j n) -> p j n", n=P))
                else:
                    f(probT[:, i % 2, 0:2, 0:n], ps[:, 2 + i % 2, 0:2 * P].rearrange("p (j n) -> p j n", n=P)[:, :, 0:n])
                    ins = f(probT[0:DEC, i % 2, 2, 0:n], ps[0:DEC, 2 + i % 2, 2 * P:2 * P + n])
                ins.then_inc(s["pte"], 1)
                if i % 2 == 0 and i < ORDER["ada2"] // 2:
                    ada_copy(ORDER["ada"] // 4 + i // 2)
                if i >= NT + 2 and (i - 2) % NT == 0:
                    head_squares((i - 2) // NT - 1)
            head_squares(HEADS - 1)
            act.wait_ge(s["rowr"], 1)
            f(rows[:, 0:2], rows[:, 0:2], ACT.Sqrt).then_inc(s["std"], 1)
            first_high("w_o")
            for k in range(KD):
                act.wait_ge(s["m"], k + 1)
                f(act_hi[:, k], tmp[:, k]).then_inc(s["mhi"], 1)
            linear("w_o", None)
            for k in range(KD):
                act.wait_ge(s["rc1"], k + 1)
                f(sq[:, k], r_T[:, k], ACT.Square).then_inc(s["sq1"], 1)
            act.wait_ge(s["varr"], 1)
            f(rows[:, 1], rows[:, 1], ACT.Sqrt).then_inc(s["std"], 1)
            first_high("w_pq")
            for k in range(KD):
                act.wait_ge(s["h2"], k + 1)
                f(act_hi[:, k], h2T[:, k]).then_inc(s["h2hi"], 1)

            def gathering_h2():
                act.wait_ge(s["h2t"], 1)
                f(h2_tok[:], ps[:, 4:6, :].rearrange("p b n -> p (b n)")).then_inc(s["h2te"], 1)
            linear("w_pq", q_blk, at={1: gathering_h2})
            def transposed(t):
                t0, n = PTILES[t]
                act.wait_ge(s["selt"], t + 1)
                f(sel[:, :, t0:t0 + n], ps[:, 4, 0:3 * P].rearrange("p (c n) -> p c n", c=3)[:, :, 0:n]).then_inc(s["sele"], 1)

            def exponentials(t):
                n = PTILES[t][1]
                act.wait_ge(s["fsub"], t + 1)
                f(expo[0:n], diff[0:n], ACT.Exp).then_inc(s["fexp"], 1)

            def early_activations(b0, b1):
                for b in range(b0, b1):
                    if b + 1 < NGR:
                        early_highs(b + 1)
                    act.wait_ge(s["emm"], 2 * b + 2)
                    wait(act, s_eo[b % 2], 16 * (b // 2))
                    f(e_out[:, b % 2], ps[:, b % 2, 0:ND], ACT.Gelu_apprx_tanh).then_inc(s["eg"], 1)

            def early_highs(b):
                act.wait_ge(s_e[b % 2], 16 * (b // 2) + 16)
                for h in range(2):
                    wait(act, s["emm"], 2 * b + h - 1)
                    f(e_hi[:, h], w_raw[:, 2 + b % 2, h * (D // 2):(h + 1) * (D // 2)]).then_inc(s["ehi"], 1)

            early_highs(0)
            e0 = EARLY_AT[0]
            early_activations(0, 3)
            exponentials(0)
            early_activations(3, e0)
            transposed(0)
            early_activations(e0, e0 + 3)
            exponentials(1)
            early_activations(e0 + 3, e0 + EARLY_AT[1])
            e0 += EARLY_AT[1]
            for q in range(NG):
                if q >= 2:
                    act.wait_ge(s_gw[q % 2], 16 * (q // 2))

                def four(g, k, w):
                    act.wait_ge(s["gmat"], g(1, 1))
                    to = piece[:, q % 2].rearrange("p i (g t) -> p g t i", t=4)[:, k()]
                    f(to, ps[:, 6 + w % 2, :].rearrange("p (t i) -> p t i", t=4)).then_inc(s["gst"], 1)
                each_four(act, q, four)
                if q % 2 == 0 and q // 2 + 1 < NPT - 1:
                    transposed(q // 2 + 1)
                n = EARLY_AT[2 + q]
                if q in CHOOSE_AFTER:
                    early_activations(e0, e0 + 2)
                    exponentials(CHOOSE_AFTER[q])
                    early_activations(e0 + 2, e0 + n)
                else:
                    early_activations(e0, e0 + n)
                e0 += n

            def u_high(g, par, j):
                w = (par + j) % 2
                act.wait_ge(s_u[w], g(8 * EARLY, 16 * ((EARLY * par + j) // 2) + 16 - 8 * EARLY * par))
                wait(act, s["amm"], g(EARLY, j - 1))
                f(w_hi[:, w], w_raw[:, w]).then_inc(s["uhi"], 1)

            def v_high(g, c):
                act.wait_ge(s_v[c % 2], g(32, c // 2 * 16 + 16))
                wait(act, s["fmm"], g(KD, 2 * c + 2 - KD))
                f(quarter(v_hi, c), raw_quarter(c)).then_inc(s["vhi"], 1)

            def gelu(g, par, i):
                w = (par + i) % 2
                act.wait_ge(s["amm"], g(EARLY, i + 1))
                wait(act, s["ga"], g(GROUP, (-2, -1, 1)[i]))
                f(a_g[:, w], ps[:, w, 0:ND], ACT.Gelu_apprx_tanh).then_inc(s["ag"], 1)

            def weighted_high(g, par, i):
                act.wait_ge(s["ga"], g(GROUP, i + 1))
                f(ga_hi[:, par, i], ga32[:, i % 2]).then_inc(s["gahi"], 1)

            def act_step(g, par, half, edge=None):
                before, after = g.plus(-1), g.plus(1)
                for j in range(EARLY if edge != "tail" else 1):
                    if j > 0:
                        gelu(g, par, j - 1)
                    elif edge != "first":
                        gelu(before, 1 - par, EARLY - 1)
                    if edge != "tail":
                        if j < EARLY - 1:
                            u_high(g, par, j + 1)
                        elif edge != "last":
                            u_high(after, 1 - par, 0)
                    if j > 0:
                        weighted_high(g, par, j - 1)
                    elif edge != "first":
                        v_high(before, 3)
                        weighted_high(before, 1 - par, EARLY - 1)
                        weighted_high(before, 1 - par, EARLY)
                if edge != "tail":
                    for c in range(3):
                        v_high(g, c)
                if edge == "turn":
                    act.wait_ge(s["act"], 1)
                    f(act_g[:], act_v[:], ACT.Gelu_apprx_tanh).then_inc(s["wgt"], 1)
            act.wait_ge(s["wused"], N_LIN)
            act.wait_ge(s["gmat"], ND // 4)
            u_high(Step(0), 0, 0)
            for i in range(2):
                act.wait_ge(s_gw[i], 16 * len(range(i, NG, 2)))
            each_step(act, act_step)
            for t, (t0, n) in enumerate(TILES):
                act.wait_ge(s["var2"], t + 1)
                f(std[0:n, t:t + 1], rstd[0:n, t:t + 1], ACT.Sqrt).then_inc(s["std2"], 1)
                act.wait_ge(s["rstd2"], t + 1)
                if t >= 4:
                    act.wait_ge(s_y[t % 4], 16 * (t // 4))
                f(y_tok[0:n, t % 4], ps[0:n, 2 + 2 * (t % 2):4 + 2 * (t % 2), :].rearrange("p b n -> p (b n)"), ACT.Identity,
                  bias=negmax[0:n, t:t + 1], scale=rstd[0:n, t:t + 1]).then_inc(s["yn"], 1)

        @block.vector
        def _(dve):
            v = nc.vector
            step = Chain(dve, s_dve)
            v.memset(ones[:], 1.0).then_inc(s["ones"], 1)
            step(v.memset(meanvar[:], 1.0))
            for t, (t0, n) in enumerate(TILES):
                dve.wait_ge(s_x[t], 16)
                for j in range(2):
                    step(v.bn_stats(stats[0:n, j], x_tok[0:n, t, j * 512:(j + 1) * 512]))
                step(v.bn_aggr(meanvar[0:n, t], stats[0:n]))
            v.tensor_scalar(rstd[:], meanvar[:, :, 1], EPS, None, ALU.add).then_inc(s["var"], 1)
            dve.wait_ge(s["std"], 1)
            step(v.reciprocal(rstd[:], std[:]))
            for t, (t0, n) in enumerate(TILES):
                v.tensor_scalar(x_tok[0:n, t], x_tok[0:n, t], meanvar[0:n, t, 0:1], rstd[0:n, t:t + 1],
                                ALU.subtract, ALU.mult).then_inc(s["xn"], 1)
            dve.wait_ge(s_vec, 16)
            for k in range(KD):
                dve.wait_ge(s["xT"], k + 1)
                b0 = 1 + 2 * (k % 3)
                v.tensor_scalar(x0T[:, k, 0:SEQ], ps[:, b0, :], vec("ln_in_g", k), vec("ln_in_b", k), ALU.mult, ALU.add)
                v.tensor_scalar(x0T[:, k, SEQ:T], ps[:, b0 + 1, 0:DEC], vec("ln_in_g", k), vec("ln_in_b", k),
                                ALU.mult, ALU.add).then_inc(s["x0e"], 1)
            def conditioning(f0, f1, src):
                dve.wait_ge(s["adat"], f1 // 4)
                b_ada = vecs[:, VEC_AT["b_ada"] + f0:VEC_AT["b_ada"] + f1].unsqueeze(2).to_broadcast([P, f1 - f0, 2])
                ins = v.tensor_tensor(mod[:, f0:f1], src.rearrange("p (f c) -> p f c", c=2), b_ada, ALU.add)
                for o0, o1 in ((SC1, SH2), (SC2, 6 * KD)):
                    o0, o1 = max(o0, f0), min(o1, f1)
                    if o0 < o1:
                        step(ins)
                        ins = v.tensor_scalar(mod[:, o0:o1], mod[:, o0:o1], 1.0, None, ALU.add)
                ins.then_inc(s["mod"], 1)
            SH1, SC1, GT1, SH2, SC2, GT2 = (KD * i for i in range(6))
            conditioning(0, 2 * KD, ps[:, 0, 0:4 * KD])
            dve.wait_ge(s["mod"], 1)
            STREAMS = ((0, SEQ, 0), (SEQ, T, 1))

            def modulate(out, src, k, scale, shift):
                for c0, c1, c in STREAMS:
                    ins = v.tensor_scalar(out[:, k, c0:c1], src[:, k, c0:c1], mod[:, scale + k, c:c + 1],
                                          mod[:, shift + k, c:c + 1], ALU.mult, ALU.add)
                return ins

            dve.wait_ge(s["x0e"], KD)
            for k in range(KD):
                modulate(tmp, x0T, k, SC1, SH1).then_inc(s["h32"], 1)
            for k in range(0, KD, 2):
                dve.wait_ge(s["hhi"], k + 1)
                v.tensor_tensor(act_lo[:, k], tmp[:, k], act_hi[:, k].bitcast(F32), ALU.subtract).then_inc(s["hlo"], 1)

            def linear(name, extra=None):
                kk, s0, g0 = WIDTH[name], SPLIT_AT[name], RING_AT[name]

                def one(b, u):
                    slot, g = (g0 + u) % RING, (s0 + u) % 2
                    if not (isinstance(b, int) and b == 0):
                        wait(dve, s["wlo"], b + s0)
                        dve.wait_ge(s["whi"], b + s0 + 1)
                        v.tensor_tensor(w_lo[:, g, 0:kk * P], w_raw[:, slot, 0:kk * P],
                                        w_hi[:, g, 0:kk * P].bitcast(F32), ALU.subtract).then_inc(s["wlo"], 1)
                    if extra is not None and not (isinstance(b, int) and b == 0):
                        extra(b - 1, u - 1)
                in_steps(dve, ORDER[name], RING, one)
                if extra is not None:
                    extra(ORDER[name] - 1, ORDER[name] - 1)

            def pair(bank):
                return ps[:, bank:bank + 2, 0:H]

            def row(i):
                return rows[:, i].rearrange("p (s h) -> p s h", s=2)

            def low_rank_squares(b, u):
                dve.wait_ge(s["evac"], b + 1)
                if isinstance(b, int) and b == 0:
                    dve.wait_ge(s["hlo"], KD // 2)
                    dve.wait_ge(s["lo_odd"], ODD["cq"])
                v.tensor_tensor(tmp[:, b], z[:, b], z[:, b], ALU.mult).then_inc(s["sqz"], 1)
            linear("w_in", low_rank_squares)
            dve.wait_ge(s["rowsA"], 1)
            v.tensor_scalar(row(0), pair(4), 1.0 / QL, EPS, ALU.mult, ALU.add)
            v.tensor_scalar(row(1), pair(6), 1.0 / KVL, EPS, ALU.mult, ALU.add).then_inc(s["cqrow"], 1)
            dve.wait_ge(s["std"], 2)
            v.reciprocal(rows[:, 0:2], rows[:, 0:2]).then_inc(s["cqrow"], 1)
            dve.wait_ge(s["cqrow"], 2)
            for k in range(QK):
                ins = v.scalar_tensor_tensor(tmp[:, k], z[:, k], vec("g_q", k), rows[:, 0], ALU.mult, ALU.mult)
            ins.then_inc(s["cqn"], 1)
            for c in range(CK):
                for c0, c1, o in ((0, SEQ, 0), (SEQ, T, PAST)):
                    ins = v.scalar_tensor_tensor(ckvT[:, c, c0 + o:c1 + o], z[:, Z_CKV + c, c0:c1], vec("g_kv", c),
                                                 rows[:, 1, c0:c1], ALU.mult, ALU.mult)
            ins.then_inc(s["ckvn"], 1)
            for k in range(0, QK, 2):
                dve.wait_ge(s["cqhi"], k + 1)
                v.tensor_tensor(act_lo[:, k], tmp[:, k], act_hi[:, k].bitcast(F32), ALU.subtract).then_inc(s["cqlo"], 1)
            dve.wait_ge(s["cqlo"], QK // 2)
            dve.wait_ge(s["lo_odd"], ODD["m"])
            dve.wait_ge(s["vmean"], 1)
            step(v.tensor_scalar(row(2), pair(6), 1.0 / (GH * P), None, ALU.mult))
            for g in range(GH):
                ins = v.tensor_tensor(z[:, Z_GV + g], z[:, Z_GV + g], rows[:, 2], ALU.subtract)
            step(ins)
            for g in range(GH):
                ins = v.tensor_tensor(tmp[:, g], z[:, Z_GV + g], z[:, Z_GV + g], ALU.mult)
            ins.then_inc(s["vc2"], 1)
            dve.wait_ge(s["vvar"], 1)
            v.tensor_scalar(row(3), pair(4), 1.0 / (GH * P), EPS, ALU.mult, ALU.add).then_inc(s["vvarr"], 1)
            dve.wait_ge(s["std"], 3)
            step(v.reciprocal(rows[:, 3], rows[:, 3]))
            for g in range(GH):
                ins = v.scalar_tensor_tensor(z[:, Z_GV + g], z[:, Z_GV + g], vec("g_v", g), rows[:, 3], ALU.mult, ALU.mult)
            step(ins)
            for g in range(GH):
                ins = v.tensor_scalar(z[:, Z_GV + g], z[:, Z_GV + g], vec("b_v", g), None, ALU.add)
            ins.then_inc(s["vn"], 1)
            dve.wait_ge(s["krmm"], 1)
            dve.wait_ge(s["vn"], 1)
            step(v.tensor_tensor(row(0), pair(6), sinT.rearrange("p (s h) -> p s h", s=2), ALU.mult))
            step(v.tensor_tensor(rows[:, 1], z[:, Z_KR], cosT, ALU.mult))
            step(v.tensor_tensor(krT[:, 0:SEQ], rows[:, 0, 0:SEQ], rows[:, 1, 0:SEQ], ALU.add))
            v.tensor_tensor(krT[:, NEW:], rows[:, 0, SEQ:T], rows[:, 1, SEQ:T], ALU.add).then_inc(s["krr"], 1)
            dve.wait_ge(s["krr"], 1)
            v.tensor_scalar(x0T[:], x0T[:], ALPHA, None, ALU.mult).then_inc(s["ax"], 1)
            dve.wait_ge(s["qmm"], 1)
            for j in range(2):
                step(v.tensor_tensor(row(2 + j), pair(4 + 2 * j), sinT.rearrange("p (s h) -> p s h", s=2), ALU.mult))
                step(v.tensor_tensor(rows[:, j], qT[:, HEADS + j], cosT, ALU.mult))
                v.tensor_tensor(qT[:, HEADS + j], rows[:, j], rows[:, 2 + j], ALU.add).then_inc(s["qr"], 1)
            dve.wait_ge(s_gm, 32)
            v.memset(wsT[CHUNK:P, :, 0:CHUNK], 0.0).then_inc(s["wsm"], 1)
            for t, (t0, n) in enumerate(TILES):
                dve.wait_ge(s["gmm"], t + 1)
                step(v.tensor_tensor(tmp[:, HEADS:KD, t0:t0 + n],
                                     ps[:, 4 + t % 4, :].rearrange("p (g n) -> p g n", n=P)[:, :, 0:n], bs[:, :, 0:n], ALU.add))
                v.tensor_tensor(tmp[:, HEADS:KD, t0:t0 + n], tmp[:, HEADS:KD, t0:t0 + n],
                                z[:, Z_GU:Z_GU + GH, t0:t0 + n], ALU.mult).then_inc(s["bt"], 1)
            units = [(h, t) for h in range(HEADS) for t in range(NT)]

            def head_out(i):
                h, t = units[i]
                t0, n = TILES[t]
                dve.wait_ge(s["pv"], i + 1)
                v.tensor_copy(tmp[:, h, t0:t0 + n], ps[:, 4 + i % 2, 0:n]).then_inc(s["pve"], 1)

            for i, (h, t) in enumerate(units):
                t0, n = TILES[t]
                dve.wait_ge(s["sc"], i + 1)
                if t < SAMPLE:
                    for r in range(2):
                        rr = slice(r * CHUNK, (r + 1) * CHUNK)
                        ins = v.tensor_reduce(rowmax[rr, i:i + 1], ps[rr, i % 2, 0:t * P + (r + 1) * CHUNK], AX.X, ALU.max)
                        step(ins)
                else:
                    step(v.tensor_reduce(rowmax[0:n, i:i + 1], ps[0:n, i % 2, 0:PAST + DEC], AX.X, ALU.max))
                v.tensor_scalar(negmax[0:n, i:i + 1], rowmax[0:n, i:i + 1], -SCALE, None, ALU.mult).then_inc(s["mx"], 1)
                dve.wait_ge(s["ex"], i + 1)
                step(v.reciprocal(rinv[0:n, i:i + 1], rowsum[0:n, i:i + 1]))
                if t < SAMPLE:
                    step(v.memset(prob[0:CHUNK, i % 2, t * P + CHUNK:(t + 1) * P], 0.0))
                nk = (t + 1) * P if t < SAMPLE else PAST + DEC
                v.tensor_scalar(prob[0:n, i % 2, 0:nk], prob[0:n, i % 2, 0:nk], rinv[0:n, i:i + 1], None,
                                ALU.mult).then_inc(s["pn"], 1)
                if i >= 1:
                    head_out(i - 1)
            head_out(len(units) - 1)
            conditioning(2 * KD, 6 * KD, ps[:, 6, 0:8 * KD])
            dve.wait_ge(s["rowsB"], 1)
            dve.wait_ge(s["out"], 16 * (1 + 2 * NT))
            for j in range(2):
                ins = v.tensor_scalar(row(j), pair(2 * j), 1.0 / (HEADS * VH), EPS, ALU.mult, ALU.add)
                step(ins) if j == 0 else ins.then_inc(s["rowr"], 1)
            dve.wait_ge(s["std"], 4)
            v.reciprocal(rows[:, 0:2], rows[:, 0:2]).then_inc(s["rowr"], 1)
            dve.wait_ge(s["rowr"], 2)
            for k in range(KD + 1):
                if k < KD:
                    g, j = ("g_out_a", k) if k < HEADS else ("g_out_b", k - HEADS)
                    v.scalar_tensor_tensor(tmp[:, k], tmp[:, k], vec(g, j), rows[:, k // HEADS],
                                           ALU.mult, ALU.mult).then_inc(s["m"], 1)
                if k % 2:
                    dve.wait_ge(s["mhi"], k)
                    v.tensor_tensor(act_lo[:, k - 1], tmp[:, k - 1], act_hi[:, k - 1].bitcast(F32),
                                    ALU.subtract).then_inc(s["mlo"], 1)
            dve.wait_ge(s["ax"], 1)
            dve.wait_ge(s["mod"], 2)

            def residual(b, u):
                s0 = SPLIT_AT["w_o"]
                dve.wait_ge(s["wused"], b + s0 + 1)
                bank = 2 * ((s0 + u) % 2)
                for c0, c1, c in ((0, H, 0), (H, SEQ, 0), (SEQ, T, 1)):
                    half = c0 // H
                    ins = v.scalar_tensor_tensor(r_T[:, b, c0:c1], ps[:, bank + half, c0 - half * H:c1 - half * H],
                                                 mod[:, GT1 + b, c:c + 1], x0T[:, b, c0:c1], ALU.mult, ALU.add)
                ins.then_inc(s["evac"], 1)
            linear("w_o", residual)
            dve.wait_ge(s["evac"], END["w_o"])
            dve.wait_ge(s["mean1"], KD)
            step(v.tensor_scalar(row(0), pair(4), 1.0 / D, None, ALU.mult))
            for k in range(KD):
                v.tensor_tensor(r_T[:, k], r_T[:, k], rows[:, 0], ALU.subtract).then_inc(s["rc1"], 1)
            dve.wait_ge(s["rc1"], KD)
            dve.wait_ge(s["var1"], 1)
            v.tensor_scalar(row(1), pair(6), 1.0 / D, EPS, ALU.mult, ALU.add).then_inc(s["varr"], 1)
            dve.wait_ge(s["std"], 5)
            step(v.reciprocal(rows[:, 1], rows[:, 1]))
            for k in range(KD + 1):
                if k < KD:
                    step(v.scalar_tensor_tensor(x0T[:, k], r_T[:, k], vec("ln1_g", k), rows[:, 1], ALU.mult, ALU.mult))
                    step(v.tensor_scalar(x0T[:, k], x0T[:, k], vec("ln1_b", k), None, ALU.add))
                    modulate(h2T, x0T, k, SC2, SH2).then_inc(s["h2"], 1)
                if k % 2:
                    dve.wait_ge(s["h2hi"], k)
                    v.tensor_tensor(act_lo[:, k - 1], h2T[:, k - 1], act_hi[:, k - 1].bitcast(F32),
                                    ALU.subtract).then_inc(s["h2lo"], 1)
            dve.wait_ge(s["h2"], KD)
            step(v.tensor_scalar(x0T[:], x0T[:], ALPHA, None, ALU.mult))

            def top16(lists):
                for vals, idx, src, scr in lists:
                    ins = v.max(vals[:, 0:8], src)
                step(ins)
                for vals, idx, src, scr in lists:
                    v.max_index(idx[:, 0:8], vals[:, 0:8], src)
                    ins = v.match_replace(scr, vals[:, 0:8], src, -3.0e38)
                step(ins)
                for vals, idx, src, scr in lists:
                    ins = v.max(vals[:, 8:16], scr)
                step(ins)
                for vals, idx, src, scr in lists:
                    ins = v.max_index(idx[:, 8:16], vals[:, 8:16], scr)
                step(ins)

            def sub_tops(b):
                dve.wait_ge(s["smm"], b + 1)
                par = b % 2
                top16([(found[0:n, par, t], found_i[0:n, par, t],
                        ps[0:n, 4 + 2 * par + t // 4, (t % 4) * NK:(t % 4 + 1) * NK], scratch[0:n, t])
                       for t, (t0, n) in enumerate(PTILES)])
                step(v.tensor_copy(top[:, :, b, :], found[:, par]))
                v.tensor_copy(top_f[:, :, b, :], found_i[:, par]).then_inc(s["top1"], 1)

            step(v.memset(found[:], 0.0))
            step(v.memset(found_i[:].bitcast(F32), 0.0))
            for b in range(HP):
                sub_tops(b)
            dve.wait_ge(s["top1"], HP)

            starts = consts[:, C_START:C_START + TOPK]
            start_steps = consts[:, C_START + TOPK:C_START + 2 * TOPK]

            def choose(t):
                t0, n = PTILES[t]
                lists = top[0:n, t].rearrange("p (h q) a -> p h q a", q=2)
                ids = top_f[0:n, t].rearrange("p (h q) a -> p h q a", q=2)
                s1, s2 = lists[:, :, 0], lists[:, :, 1]
                for a0 in range(5):
                    out = cand[0:n, :, START[a0]:START[a0] + ROW[a0]]
                    v.tensor_tensor(out, s2[:, :, 0:ROW[a0]], s1[:, :, a0:a0 + 1].to_broadcast([n, PH, ROW[a0]]), ALU.add)
                for i in range(2):
                    v.tensor_tensor(cand[0:n, :, START[5] + i:START[8]:2], s1[:, :, 5:8],
                                    s2[:, :, i:i + 1].to_broadcast([n, PH, 3]), ALU.add)
                step(v.tensor_tensor(cand[0:n, :, START[8]:NCAND], s1[:, :, 8:16], s2[:, :, 0:1].to_broadcast([n, PH, 8]), ALU.add))
                top16([(fin[0:n, h], pos[0:n, h], cand[0:n, h], cand2[0:n, h, 0:NCAND]) for h in range(PH)])
                v.tensor_tensor(diff[0:n].rearrange("p (h k) -> p h k", h=PH), fin[0:n],
                                fin[0:n, :, 0:1].to_broadcast([n, PH, TOPK]), ALU.subtract).then_inc(s["fsub"], 1)
                steps = step_i[0:n]
                step(v.tensor_copy(steps[:, :, 0:1], ids[:, :, 0, 0:1]))
                step(v.tensor_tensor(steps[:, :, 1:], ids[:, :, 0, 1:], ids[:, :, 0, 0:TOPK - 1], ALU.subtract))
                step(v.scalar_tensor_tensor(steps, steps, 64.0, start_steps[0:n].unsqueeze(1).to_broadcast([n, PH, TOPK]),
                                            ALU.mult, ALU.add))
                step(v.tensor_copy(pos_f[0:n], pos[0:n].rearrange("p h k -> p (h k)")))
                h4 = hit[0:n].rearrange("p (h k) a -> p h k a", h=PH)
                step(v.tensor_tensor(hit[0:n], pos_f[0:n].unsqueeze(2).to_broadcast([n, SLOTS, TOPK]),
                                     starts[0:n].unsqueeze(1).to_broadcast([n, SLOTS, TOPK]), ALU.is_ge))
                step(v.tensor_tensor(h4, h4, steps.unsqueeze(2).to_broadcast([n, PH, TOPK, TOPK]), ALU.mult))
                step(v.tensor_reduce(num_f[0:n], hit[0:n], AX.X, ALU.add))
                step(v.tensor_copy(num_u[0:n, 0], num_f[0:n]))
                step(v.tensor_scalar(num_u[0:n, 1], num_u[0:n, 0], 63, None, ALU.bitwise_and))
                step(v.tensor_scalar(num_u[0:n, 0], num_u[0:n, 0], 6, None, ALU.logical_shift_right))
                if t >= 1:
                    dve.wait_ge(s["selt"], t)
                step(v.tensor_copy(chosen[0:n, 0], num_u[0:n, 0]))
                step(v.tensor_copy(num_f[0:n], num_u[0:n, 1]))
                step(v.tensor_tensor(num_f[0:n], pos_f[0:n], num_f[0:n], ALU.subtract))
                step(v.tensor_tensor(hit[0:n], num_f[0:n].unsqueeze(2).to_broadcast([n, SLOTS, TOPK]),
                                     iota[0:n, 0:TOPK].unsqueeze(1).to_broadcast([n, SLOTS, TOPK]), ALU.is_equal))
                step(v.tensor_tensor(h4, h4, ids[:, :, 1].unsqueeze(2).to_broadcast([n, PH, TOPK, TOPK]), ALU.mult))
                step(v.tensor_reduce(chosen[0:n, 1], hit[0:n], AX.X, ALU.add))
                dve.wait_ge(s["fexp"], t + 1)
                e3 = expo[0:n].rearrange("p (h k) -> p h k", h=PH)
                step(v.tensor_reduce(ssum[0:n, 0:PH], e3, AX.X, ALU.add))
                step(v.reciprocal(ssum[0:n, 0:PH], ssum[0:n, 0:PH]))
                if t == NPT - 1:
                    step(v.scalar_tensor_tensor(pos_f[0:n], chosen[0:n, 0], float(NK), chosen[0:n, 1], ALU.mult, ALU.add))
                    v.tensor_copy(expert[:], pos_f[:])
                g3 = (gate_s[:] if t == NPT - 1 else chosen[0:n, 2]).rearrange("p (h k) -> p h k", h=PH)
                v.tensor_tensor(g3, e3, ssum[0:n, 0:PH].unsqueeze(2).to_broadcast([n, PH, TOPK]), ALU.mult).then_inc(s["chose"], 1)
                dve.wait_ge(s["chose"], t + 1)

            choose(0)
            choose(1)
            for q in range(NG):
                dve.wait_ge(s["sele"], q // 2 + 1)

                def rows_of(g, k, w):
                    wait(dve, s["gmat"], g(1, -3))
                    for c, rows4, done in ((1, one_j, "eqj"), (0, one_i, "onei")):
                        number = sel[:, c].rearrange("p (g u) -> p g u", u=4)[:, g()]
                        v.tensor_tensor(rows4[:, w], iota.unsqueeze(1).to_broadcast([P, 4, NK]),
                                        number.unsqueeze(2).to_broadcast([P, 4, NK]), ALU.is_equal).then_inc(s[done], 1)
                each_four(dve, q, rows_of)
                if q in CHOOSE_AFTER:
                    choose(CHOOSE_AFTER[q])
            dve.wait_ge(s["gmat"], ND // 4)

            def u_low(g, par, j):
                w = (par + j) % 2
                dve.wait_ge(s["uhi"], g(EARLY, j + 1))
                v.tensor_tensor(w_lo[:, w], w_raw[:, w], w_hi[:, w].bitcast(F32), ALU.subtract).then_inc(s["ulo"], 1)

            def weighted(g, par, i):
                if i < EARLY:
                    src = a_g[:, (par + i) % 2]
                    dve.wait_ge(s["ag"], g(EARLY, i + 1))
                else:
                    src = a_early[:, par]
                    dve.wait_ge(s_er[par], g(8, 16 - 8 * par))
                dve.wait_ge(s_gi[i // 2], g(16, 16))
                wait(dve, s["gahi"], g(GROUP, i - 1))
                wait(dve, s["galo"], g(GROUP, i - 1))
                v.tensor_tensor(ga32[:, i % 2].rearrange("p (s t) -> p s t", s=NG), src.rearrange("p (s t) -> p s t", s=NG),
                                g_in[:, i // 2, :, i % 2, :], ALU.mult).then_inc(s["ga"], 1)

            def weighted_low(g, par, i):
                dve.wait_ge(s["gahi"], g(GROUP, i + 1))
                v.tensor_tensor(ga_lo[:, par, i], ga32[:, i % 2], ga_hi[:, par, i].bitcast(F32), ALU.subtract).then_inc(s["galo"], 1)

            def v_low(g, c):
                dve.wait_ge(s["vhi"], g(4, c + 1))
                v.tensor_tensor(quarter(v_lo, c), raw_quarter(c), quarter(v_hi, c).bitcast(F32),
                                ALU.subtract).then_inc(s["vlo"], 1)

            def indices(group, par):
                v.tensor_copy(idx8[:, par], expert[:].rearrange("p (g u) -> p g u", u=PER)[:, group]).then_inc(s["idx"], 1)

            def slot_op(g, par, half, u):
                dve.wait_ge(s_g[u % GB], g(PER // GB * 16, u // GB * 16 + 16))
                if half == 0:
                    v.tensor_tensor_reduce(gath[:, u % GB], gath[:, u % GB], h2_tok[:], 1.0, 0.0, ALU.mult, ALU.add,
                                           act8[:, par, u:u + 1]).then_inc(s["gd"], 1)
                else:
                    dve.wait_ge(s["gd"], g(PER, u))
                    w = act_g[:].rearrange("p (g u) -> p g u", u=PER)[:, g(1, -(NGR // 2)), u:u + 1]
                    v.scalar_tensor_tensor(f_tok[:], gath[:, u % GB], w, f_tok[:], ALU.mult, ALU.add).then_inc(s["gd"], 1)

            def dve_step(g, par, half, edge=None):
                before, after = g.plus(-1), g.plus(1)
                for j in range(EARLY if edge != "tail" else 1):
                    if edge != "tail":
                        if j < EARLY - 1:
                            u_low(g, par, j + 1)
                        elif edge != "last":
                            u_low(after, 1 - par, 0)
                    if j > 0:
                        weighted(g, par, j - 1)
                        weighted_low(g, par, j - 1)
                    elif edge != "first":
                        weighted(before, 1 - par, EARLY - 1)
                        weighted(before, 1 - par, EARLY)
                        v_low(before, 3)
                        weighted_low(before, 1 - par, EARLY - 1)
                        weighted_low(before, 1 - par, EARLY)
                    if j == 1 and edge not in ("last", "tail"):
                        indices(0 if edge == "turn" else g(1, 1) if half == 0 else g(1, 1 - NGR // 2), 1 - par)
                    if edge != "tail" and j > 0:
                        slot_op(g, par, half, j - 1)
                for d in range(KD):
                    if edge != "first":
                        dve.wait_ge(s["fmm"], g(KD, d + 1 - KD))
                        wait(dve, s["fe"], g(KD, d + 1 - 2 * KD))
                        v.scalar_tensor_tensor(x0T[:, d, 0:ND], ps[:, 2 + d % 4, 0:ND], mod[:, GT2 + d, 0:1],
                                               x0T[:, d, 0:ND], ALU.mult, ALU.add).then_inc(s["fe"], 1)
                    if edge != "tail" and d % 2 == 0 and d >= 2:
                        v_low(g, d // 2 - 1)
                    if edge != "tail" and d in (0, 1, 3, 4, 5, 7):
                        slot_op(g, par, half, 2 + (0, 1, 3, 4, 5, 7).index(d))
                if edge == "tail":
                    return
                if half == 0:
                    dve.wait_ge(s["gd"], g(PER, PER))
                    v.tensor_copy(act_v[:].rearrange("p (g u) -> p g u", u=PER)[:, g()], act8[:, par]).then_inc(s["dots"], 1)
                if edge == "turn":
                    dve.wait_ge(s["dots"], NGR // 2)
                    v.memset(f_tok[:], 0.0).then_inc(s["act"], 1)
                    dve.wait_ge(s["wgt"], 1)
                    v.tensor_tensor(act_g[:], act_g[:], gate_s[:], ALU.mult).then_inc(s["act"], 1)
                    dve.wait_ge(s["act"], 2)

            u_low(Step(0), 0, 0)
            indices(0, 0)
            each_step(dve, dve_step)
            dve.wait_ge(s["ft"], 1)
            for k in range(KD):
                for c0, c1, c in ((ND, SEQ, 0), (SEQ, T, 1)):
                    ins = v.scalar_tensor_tensor(x0T[:, k, c0:c1], ps[:, k // 4, (k % 4) * P + c0 - ND:(k % 4) * P + c1 - ND],
                                                 mod[:, GT2 + k, c:c + 1], x0T[:, k, c0:c1], ALU.mult, ALU.add)
            ins.then_inc(s["r2"], 1)

            def times_gamma(t):
                n = TILES[t][1]
                if t == 0:
                    dve.wait_ge(s_gb, 32)
                dve.wait_ge(s["yn"], t + 1)
                v.tensor_tensor(y_tok[0:n, t % 4], y_tok[0:n, t % 4], gb2[0:n, 0], ALU.mult).then_inc(s["yg"], 1)

            for t, (t0, n) in enumerate(TILES):
                dve.wait_ge(s["yt"], t + 1)
                src = ps[0:n, 2 + 2 * (t % 2):4 + 2 * (t % 2), :]
                for j in range(2):
                    step(v.bn_stats(stats[0:n, j], src[:, j]))
                step(v.bn_aggr(meanvar[0:n, t], stats[0:n]))
                v.tensor_scalar(rstd[0:n, t:t + 1], meanvar[0:n, t, 1:2], EPS, None, ALU.add).then_inc(s["var2"], 1)
                dve.wait_ge(s["std2"], t + 1)
                step(v.reciprocal(rstd[0:n, t:t + 1], std[0:n, t:t + 1]))
                v.tensor_scalar(negmax[0:n, t:t + 1], meanvar[0:n, t, 0:1], rstd[0:n, t:t + 1], -1.0,
                                ALU.mult, ALU.mult).then_inc(s["rstd2"], 1)
                if t >= 1:
                    times_gamma(t - 1)
            times_gamma(NT - 1)


_OUTS = dict(y_prompt=(1, SEQ, D), y_sample=(1, DEC, D), ckv_p=(1, 1, SEQ, KVL), kr_p=(1, 1, SEQ, ROPE),
             ckv_s=(1, 1, DEC, KVL), kr_s=(1, 1, DEC, ROPE), new_v=(1, 1, DEC, GH * P))


def layout(x):
    import numpy as np

    def blocked(w):
        n = w.shape[1] // P
        return w.reshape(w.shape[0] // P, P, n, P).transpose(2, 1, 0, 3).reshape(n, P, w.shape[0])

    def columns(v):
        return v.reshape(-1, P).T

    x = {k: np.asarray(v) for k, v in x.items()}
    w_in = x["w_in"][0]
    kr = w_in[:, QL + KVL:QL + KVL + ROPE]
    w_in = np.concatenate([w_in[:, :QL + KVL], kr, kr, w_in[:, QL + KVL + ROPE:]], axis=1)
    uq = x["w_uq"][0].reshape(QL, HEADS, NOPE + ROPE)
    w_uq = np.concatenate([uq[:, :, :NOPE].reshape(QL, -1), uq[:, :, NOPE:].reshape(QL, -1)], axis=1)
    c = np.stack([x["c_prompt"][0], x["c_sample"][0]])
    vecs = {k: columns(x[k].reshape(-1)) for k in VEC_LEN if k != "c"}
    vecs["c"] = c.reshape(2, KD, P).transpose(2, 1, 0).reshape(P, 2 * KD)
    krc = x["cache_krope"][0, 0].T
    half = ROPE // 2
    freq = np.power(np.float32(10000.0), -np.arange(half, dtype=np.float32) * np.float32(2.0 / ROPE)).astype(np.float32)
    positions = np.concatenate([np.arange(SEQ), PAST + np.arange(DEC)]).astype(np.float32)
    angle = positions[:, None] * freq[None, :]
    cos = np.tile(np.cos(angle).T, (4, 1))
    sin = np.tile(np.concatenate([-np.sin(angle).T, np.sin(angle).T]), (2, 1))
    perm = np.zeros((P, P))
    perm[np.arange(P) ^ half, np.arange(P)] = 1.0
    consts = np.concatenate([np.eye(P), perm, cos, sin, np.tile(np.arange(NK), (P, 1)),
                             np.tile(START, (P, 1)), np.tile(np.diff([0] + START), (P, 1))], axis=1).astype(np.float32)
    out = dict(
        x_prompt=x["x_prompt"][0], x_sample=x["x_sample"][0], consts=consts,
        vecs=np.concatenate([vecs[k] for k in VEC_LEN], axis=1),
        cacheT=x["cache_ckv"][0, 0].T.reshape(CK, P, PAST).transpose(1, 0, 2),
        krcacheT=np.concatenate([krc, krc], axis=0),
        ada=x["w_ada"][0].reshape(4, 2, P, 12, 512).transpose(3, 0, 2, 1, 4).reshape(48, P, D),
        w_in=blocked(w_in), w_uq=blocked(w_uq), w_o=blocked(x["w_o"][0]), w_pq=blocked(x["w_pq"][0]),
        w_uk=x["w_uk"][0].reshape(CK, P, -1).transpose(1, 0, 2), w_uv=x["w_uv"][0].reshape(CK, P, -1).transpose(1, 0, 2),
        wsT=x["w_s"][0].transpose(2, 0, 1), b_s=x["b_s"][0].reshape(-1),
        skT=x["sub_keys"][0].transpose(3, 0, 1, 2).reshape(P, HP, NK),
        peer_uT=x["peer_u"][0].reshape(NB, P, KD, P).transpose(0, 3, 2, 1).reshape(NB, P, D),
        peer_vq=x["peer_v"][0].reshape(NGR, GROUP, P, 4, D // 4).transpose(0, 3, 2, 1, 4).reshape(NGR, 4, P, D),
        peer_u=x["peer_u"][0], peer_v=x["peer_v"][0], ln2_g=x["ln2_g"][0], ln2_b=x["ln2_b"][0])
    return {k: np.ascontiguousarray(v) for k, v in out.items()}


def kernel(**inputs):
    import concourse.bacc as bacc
    from concourse.bass_utils import run_bass_kernel_spmd

    nc = bacc.Bacc("TRN2", target_bir_lowering=False, num_devices=1)
    arrays = layout(inputs)
    a = {k: nc.dram_tensor(k, v.shape, F32, kind="ExternalInput").ap() for k, v in arrays.items()}
    for k, shape in _OUTS.items():
        a[k] = nc.dram_tensor(k, shape[-2:], F32, kind="ExternalOutput").ap()
    build(nc, a)
    r = run_bass_kernel_spmd(nc, [arrays], core_ids=[0])
    return tuple(r.results[0][k].reshape(shape) for k, shape in _OUTS.items())
```
